# Optimizing a Trainium2 kernel written in Bass

```python
import jax, jax.numpy as jnp
from jax import lax
import numpy as np
import math

D_MODEL = 1024
BATCH = 1
SEQ = 1024
DEPTH = 1

HEAD_DIM = 64
D_MIX = D_MODEL
D_CONV = D_MIX // 2
D_ATTN = D_MIX - D_CONV
N_HEADS = D_ATTN // HEAD_DIM
CONV_WIDTH = 3
DILATED_BRANCHES = ((128, 1), (512, 4), (2048, 16))
BLOCK = 128
D_FF = ((-(-8 * D_MODEL // 3) + 255) // 256) * 256
D_IN = 3 * D_CONV + 3 * D_ATTN
EPS = 1e-6


def rms_norm(x, g):
    xf = x.astype(jnp.float32)
    y = xf * lax.rsqrt(jnp.mean(xf * xf, axis=-1, keepdims=True) + EPS)
    return (y * g.astype(jnp.float32)).astype(x.dtype)

def short_conv(u, w):
    return lax.conv_general_dilated(
        u, w[:, None, :].astype(u.dtype), window_strides=(1,),
        padding=[(CONV_WIDTH - 1, 0)], dimension_numbers=("NWC", "WIO", "NWC"),
        feature_group_count=u.shape[-1])

def dilated_branch(q, k, v, window, dil):
    B, S, H, dh = q.shape
    M = S // dil
    L = window // dil
    nb = -(-M // BLOCK)
    Mp = nb * BLOCK
    pad = Mp - M

    def to_sub(t):
        return t.reshape(B, M, dil, H, dh).transpose(0, 2, 1, 3, 4).reshape(B * dil, M, H, dh)

    qs, ks, vs = to_sub(q), to_sub(k), to_sub(v)
    Bd = B * dil
    qb = jnp.pad(qs, ((0, 0), (0, pad), (0, 0), (0, 0))).reshape(Bd, nb, BLOCK, H, dh)

    def band(t):
        tp = jnp.pad(t, ((0, 0), (BLOCK, pad), (0, 0), (0, 0)))
        prev = tp[:, :Mp].reshape(Bd, nb, BLOCK, H, dh)
        cur = tp[:, BLOCK:].reshape(Bd, nb, BLOCK, H, dh)
        return jnp.concatenate([prev, cur], axis=2)

    kw, vw = band(ks), band(vs)
    s = jnp.einsum("bnqhd,bnkhd->bnhqk", qb, kw, preferred_element_type=jnp.float32)

    i = jnp.arange(BLOCK)[:, None]
    j = jnp.arange(2 * BLOCK)[None, :]
    dist = BLOCK + i - j
    kpos = (jnp.arange(nb)[:, None, None] - 1) * BLOCK + j[None]
    valid = ((dist >= 0) & (dist <= L))[None] & (kpos >= 0)
    s = jnp.where(valid[None, :, None], s, -jnp.inf)

    m = jnp.max(s, axis=-1, keepdims=True)
    e = jnp.exp(s - m)
    den = jnp.sum(e, axis=-1, keepdims=True)
    p = e / den
    lse = (m + jnp.log(den))[..., 0]
    o = jnp.einsum("bnhqk,bnkhd->bnqhd", p.astype(vw.dtype), vw)

    o = o.reshape(Bd, Mp, H, dh)[:, :M]
    lse = lse.transpose(0, 1, 3, 2).reshape(Bd, Mp, H)[:, :M]
    o = o.reshape(B, dil, M, H, dh).transpose(0, 2, 1, 3, 4).reshape(B, S, H, dh)
    lse = lse.reshape(B, dil, M, H).transpose(0, 2, 1, 3).reshape(B, S, H)
    return o, lse

def dilated_mixture(q, k, v):
    outs, lses = [], []
    for window, dil in DILATED_BRANCHES:
        o, lse = dilated_branch(q, k, v, window, dil)
        outs.append(o)
        lses.append(lse)
    w = jax.nn.softmax(jnp.stack(lses, axis=0), axis=0)
    o = jnp.sum(w[..., None] * jnp.stack(outs, axis=0).astype(jnp.float32), axis=0)
    return o.astype(q.dtype)

def first_inputs(seed: int = 0) -> dict:
    key = jax.random.key(seed)
    ks = jax.random.split(key, 13)
    f32 = jnp.float32

    def gain(k_, n):
        return 1.0 + 0.05 * jax.random.normal(k_, (DEPTH, n), f32)

    return {
        "x": jax.random.normal(ks[0], (BATCH, SEQ, D_MODEL), f32),
        "g_mix": gain(ks[1], D_MODEL),
        "w_in": jax.random.normal(ks[2], (DEPTH, D_MODEL, D_IN), f32) * D_MODEL ** -0.5,
        "conv_w": jax.random.normal(ks[3], (DEPTH, CONV_WIDTH, D_CONV), f32) * CONV_WIDTH ** -0.5,
        "g_q": gain(ks[4], HEAD_DIM),
        "g_k": gain(ks[5], HEAD_DIM),
        "g_conv_out": gain(ks[6], D_CONV),
        "g_attn_out": gain(ks[7], D_ATTN),
        "w_out": jax.random.normal(ks[8], (DEPTH, D_MIX, D_MODEL), f32) * D_MIX ** -0.5,
        "g_ffn": gain(ks[9], D_MODEL),
        "w_gate": jax.random.normal(ks[10], (DEPTH, D_MODEL, D_FF), f32) * D_MODEL ** -0.5,
        "w_up": jax.random.normal(ks[11], (DEPTH, D_MODEL, D_FF), f32) * D_MODEL ** -0.5,
        "w_down": jax.random.normal(ks[12], (DEPTH, D_FF, D_MODEL), f32) * D_FF ** -0.5,
    }

def first_block(x, g_mix, w_in, conv_w, g_q, g_k, g_conv_out, g_attn_out, w_out,
              g_ffn, w_gate, w_up, w_down):
    B, S, _ = x.shape
    splits = [D_CONV, 2 * D_CONV, 3 * D_CONV, 3 * D_CONV + D_ATTN, 3 * D_CONV + 2 * D_ATTN]
    for l in range(DEPTH):
        h = rms_norm(x, g_mix[l])
        z = h @ w_in[l]
        u, gb, gc, q, k, v = jnp.split(z, splits, axis=-1)

        y_conv = gb * short_conv(gc * u, conv_w[l])

        q = rms_norm(q.reshape(B, S, N_HEADS, HEAD_DIM), g_q[l]) * (HEAD_DIM ** -0.5)
        k = rms_norm(k.reshape(B, S, N_HEADS, HEAD_DIM), g_k[l])
        v = v.reshape(B, S, N_HEADS, HEAD_DIM)
        y_attn = dilated_mixture(q, k, v).reshape(B, S, D_ATTN)

        mix = jnp.concatenate([rms_norm(y_conv, g_conv_out[l]),
                               rms_norm(y_attn, g_attn_out[l])], axis=-1)
        x = x + mix @ w_out[l]

        h = rms_norm(x, g_ffn[l])
        x = x + (jax.nn.silu(h @ w_gate[l]) * (h @ w_up[l])) @ w_down[l]
    return x


N_META = 16
GRID_W = 64
Q_BLOCK = 128

A_HEADS = 8
A_HEAD_DIM = 64
A_QK_WIDTH = A_HEADS * 2 * A_HEAD_DIM
A_V_WIDTH = A_HEADS * 2 * A_HEAD_DIM

B_HEADS = 8
B_KV_HEADS = 2
B_GROUP = B_HEADS // B_KV_HEADS
B_HEAD_DIM = 128
B_Q_WIDTH = B_HEADS * B_HEAD_DIM
B_KV_WIDTH = B_KV_HEADS * B_HEAD_DIM
ROPE_THETA = 10000.0

SPLITS = (A_QK_WIDTH, A_QK_WIDTH, A_V_WIDTH, B_Q_WIDTH, B_KV_WIDTH, B_KV_WIDTH, D_MODEL, D_MODEL)
IN_WIDTH = sum(SPLITS)

N_EXPERTS = 16
EXPERT_FF = 512
CAPACITY_FACTOR = 2


def rms_norm_2(x, g):
    xf = x.astype(jnp.float32)
    y = xf * lax.rsqrt(jnp.mean(xf * xf, axis=-1, keepdims=True) + EPS)
    return (y * g.astype(jnp.float32)).astype(x.dtype)

def sweep_queries(block_fn, *qs):
    out_meta = block_fn(*[a[:, :N_META] for a in qs])

    def to_blocks(a):
        r = a[:, N_META:]
        n = r.shape[1] // Q_BLOCK
        r = r.reshape((r.shape[0], n, Q_BLOCK) + r.shape[2:])
        return jnp.moveaxis(r, 1, 0)

    out_real = lax.map(lambda args: block_fn(*args), tuple(to_blocks(a) for a in qs))
    out_real = jnp.moveaxis(out_real, 0, 1)
    out_real = out_real.reshape((out_real.shape[0], -1) + out_real.shape[3:])
    return jnp.concatenate([out_meta, out_real], axis=1)

def alibi_slopes(n_heads):
    return jnp.exp2(-8.0 * jnp.arange(1, n_heads + 1, dtype=jnp.float32) / n_heads)

def diff_attention(q, k, v, pos, slopes, lam):
    scale = A_HEAD_DIM ** -0.5
    k_meta = pos < N_META

    def block(qb, pb):
        qp = pb[0]
        s = jnp.einsum('bqhmd,bkhmd->bhmqk', qb, k).astype(jnp.float32) * scale
        dist = jnp.abs(qp[:, None] - pos[None, :]).astype(jnp.float32)
        dist = jnp.where((qp[:, None] < N_META) | k_meta[None, :], 0.0, dist)
        s = s - slopes[None, :, None, None, None] * dist
        p = jax.nn.softmax(s, axis=-1)
        w = p[:, :, 0] - lam * p[:, :, 1]
        return jnp.einsum('bhqk,bkhe->bqhe', w.astype(v.dtype), v)

    return sweep_queries(block, q, pos[None])

def gqa_attention(q, k, v):
    scale = B_HEAD_DIM ** -0.5

    def block(qb):
        s = jnp.einsum('bqngd,bknd->bngqk', qb, k).astype(jnp.float32) * scale
        p = jax.nn.softmax(s, axis=-1)
        return jnp.einsum('bngqk,bknd->bqngd', p.astype(v.dtype), v)

    return sweep_queries(block, q)

def axial_angles(total_len):
    n_tok = total_len - N_META
    rows = n_tok // GRID_W
    row_id = jnp.repeat(jnp.arange(rows, dtype=jnp.int32), GRID_W)
    col_id = jnp.tile(jnp.arange(GRID_W, dtype=jnp.int32), rows)
    zeros = jnp.zeros((N_META,), jnp.int32)
    row_id = jnp.concatenate([zeros, row_id])
    col_id = jnp.concatenate([zeros, col_id])
    half = B_HEAD_DIM // 2
    inv_freq = ROPE_THETA ** (-jnp.arange(0, half, 2, dtype=jnp.float32) / half)
    return (row_id.astype(jnp.float32)[:, None] * inv_freq[None, :],
            col_id.astype(jnp.float32)[:, None] * inv_freq[None, :])

def rotate(x, ang):
    m = ang.shape[-1]
    cos = jnp.cos(ang)[None, :, None, :].astype(x.dtype)
    sin = jnp.sin(ang)[None, :, None, :].astype(x.dtype)
    x1, x2 = x[..., :m], x[..., m:]
    return jnp.concatenate([x1 * cos - x2 * sin, x2 * cos + x1 * sin], axis=-1)

def axial_rope(x, ang_row, ang_col):
    half = x.shape[-1] // 2
    return jnp.concatenate([rotate(x[..., :half], ang_row), rotate(x[..., half:], ang_col)], axis=-1)

def expert_choice_ffn(u, w_router, w_gate, w_up, w_down):
    b, L, d = u.shape
    cap = CAPACITY_FACTOR * L // N_EXPERTS
    logits = jnp.einsum('bld,de->ble', u, w_router).astype(jnp.float32)
    aff = jax.nn.softmax(logits, axis=-1)
    top_aff, top_idx = lax.top_k(jnp.swapaxes(aff, 1, 2), cap)
    xs = jax.vmap(lambda ub, ib: ub[ib])(u, top_idx)
    hid = jax.nn.silu(jnp.einsum('becd,edf->becf', xs, w_gate)) * jnp.einsum('becd,edf->becf', xs, w_up)
    y = jnp.einsum('becf,efd->becd', hid, w_down) * top_aff[..., None].astype(u.dtype)
    return jax.vmap(lambda yb, ib: jnp.zeros((L, d), yb.dtype).at[ib.reshape(-1)].add(yb.reshape(-1, d)))(y, top_idx)

def second_inputs(seed: int = 0) -> dict:
    key = jax.random.key(seed)
    ks = jax.random.split(key, 24)
    f32 = jnp.float32

    def nrm(k, shape, scale):
        return jax.random.normal(k, shape, f32) * scale

    def gain(k, shape):
        return 1.0 + 0.02 * jax.random.normal(k, shape, f32)

    return {
        'x': nrm(ks[0], (BATCH, SEQ, D_MODEL), 1.0),
        'meta_tokens': nrm(ks[1], (N_META, D_MODEL), 1.0),
        'g_mix': gain(ks[2], (DEPTH, D_MODEL)),
        'w_in': nrm(ks[3], (DEPTH, D_MODEL, IN_WIDTH), D_MODEL ** -0.5),
        'lambda_q1': nrm(ks[4], (DEPTH, A_HEAD_DIM), 0.1),
        'lambda_k1': nrm(ks[5], (DEPTH, A_HEAD_DIM), 0.1),
        'lambda_q2': nrm(ks[6], (DEPTH, A_HEAD_DIM), 0.1),
        'lambda_k2': nrm(ks[7], (DEPTH, A_HEAD_DIM), 0.1),
        'g_subln': gain(ks[8], (DEPTH, 2 * A_HEAD_DIM)),
        'g_qnorm': gain(ks[9], (DEPTH, B_HEAD_DIM)),
        'g_knorm': gain(ks[10], (DEPTH, B_HEAD_DIM)),
        'w_branch_a': nrm(ks[11], (DEPTH, A_V_WIDTH, D_MODEL), A_V_WIDTH ** -0.5),
        'w_branch_b': nrm(ks[12], (DEPTH, B_Q_WIDTH, D_MODEL), B_Q_WIDTH ** -0.5),
        'w_out': nrm(ks[13], (DEPTH, D_MODEL, D_MODEL), D_MODEL ** -0.5),
        'g_ffn': gain(ks[14], (DEPTH, D_MODEL)),
        'w_router': nrm(ks[15], (DEPTH, D_MODEL, N_EXPERTS), D_MODEL ** -0.5),
        'w_gate': nrm(ks[16], (DEPTH, N_EXPERTS, D_MODEL, EXPERT_FF), D_MODEL ** -0.5),
        'w_up': nrm(ks[17], (DEPTH, N_EXPERTS, D_MODEL, EXPERT_FF), D_MODEL ** -0.5),
        'w_down': nrm(ks[18], (DEPTH, N_EXPERTS, EXPERT_FF, D_MODEL), EXPERT_FF ** -0.5),
        'g_final': gain(ks[19], (D_MODEL,)),
    }

def second_block(x, meta_tokens, g_mix, w_in, lambda_q1, lambda_k1, lambda_q2, lambda_k2,
              g_subln, g_qnorm, g_knorm, w_branch_a, w_branch_b, w_out, g_ffn,
              w_router, w_gate, w_up, w_down, g_final):
    b = x.shape[0]
    meta = jnp.broadcast_to(meta_tokens[None].astype(x.dtype), (b, N_META, x.shape[-1]))
    h = jnp.concatenate([meta, x], axis=1)
    L = h.shape[1]
    pos = jnp.arange(L, dtype=jnp.int32)
    ang_row, ang_col = axial_angles(L)
    slopes = alibi_slopes(A_HEADS)
    cut = list(np.cumsum(SPLITS)[:-1])

    for layer in range(DEPTH):
        u = rms_norm_2(h, g_mix[layer])
        z = jnp.einsum('bld,df->blf', u, w_in[layer])
        qa, ka, va, qb, kb, vb, ga, gb = jnp.split(z, cut, axis=-1)

        lam_init = 0.8 - 0.6 * math.exp(-0.3 * layer)
        lam = (jnp.exp(jnp.sum(lambda_q1[layer].astype(jnp.float32) * lambda_k1[layer].astype(jnp.float32)))
               - jnp.exp(jnp.sum(lambda_q2[layer].astype(jnp.float32) * lambda_k2[layer].astype(jnp.float32)))
               + lam_init)
        oa = diff_attention(qa.reshape(b, L, A_HEADS, 2, A_HEAD_DIM),
                            ka.reshape(b, L, A_HEADS, 2, A_HEAD_DIM),
                            va.reshape(b, L, A_HEADS, 2 * A_HEAD_DIM), pos, slopes, lam)
        oa = (rms_norm_2(oa, g_subln[layer]) * (1.0 - lam_init)).reshape(b, L, A_V_WIDTH)

        qh = axial_rope(rms_norm_2(qb.reshape(b, L, B_HEADS, B_HEAD_DIM), g_qnorm[layer]), ang_row, ang_col)
        kh = axial_rope(rms_norm_2(kb.reshape(b, L, B_KV_HEADS, B_HEAD_DIM), g_knorm[layer]), ang_row, ang_col)
        ob = gqa_attention(qh.reshape(b, L, B_KV_HEADS, B_GROUP, B_HEAD_DIM), kh,
                           vb.reshape(b, L, B_KV_HEADS, B_HEAD_DIM)).reshape(b, L, B_Q_WIDTH)

        ya = jnp.einsum('blf,fd->bld', oa, w_branch_a[layer])
        yb = jnp.einsum('blf,fd->bld', ob, w_branch_b[layer])
        merged = jax.nn.sigmoid(ga) * ya + jax.nn.sigmoid(gb) * yb
        h = h + jnp.einsum('bld,de->ble', merged, w_out[layer])

        h = h + expert_choice_ffn(rms_norm_2(h, g_ffn[layer]), w_router[layer], w_gate[layer],
                                  w_up[layer], w_down[layer])

    return rms_norm_2(h, g_final)[:, N_META:]


def setup_inputs(seed=0):
    out = dict(first_inputs(seed))
    for name, value in second_inputs(seed + 1).items():
        if name != "x":
            out[name + "_2"] = value
    return out


def reference(
    x, g_mix, w_in, conv_w, g_q, g_k, g_conv_out, g_attn_out, w_out, g_ffn, w_gate, w_up,
    w_down, meta_tokens_2, g_mix_2, w_in_2, lambda_q1_2, lambda_k1_2, lambda_q2_2, lambda_k2_2,
    g_subln_2, g_qnorm_2, g_knorm_2, w_branch_a_2, w_branch_b_2, w_out_2, g_ffn_2, w_router_2,
    w_gate_2, w_up_2, w_down_2, g_final_2,
):
    x = first_block(
        x, g_mix, w_in, conv_w, g_q, g_k, g_conv_out, g_attn_out, w_out, g_ffn, w_gate, w_up,
        w_down,
    )
    return second_block(
        x, meta_tokens_2, g_mix_2, w_in_2, lambda_q1_2, lambda_k1_2, lambda_q2_2, lambda_k2_2,
        g_subln_2, g_qnorm_2, g_knorm_2, w_branch_a_2, w_branch_b_2, w_out_2, g_ffn_2,
        w_router_2, w_gate_2, w_up_2, w_down_2, g_final_2,
    )


_drawn_inputs = setup_inputs


def setup_inputs(seed=0):
    import zlib

    import numpy as np

    out = dict(_drawn_inputs(seed))
    spreads = {}
    factors = {'g_mix_2': 4.924,
     'lambda_q1_2': 8.0,
     'lambda_k1_2': 4.605,
     'lambda_q2_2': 4.027,
     'lambda_k2_2': 3.119,
     'g_subln_2': 8.0,
     'g_qnorm_2': 8.0,
     'g_knorm_2': 8.0,
     'g_ffn_2': 5.292}
    for name, (base, spread) in spreads.items():
        noise = np.random.default_rng([zlib.crc32(name.encode()), seed]).standard_normal(out[name].shape)
        drawn = base * np.exp(spread * noise) if base else spread * noise
        out[name] = __import__('jax').numpy.asarray(drawn.astype(out[name].dtype))
    for name, factor in factors.items():
        out[name] = (out[name] * factor).astype(out[name].dtype)
    return out
```

```python
from contextlib import ExitStack

import concourse.bass as bass
import numpy as np
from concourse import mybir

F32 = mybir.dt.float32
U32 = mybir.dt.uint32
ALU = mybir.AluOpType
ACT = mybir.ActivationFunctionType
AX = mybir.AxisListType.X

P = 128
D = 1024
KD = D // P
T1 = 1024
META = 16
T2 = T1 + META
CH = 348
TP = 3 * CH
NT = T1 // P
BANK = 512
EPS = 1e-6

DC = 512
DCT = DC // P
HD = 64
FF = 2816
NF = FF // P
QA, KA, VA, QB, KB, VB, GA, GB = 0, 8, 16, 24, 32, 34, 36, 44
HEADS = 8
KV = 2
GROUP = HEADS // KV
HB = 128
NE = 16
EF = 512
EK = EF // P
CAP = 2 * T2 // NE
REST = CAP - P
ROUNDS = -(-CAP // 8)
LAM_INIT = 0.8 - 0.6 * float(np.exp(-0.3 * 0))
BIG = 3.0e38
MASKED = -1.0e30
CREDIT = 1

NORM_GAINS = [n * KD for n in range(4)]
CONV_W = 4 * KD
G_CONV = CONV_W + 3 * DCT
G_ATTN = G_CONV + DCT
G_Q, G_K, G_SUB, G_QN, G_KN = range(G_ATTN + DCT, G_ATTN + DCT + 5)
GAINS = G_KN + 1


def host_constants():
    eye = np.eye(P, dtype=np.float32)
    ones = np.ones((P, P), np.float32)
    block = np.kron(np.eye(2), np.ones((HD, HD))).astype(np.float32)
    swap = np.zeros((P, P), np.float32)
    for half in (0, 64):
        for i in range(32):
            swap[half + 32 + i, half + i] = -1.0
            swap[half + i, half + 32 + i] = 1.0
    delta = np.arange(P)[:, None] - (np.arange(T1)[None, :] - (T1 - P))
    count = np.zeros(delta.shape, np.float32)
    for window, dil in ((128, 1), (512, 4), (2048, 16)):
        count += (delta >= 0) & (delta % dil == 0) & (delta <= window)
    log_count = np.where(count > 0, np.log(np.maximum(count, 1)), MASKED).astype(np.float32)
    neg_dist = -np.abs(np.arange(P)[:, None] - (np.arange(2 * T1 - P)[None, :] - (T1 - P))).astype(np.float32)
    half = HB // 2
    inv = (np.float32(10000.0) ** (-np.arange(0, half, 2, dtype=np.float32) / np.float32(half))).astype(np.float32)
    tok = np.arange(T1)
    row = np.concatenate([tok // 64, np.zeros(META, int)]).astype(np.float32)
    col = np.concatenate([tok % 64, np.zeros(META, int)]).astype(np.float32)
    ang_r, ang_c = inv[:, None] * row[None], inv[:, None] * col[None]
    ang = np.concatenate([ang_r, ang_r, ang_c, ang_c], 0)
    cos = np.cos(ang).astype(np.float32)
    sin = np.sin(ang).astype(np.float32)
    return {"eye": eye, "ones": ones, "block": block, "swap": swap, "log_count": log_count, "neg_dist": neg_dist,
            "cos": cos, "sin": sin}


def build(nc, A, out):
    ctx = ExitStack()
    with ctx:
        base = [-(-nc.sbuf_base // 64) * 64]

        def at(name, shape, offset, dt=F32):
            return nc.alloc_sbuf_tensor_at(name, shape, dt, offset=offset)

        def size(shape):
            return 4 * int(np.prod(shape[1:]))

        def put(name, shape, dt=F32):
            t = at(name, shape, base[0], dt)
            base[0] += -(-size(shape) // 32) * 32
            return t

        class Overlay:

            def __init__(self, start, end):
                self.at, self.end = start, end

            def put(self, name, shape, dt=F32):
                t = at(name, shape, self.at, dt)
                self.at += -(-size(shape) // 32) * 32
                assert self.at <= self.end, (name, self.at, self.end)
                return t

        def sem(name):
            return ctx.enter_context(nc.semaphore(name))

        eye = put("eye_sb", [P, P])
        ones = put("ones_sb", [P, P])
        block64 = put("block_sb", [P, P])
        swap = put("swap_sb", [P, P])
        gains = put("gains_sb", [P, GAINS])
        g_heads = put("g_heads_sb", [P, 3])
        G_Q8, G_SUBI, G_QNS = range(3)
        lams = put("lams_sb", [P, 4, HD])
        lam_sm = put("lam_small", [P, 8])
        eps = put("eps_sb", [P, 1])
        zero = put("zero_sb", [P, 1])
        small = put("small_sb", [P, 64])
        ring = [put(f"ring{j}", [P, KD, P]) for j in range(6)]
        ring0 = base[0] - 6 * 4096
        xT_at = base[0]
        xT = put("xT", [P, KD, TP])
        uT = put("uT", [P, KD, TP])
        norm0 = base[0]
        sq = [put(f"sq{j}", [P, TP]) for j in range(2)]
        acc = put("acc", [P, TP])
        sd = put("sd", [P, TP])
        rs = put("rs", [P, TP])
        scratch = base[0]
        top = nc.sbuf_usable_end

        o = Overlay(scratch, top)
        x_in = o.put("x_in", [P, NT, D])
        meta_in = o.put("meta_in", [META, D])
        o = Overlay(scratch, top)
        mixT = o.put("mixT", [P, KD, T1])
        mix_end = o.at
        u_sb = o.put("u_sb", [P, T1])
        gated = o.put("gated", [P, 2 + T1])
        conv = o.put("conv", [P, T1])
        o = Overlay(mix_end, top)
        y_tok = o.put("y_tok", [P, NT, DC])
        bias1 = o.put("bias1", [P, T1])
        qT1 = o.put("qT1", [P, T1])
        kT1 = o.put("kT1", [P, T1])
        V1 = o.put("V1", [P, NT, P])
        E1 = [o.put(f"E1_{j}", [P, T1]) for j in range(3)]
        PT1 = [o.put(f"PT1_{j}", [P, NT, P]) for j in range(2)]
        ss1 = o.put("ss1", [P, 2 * NT])
        o = Overlay(scratch, top)
        hid = o.put("hid", [P, NF, T1])
        down_w = [at(f"down_w{j}", [P, NF, P], ring0 + j * 12288) for j in range(2)]
        silu1 = sq

        oaT = at("oaT", [P, HEADS, TP], xT_at)
        o = Overlay(scratch, top)
        o_tok = o.put("o_tok", [P, NT + 1, D])
        biasH = o.put("biasH", [P, 2 * T1 - P])
        kmeta = o.put("kmeta", [P, 2 * META])
        qTa = o.put("qTa", [P, TP])
        kTa = o.put("kTa", [P, TP])
        Va = o.put("Va", [P, NT + 1, P])
        EA = [[o.put(f"EA{j}{m}", [P, T2]) for m in range(2)] for j in range(2)]
        PTa = [o.put(f"PTa{j}", [P, NT + 1, P]) for j in range(2)]
        ss2 = at("ss2", [P, NT + 1, HEADS], norm0)
        junk = at("junk", [P, P], norm0 + 512)
        rs2 = at("rs2", [P, NT + 1, HEADS], norm0 + 1024 + 512)
        o = Overlay(scratch, top)
        obT = o.put("obT", [P, HEADS, TP])
        ob_end = o.at
        q_grp = o.put("q_grp", [P, GROUP, T2])
        swapped = o.put("swapped", [P, T2])
        cos = o.put("cos_sb", [P, T2])
        sin = o.put("sin_sb", [P, T2])
        kTb = o.put("kTb", [P, T2])
        Vb = o.put("Vb", [P, NT + 1, HB])
        qs = o.put("qs", [P, T2])
        EB = [o.put(f"EB{j}", [P, T2]) for j in range(2)]
        PTb = [o.put(f"PTb{j}", [P, NT + 1, P]) for j in range(2)]
        o = Overlay(ob_end, top)
        mergedT = o.put("mergedT", [P, KD, TP])
        h_row = [at(f"h_row{j}", [P, D], ring0 + j * 4096) for j in range(2)]
        u_row = [at(f"u_row{j}", [P, D], ring0 + 8192 + j * 4096) for j in range(2)]
        o = Overlay(scratch, top)
        w_gate = o.put("w_gate_sb", [P, EK, KD, P])
        w_up = o.put("w_up_sb", [P, EK, KD, P])
        w_down = o.put("w_down_sb", [P, EK, D])
        xs = [o.put("xs_a", [P, D]), o.put("xs_b", [REST, D])]
        xsT = o.put("xsT", [P, KD, CAP])
        hidT = o.put("hidT", [P, EK, CAP])
        silu_e = [o.put(f"silu_e{j}", [P, CAP]) for j in range(2)]
        yT = o.put("yT", [P, KD, CAP])
        y_row = [o.put("y_row_a", [P, D]), o.put("y_row_b", [REST, D])]
        router = o.put("router_sb", [P, KD, NE])
        aff = o.put("aff", [P, NT + 1, NE])
        affT = o.put("affT", [NE, T2])
        best = o.put("best", [NE, 8 * ROUNDS])
        where = o.put("where", [NE, 8 * ROUNDS], U32)
        where_f = o.put("where_f", [NE, 8 * ROUNDS])
        pick = [o.put("pick_a", [P, NE], U32), o.put("pick_b", [REST, NE], U32)]
        pick_g = [o.put("pick_g_a", [P, 1], U32), o.put("pick_g_b", [REST, 1], U32)]
        pick_s = [o.put("pick_s_a", [P, 1], U32), o.put("pick_s_b", [REST, 1], U32)]
        weight = [o.put("weight_a", [P, NE]), o.put("weight_b", [REST, NE])]
        fin = [at(f"fin{j}", [P, D], xT_at + j * 4096) for j in range(NT)]
        g_fin = at("g_fin", [P, D], xT_at + TP * 4 * KD)
        fin_sq = at("fin_sq", [P, D], xT_at + TP * 4 * KD + 4096)
        fin_s = at("fin_s", [P, 3, NT], xT_at + TP * 4 * KD + 8192)

        PS = ctx.enter_context(nc.psum_tensor("PS", [P, 8, BANK], F32))

        def bank(b, n=BANK, start=0, rows=P):
            return PS[0:rows, b, start:start + n]

        def banks(b, n, width):
            return PS[:, b:b + n, 0:width]

        def wide(b, n, rows=P):
            return PS[0:rows, :, :].rearrange("p b n -> p (b n)")[:, b * BANK:b * BANK + n]

        def thirds(t):
            return t.rearrange("p (n w) -> p n w", w=CH)

        x_keep = nc.dram_tensor("x_keep", (P, KD, TP), F32, kind="Internal").ap()
        h_rows = nc.dram_tensor("h_rows", (T2, D), F32, kind="Internal").ap()
        u_rows = nc.dram_tensor("u_rows", (T2, D), F32, kind="Internal").ap()

        def cols(w, tile):
            return w[bass.ds(tile, 1)].rearrange("a p c n -> p (a c) n")

        lasting = """seen eye_ld const_ld gain_ld lam_ld eps_set pad_set gain_set lam_dot lam_exp lam_done dist_ld keep_st as_init""".split()
        first_block = """meta_ld bias_ld x_t x_act x_dve conv_z0 conv_z1 conv_z2 conv_u conv_a conv_k conv_y mix_sq mix_acc cn_sum cn_sd cn_r cn_n
            a1_q a1_k a1_v a1_sq a1_ss a1_sd a1_r a1_qn a1_vs a1_s a1_max a1_e a1_t a1_pt_lo a1_pt_hi a1_o a1_y a1_rd a1_ysq a1_ysd
            a1_yr a1_yn a1_yt a1_mix a1_mixd wo_z wo_x up_g up_u up_s up_h dn_z dn_x""".split()
        second_block = """aa_bias aa_q aa_k aa_v aa_qs aa_ks aa_vs aa_s aa_part aa_max aa_e aa_sm aa_c aa_t aa_pt aa_pt9 aa_o aa_y aa_ssq as_sd
            as_r as_n as_t as_o ob_v ob_vs ob_z ob_raw ob_sq ob_ss ob_sd ob_r ob_sw ob_m ob_m2 ob_m3 ob_q rope_ld bb_qs bb_s bb_part
            bb_max bb_e bb_rd bb_p bb_t bb_pt bb_pt9 bb_o bb_ob mg_ga mg_ya mg_gb mg_yb mg_sa mg_sb mg_ma mg_mb mg_tmp w2_z w2_x
            keep_ld router_ld lg_z lg_set lg_c lg_max lg_sub lg_e lg_sum lg_r lg_aff lg_t lg_tc hr_t hr_c ur_t ur_c tk_max tk_idx
            tk_rep tk_f tk_t tk_c ex_pick_g ex_pick_s ex_xa ex_xb ex_xt ex_xc ex_g ex_u ex_s ex_h ex_y ex_yt ex_r ex_ra ex_rb
            ex_add_a ex_add_b ex_free gfin_ld fin_q fin_sd fin_r fin_o fin_st""".split()
        S = {n: sem(n) for n in lasting}
        first_sems = {n: nc.alloc_semaphore(name=n) for n in first_block}
        S.update(first_sems)
        ring_ld = [sem(f"ring_ld{j}") for j in range(6)]
        xin_lds = [sem(f"xin_ld{j}") for j in range(NT)]
        N = {s: sem(f"norm_{s}") for s in ("sq", "acc", "ss", "sd", "r", "h")}

        def load(sp, j, src):
            sp.dma_start(ring[j][:, :, :], src).then_inc(ring_ld[j], 16)

        def norm_root(act, k, width, src, n_banks, w):
            for c in range(KD):
                if c >= 2:
                    act.wait_ge(N["acc"], k * KD + c - 1)
                act.activation(sq[c % 2][:, 0:width], src[:, c, 0:width], ACT.Square).then_inc(N["sq"], 1)
            act.wait_ge(N["ss"], k + 1)
            act.activation(sd[:, 0:width].rearrange("p (n w) -> p n w", w=w), banks(0, n_banks, w), ACT.Sqrt,
                           scale=1.0 / D, bias=eps[:, :]).then_inc(N["sd"], 1)

        def norm_apply(dve, k, width, src, dst):
            for c in range(KD):
                dve.wait_ge(N["sq"], k * KD + c + 1)
                if c == 0:
                    dve.tensor_copy(acc[:, 0:width], sq[0][:, 0:width]).then_inc(N["acc"], 1)
                else:
                    dve.wait_ge(N["acc"], k * KD + c)
                    dve.tensor_tensor(acc[:, 0:width], acc[:, 0:width], sq[c % 2][:, 0:width], ALU.add).then_inc(N["acc"], 1)
            dve.wait_ge(N["sd"], k + 1)
            dve.reciprocal(rs[:, 0:width], sd[:, 0:width]).then_inc(N["r"], 1)
            dve.wait_ge(N["r"], k + 1)
            for c in range(KD):
                dve.scalar_tensor_tensor(dst[:, c, 0:width], src[:, c, 0:width], gains[:, NORM_GAINS[k] + c:NORM_GAINS[k] + c + 1], rs[:, 0:width],
                                         ALU.mult, ALU.mult).then_inc(N["h"], 1)

        def seen(engine):
            engine.sem_inc(S["seen"], 1)

        mm = nc.tensor.matmul

        def turn(out, in_, k=P):
            return nc.tensor.transpose(out, in_, eye[0:k, 0:k])

        def project(w, src, first, n, width):
            for c in range(KD):
                for b in range(n):
                    last = mm(bank(first + b, width), w[:, c, :], src[:, c, b * width:(b + 1) * width], start=(c == 0), stop=(c == KD - 1))
            return last

        def total(first, n, width, src):
            for b in range(n):
                last = mm(bank(first + b, width), ones[:, :], src[:, b * width:(b + 1) * width], start=True, stop=True)
            return last

        def norm_sum(pe, k, n, width):
            pe.wait_ge(N["acc"], (k + 1) * KD)
            total(0, n, width, acc).then_inc(N["ss"], 1)

        def residual(dve, d, first, n, w, done, count):
            x = xT[:, bass.ds(d, 1), 0:n * w].rearrange("p a (n w) -> p (a n) w", w=w)
            dve.tensor_tensor(x, x, banks(first, n, w), ALU.add).then_inc(S[done], 1)

        with nc.Block() as block:
            @block.sync
            def _(sp):
                for t in range(NT):
                    sp.dma_start(x_in[:, t, :], A["x"][0, t * P:(t + 1) * P, :]).then_inc(xin_lds[t], 16)
                    if t == 0:
                        sp.dma_start(eye[:, :], A["eye"]).then_inc(S["eye_ld"], 16)
                sp.dma_start(meta_in[:, :], A["meta_tokens_2"]).then_inc(S["meta_ld"], 16)
                w_in = A["w_in"]
                for j in range(3):
                    load(sp, j, cols(w_in, j * DCT))
                for j in range(3):
                    load(sp, 3 + j, cols(w_in, (3 + j) * DCT))
                sp.dma_start(ones[:, :], A["ones"]).then_inc(S["const_ld"], 16)
                sp.dma_start(block64[:, :], A["block"]).then_inc(S["const_ld"], 16)
                sp.dma_start(swap[:, :], A["swap"]).then_inc(S["const_ld"], 16)
                with sp.Fori(1, DC // P) as i:
                    for j in range(3):
                        sp.wait_ge(S[f"conv_z{j}"], i)
                        load(sp, j, cols(w_in, j * DCT + i))
                sp.wait_ge(S["x_t"], 2 * NT + 2)
                sp.wait_ge(S["conv_y"], DC // P + CREDIT)
                sp.dma_start(bias1[:, :], A["log_count"]).then_inc(S["bias_ld"], 16)
                with sp.Fori(1, DC // P) as p:
                    for j, done in enumerate(("a1_q", "a1_k")):
                        sp.wait_ge(S[done], p)
                        load(sp, 3 + j, cols(w_in, (3 + j) * DCT + p))
                    sp.wait_ge(S["a1_v"], 2 * p)
                    load(sp, 5, cols(w_in, 5 * DCT + p))
                sp.wait_ge(S["conv_z0"], DC // P)
                sp.wait_ge(S["conv_z1"], DC // P)
                w_out = A["w_out"]
                load(sp, 0, cols(w_out, 0))
                load(sp, 1, cols(w_out, 1))
                with sp.Fori(1, KD // 2) as i:
                    for j in range(2):
                        sp.wait_ge(S["wo_z"], 2 * i - 1 + j)
                        load(sp, j, cols(w_out, i * 2 + j))
                sp.wait_ge(S["a1_v"], 2 * (DC // P))
                sp.wait_ge(S["conv_z2"], DC // P)
                w_g, w_u = A["w_gate"], A["w_up"]
                for j in range(2):
                    load(sp, 2 + 2 * j, cols(w_g, j))
                    load(sp, 3 + 2 * j, cols(w_u, j))
                with sp.Fori(1, NF // 2) as i:
                    for j in range(2):
                        sp.wait_ge(S["up_g"], 2 * i - 1 + j)
                        load(sp, 2 + 2 * j, cols(w_g, i * 2 + j))
                        sp.wait_ge(S["up_u"], 2 * i - 1 + j)
                        load(sp, 3 + 2 * j, cols(w_u, i * 2 + j))
                w_d = A["w_down"]
                sp.wait_ge(S["wo_z"], KD)
                sp.wait_ge(S["up_g"], NF)
                sp.dma_start(down_w[0][:, :, :], cols(w_d, 0)).then_inc(ring_ld[0], 16)
                sp.wait_ge(S["up_u"], NF)
                sp.dma_start(down_w[1][:, :, :], cols(w_d, 1)).then_inc(ring_ld[3], 16)
                with sp.Fori(1, KD // 2) as i:
                    for j in range(2):
                        sp.wait_ge(S["dn_z"], 2 * i - 1 + j)
                        sp.dma_start(down_w[j][:, :, :], cols(w_d, i * 2 + j)).then_inc(ring_ld[3 * j], 16)
                w_in2 = A["w_in_2"]
                sp.wait_ge(S["dn_z"], KD)
                for j, c in enumerate((QA, KA, VA)):
                    load(sp, j, cols(w_in2, c))
                sp.dma_start(biasH[:, :], A["neg_dist"]).then_inc(S["dist_ld"], 16)
                sp.wait_ge(N["h"], 3 * KD)
                sp.dma_start(x_keep, xT[:, :, :]).then_inc(S["keep_st"], 16)

            @block.gpsimd
            def _(pool):
                pool.memset(eps[:, :], EPS).then_inc(S["eps_set"], 1)
                pool.memset(zero[:, :], 0.0).then_inc(S["eps_set"], 1)
                pool.memset(xT[:, :, T2:TP], 0.0).then_inc(S["pad_set"], 1)

            @block.scalar
            def _(act):
                act.sem_inc(S["conv_u"], CREDIT)
                act.dma_start(gains[:, :], A["vectors"]).then_inc(S["gain_ld"], 16)
                for n, g in enumerate(("lambda_q1_2", "lambda_k1_2", "lambda_q2_2", "lambda_k2_2")):
                    act.dma_start(lams[:, n, :], A[g].broadcast_to([P, HD])).then_inc(S["lam_ld"], 16)

                for t in range(NT):
                    act.wait_ge(S["x_t"], 2 * t + 2)
                    act.activation(xT[:, 4:8, t * P:(t + 1) * P], bank(2 * (t % 4) + 1).rearrange("p (c n) -> p c n", n=P), ACT.Copy).then_inc(S["x_act"], 1)
                act.wait_ge(S["x_t"], 2 * NT + 2)
                act.activation(xT[:, 4:8, T1:T2], bank(1, 4 * META).rearrange("p (c n) -> p c n", n=META), ACT.Copy).then_inc(S["x_act"], 1)
                act.wait_ge(S["x_act"], NT + 1)
                act.wait_ge(S["x_dve"], NT + 1)
                act.wait_ge(S["eps_set"], 2)
                norm_root(act, 0, T1, xT, 2, BANK)
                with act.Fori(0, DC // P) as i:
                    act.wait_ge(S["conv_z0"], i + 1)
                    act.wait_ge(S["conv_a"], i + CREDIT)
                    act.activation(u_sb[:, :], wide(0, T1), ACT.Copy).then_inc(S["conv_u"], 1)
                    act.wait_ge(S["conv_y"], i + 1 + CREDIT)
                    act.wait_ge(S["mix_acc"], i + CREDIT)
                    act.activation(sq[0][:, 0:T1], mixT[:, bass.ds(i, 1), :].rearrange("p a n -> p (a n)"), ACT.Square).then_inc(S["mix_sq"], 1)
                act.wait_ge(S["cn_sum"], 1)
                act.activation(sd[:, 0:T1], wide(6, T1), ACT.Sqrt, scale=1.0 / DC, bias=eps[:, :]).then_inc(S["cn_sd"], 1)
                act.wait_ge(S["cn_r"], 1)
                with act.Fori(0, DC // P) as p:
                    for n, done in ((0, "a1_q"), (1, "a1_k")):
                        act.wait_ge(S[done], p + 1)
                        act.activation(sq[n][:, 0:T1], wide(2 * n, T1), ACT.Square).then_inc(S["a1_sq"], 1)
                    for n, buf in ((0, sd), (1, acc)):
                        act.wait_ge(S["a1_ss"], 2 * p + n + 1)
                        act.activation(buf[:, 0:T1], wide(4, T1), ACT.Sqrt, scale=1.0 / HD, bias=eps[:, :]).then_inc(S["a1_sd"], 1)
                        act.wait_ge(S["a1_v"], 2 * p + n + 1)
                        act.activation(V1[:, 4 * n:4 * n + 4, :], bank(6 + n).rearrange("p (t n) -> p t n", n=P), ACT.Copy).then_inc(S["a1_vs"], 1)

                    def pt_hi(u):
                        t = u // 2
                        if t >= 4:
                            act.wait_ge(S["a1_t"], 16 * p + u + 1)
                            act.wait_ge(S["a1_o"], 16 * p + u - 1)
                            act.activation(PT1[u % 2][:, 4:t + 1, :], bank(5, (t - 3) * P).rearrange("p (j n) -> p j n", n=P), ACT.Copy).then_inc(S["a1_pt_hi"], 1)

                    for u in range(16):
                        nk = (u // 2 + 1) * P
                        act.wait_ge(S["a1_max"], 16 * p + u + 1)
                        act.activation(E1[u % 3][:, 0:nk], E1[u % 3][:, 0:nk], ACT.Exp, scale=-1.0, bias=small[:, u % 4:u % 4 + 1],
                                       accum_out=small[:, 4 + u % 4:5 + u % 4]).then_inc(S["a1_e"], 1)
                        if u:
                            pt_hi(u - 1)
                    pt_hi(15)
                for t in range(NT):
                    act.wait_ge(S["a1_y"], 16 * (DC // P) + CREDIT)
                    act.activation(sq[0][:, 0:DC], y_tok[:, t, :], ACT.Square, accum_out=ss1[:, t:t + 1]).then_inc(S["a1_ysq"], 1)
                    act.wait_ge(S["a1_ysq"], t + 1)
                act.activation(ss1[:, NT:2 * NT], ss1[:, 0:NT], ACT.Sqrt, scale=1.0 / DC, bias=eps[:, :]).then_inc(S["a1_ysd"], 1)
                for t in range(0, NT, 2):
                    act.wait_ge(S["a1_yt"], t + 2)
                    for fi in range(4):
                        act.activation(mixT[:, 4 + fi, (t + 1) * P:(t + 2) * P], bank(5, P, fi * P), ACT.Copy, scale=gains[:, G_ATTN + fi:G_ATTN + fi + 1]).then_inc(S["a1_mix"], 1)
                act.wait_ge(S["wo_x"], KD + 2 * CREDIT)
                norm_root(act, 1, T1, xT, 2, BANK)
                with act.Fori(0, NF // 2) as i:
                    for j in range(2):
                        act.wait_ge(S["up_g"], 2 * i + j + 1)
                        act.wait_ge(S["up_h"], 2 * i + j - 1 + 2 * CREDIT)
                        act.activation(silu1[j][:, 0:T1], wide(4 * j, T1), ACT.Silu).then_inc(S["up_s"], 1)
                act.wait_ge(S["dn_x"], KD + 2 * CREDIT)
                act.wait_ge(S["pad_set"], 1)
                norm_root(act, 2, TP, xT, 3, CH)
                act.wait_ge(S["lam_dot"], 2)
                act.activation(lam_sm[:, 2:4], lam_sm[:, 0:2], ACT.Exp).then_inc(S["lam_exp"], 1)

            @block.vector
            def _(dve):
                for n in ("conv_a", "conv_y", "a1_y"):
                    dve.sem_inc(S[n], CREDIT)
                for n in ("up_h", "wo_x", "dn_x"):
                    dve.sem_inc(S[n], 2 * CREDIT)

                for t in range(NT):
                    dve.wait_ge(S["x_t"], 2 * t + 1)
                    dve.tensor_copy(xT[:, 0:4, t * P:(t + 1) * P], bank(2 * (t % 4)).rearrange("p (c n) -> p c n", n=P)).then_inc(S["x_dve"], 1)
                dve.wait_ge(S["x_t"], 2 * NT + 1)
                dve.tensor_copy(xT[:, 0:4, T1:T2], bank(0, 4 * META).rearrange("p (c n) -> p c n", n=META)).then_inc(S["x_dve"], 1)
                dve.wait_ge(S["gain_ld"], 16)
                for dst, src, k in ((G_Q8, G_Q, HD ** -0.5), (G_SUBI, G_SUB, 1.0 - LAM_INIT), (G_QNS, G_QN, HB ** -0.5)):
                    dve.tensor_scalar(g_heads[:, dst:dst + 1], gains[:, src:src + 1], float(k), None, ALU.mult).then_inc(S["gain_set"], 1)
                norm_apply(dve, 0, T1, xT, uT)
                dve.memset(acc[:, 0:T1], 0.0).then_inc(S["mix_acc"], 1)
                dve.memset(gated[:, 0:2], 0.0).then_inc(S["conv_k"], 1)
                with dve.Fori(0, DC // P) as i:
                    k0 = i * 3 + 1
                    dve.wait_ge(S["conv_z2"], i + 1)
                    dve.wait_ge(S["conv_u"], i + 1 + CREDIT)
                    dve.wait_ge(S["conv_k"], k0)
                    dve.tensor_tensor(gated[:, 2:2 + T1], wide(4, T1), u_sb[:, :], ALU.mult).then_inc(S["conv_a"], 1)
                    dve.wait_ge(S["conv_a"], i + 1 + CREDIT)
                    for k in range(3):
                        w = gains[:, bass.ds(CONV_W + (2 - k) * DCT + i, 1)]
                        src = gated[:, 2 - k:2 - k + T1]
                        if k == 0:
                            dve.wait_ge(S["conv_y"], i + CREDIT)
                            dve.tensor_scalar(conv[:, :], src, w, None, ALU.mult).then_inc(S["conv_k"], 1)
                        else:
                            dve.wait_ge(S["conv_k"], k0 + k)
                            dve.scalar_tensor_tensor(conv[:, :], src, w, conv[:, :], ALU.mult, ALU.add).then_inc(S["conv_k"], 1)
                    dve.wait_ge(S["conv_k"], k0 + 3)
                    dve.wait_ge(S["conv_z1"], i + 1)
                    dve.tensor_tensor(mixT[:, bass.ds(i, 1), :].rearrange("p a n -> p (a n)"), wide(2, T1), conv[:, :], ALU.mult).then_inc(S["conv_y"], 1)
                    dve.wait_ge(S["mix_sq"], i + 1)
                    dve.wait_ge(S["mix_acc"], i + CREDIT)
                    dve.tensor_tensor(acc[:, 0:T1], acc[:, 0:T1], sq[0][:, 0:T1], ALU.add).then_inc(S["mix_acc"], 1)
                dve.wait_ge(S["cn_sd"], 1)
                dve.reciprocal(rs[:, 0:T1], sd[:, 0:T1]).then_inc(S["cn_r"], 1)
                dve.wait_ge(S["cn_r"], 1)
                dve.wait_ge(S["conv_y"], DC // P + CREDIT)
                for i in range(DC // P):
                    dve.scalar_tensor_tensor(mixT[:, i, :], mixT[:, i, :], gains[:, G_CONV + i:G_CONV + i + 1], rs[:, 0:T1], ALU.mult, ALU.mult).then_inc(S["cn_n"], 1)
                dve.wait_ge(S["bias_ld"], 16)
                dve.wait_ge(S["gain_set"], 3)
                dve.wait_ge(S["cn_n"], DCT)
                with dve.Fori(0, DC // P) as p:
                    for n, (dst, root, gain) in enumerate(((qT1, sd, g_heads[:, G_Q8:G_Q8 + 1]), (kT1, acc, gains[:, G_K:G_K + 1]))):
                        if n:
                            dve.wait_ge(S["a1_qn"], 2 * p + 1)
                        dve.wait_ge(S["a1_sd"], 2 * p + n + 1)
                        dve.reciprocal(rs[:, 0:T1], root[:, 0:T1]).then_inc(S["a1_r"], 1)
                        dve.wait_ge(S["a1_r"], 2 * p + n + 1)
                        dve.scalar_tensor_tensor(dst[:, :], wide(2 * n, T1), gain, rs[:, 0:T1], ALU.mult, ALU.mult).then_inc(S["a1_qn"], 1)

                    def scores(u):
                        t, a = u // 2, u % 2
                        nk = (t + 1) * P
                        dve.wait_ge(S["a1_s"], 8 * p + t + 1)
                        if u >= 3:
                            dve.wait_ge(S["a1_t"], 16 * p + u - 2)
                        if u >= 4:
                            dve.wait_ge(S["a1_e"], 16 * p + u - 3)
                        seen(dve)
                        dve.tensor_tensor_reduce(E1[u % 3][:, 0:nk], wide(2 * a, nk), bias1[:, T1 - nk:T1], -1.0, BIG, ALU.add, ALU.min,
                                                 small[:, u % 4:u % 4 + 1]).then_inc(S["a1_max"], 1)

                    def take_pt(u):
                        n = min(u // 2 + 1, 4)
                        dve.wait_ge(S["a1_t"], 16 * p + u + 1)
                        if u >= 2:
                            dve.wait_ge(S["a1_o"], 16 * p + u - 1)
                        dve.tensor_copy(PT1[u % 2][:, 0:n, :], bank(4, n * P).rearrange("p (j n) -> p j n", n=P)).then_inc(S["a1_pt_lo"], 1)

                    def result(u):
                        dve.wait_ge(S["a1_e"], 16 * p + u + 1)
                        dve.reciprocal(small[:, 16 + u % 4:17 + u % 4], small[:, 4 + u % 4:5 + u % 4]).then_inc(S["a1_rd"], 1)
                        dve.wait_ge(S["a1_rd"], 16 * p + u + 1)
                        dve.wait_ge(S["a1_o"], 16 * p + u + 1)
                        dve.tensor_scalar(y_tok[:, u // 2, bass.ds(p * P + (u % 2) * HD, HD)], bank(6 + u % 2, HD), small[:, 16 + u % 4:17 + u % 4],
                                          None, ALU.mult).then_inc(S["a1_y"], 1)

                    for u in range(16):
                        scores(u)
                        if u >= 1:
                            take_pt(u - 1)
                        if u >= 2:
                            result(u - 2)
                    take_pt(15)
                    result(14)
                    result(15)
                dve.wait_ge(S["a1_ysd"], 1)
                dve.reciprocal(ss1[:, 0:NT], ss1[:, NT:2 * NT]).then_inc(S["a1_yr"], 1)
                dve.wait_ge(S["a1_yr"], 1)
                for t in range(NT):
                    dve.tensor_scalar(y_tok[:, t, :], y_tok[:, t, :], ss1[:, t:t + 1], None, ALU.mult).then_inc(S["a1_yn"], 1)
                for t in range(0, NT, 2):
                    dve.wait_ge(S["a1_yt"], t + 1)
                    for fi in range(4):
                        dve.tensor_scalar(mixT[:, 4 + fi, t * P:(t + 1) * P], bank(4, P, fi * P), gains[:, G_ATTN + fi:G_ATTN + fi + 1], None, ALU.mult).then_inc(S["a1_mixd"], 1)
                with dve.Fori(0, KD // 2) as i:
                    for j in range(2):
                        dve.wait_ge(S["wo_z"], 2 * i + j + 1)
                        residual(dve, 2 * i + j, 2 * j, 2, BANK, "wo_x", None)
                dve.wait_ge(S["wo_x"], KD + 2 * CREDIT)
                norm_apply(dve, 1, T1, xT, uT)
                with dve.Fori(0, NF // 2) as i:
                    for j in range(2):
                        dve.wait_ge(S["up_s"], 2 * i + j + 1)
                        dve.wait_ge(S["up_u"], 2 * i + j + 1)
                        dve.tensor_tensor(hid[:, bass.ds(2 * i + j, 1), :].rearrange("p a n -> p (a n)"), silu1[j][:, 0:T1], wide(4 * j + 2, T1), ALU.mult).then_inc(S["up_h"], 1)
                with dve.Fori(0, KD // 2) as i:
                    for j in range(2):
                        dve.wait_ge(S["dn_z"], 2 * i + j + 1)
                        residual(dve, 2 * i + j, 2 * j, 2, BANK, "dn_x", None)
                dve.wait_ge(S["dn_x"], KD + 2 * CREDIT)
                norm_apply(dve, 2, TP, xT, uT)
                dve.wait_ge(S["lam_ld"], 64)
                for n in range(2):
                    dve.tensor_tensor_reduce(junk[:, n * HD:(n + 1) * HD], lams[:, 2 * n, :], lams[:, 2 * n + 1, :], 1.0, 0.0, ALU.mult, ALU.add,
                                             lam_sm[:, n:n + 1]).then_inc(S["lam_dot"], 1)
                dve.wait_ge(S["lam_exp"], 1)
                dve.tensor_scalar(lam_sm[:, 4:5], lam_sm[:, 3:4], lam_sm[:, 2:3], -LAM_INIT, ALU.subtract, ALU.add).then_inc(S["lam_done"], 1)
                dve.wait_ge(S["lam_done"], 1)
                dve.memset(ss2[:, :, :], 1.0).then_inc(S["as_init"], 1)

            @block.tensor
            def _(pe):
                pe.wait_ge(S["eye_ld"], 16)
                for t in range(NT):
                    pe.wait_ge(xin_lds[t], 16)
                    for half in range(2):
                        if t >= 4:
                            pe.wait_ge(S["x_act" if half else "x_dve"], t - 3)
                        for c in range(4):
                            last = turn(bank(2 * (t % 4) + half, P, c * P), x_in[:, t, (4 * half + c) * P:(4 * half + c + 1) * P])
                        last.then_inc(S["x_t"], 1)
                pe.wait_ge(S["meta_ld"], 16)
                for half in range(2):
                    pe.wait_ge(S["x_act" if half else "x_dve"], 5)
                    for c in range(4):
                        last = turn(bank(half, META, c * META), meta_in[:, (4 * half + c) * P:(4 * half + c + 1) * P], META)
                    last.then_inc(S["x_t"], 1)
                pe.wait_ge(S["const_ld"], 48)
                pe.wait_ge(S["x_dve"], NT + 1)
                norm_sum(pe, 0, 2, BANK)
                pe.wait_ge(N["sd"], 1)
                pe.wait_ge(N["h"], KD)
                with pe.Fori(0, DC // P) as i:
                    for j, free in enumerate(("conv_u", "conv_y", "conv_a")):
                        pe.wait_ge(S[free], i + CREDIT)
                        pe.wait_ge(ring_ld[j], 16 * i + 16)
                        project(ring[j], uT, 2 * j, 2, BANK).then_inc(S[f"conv_z{j}"], 1)
                pe.wait_ge(S["mix_acc"], DC // P + CREDIT)
                total(6, 2, BANK, acc).then_inc(S["cn_sum"], 1)
                pe.wait_ge(S["conv_y"], DC // P + CREDIT)
                pe.wait_ge(S["cn_sd"], 1)
                with pe.Fori(0, DC // P) as p:
                    pe.wait_ge(ring_ld[3], 16 * p + 16)
                    project(ring[3], uT, 0, 2, BANK).then_inc(S["a1_q"], 1)
                    pe.wait_ge(ring_ld[4], 16 * p + 16)
                    project(ring[4], uT, 2, 2, BANK).then_inc(S["a1_k"], 1)
                    pe.wait_ge(ring_ld[5], 16 * p + 16)
                    pe.wait_ge(S["a1_y"], 16 * p + CREDIT)
                    for n, root in ((0, sq[0]), (1, sq[1])):
                        pe.wait_ge(S["a1_sq"], 2 * p + n + 1)
                        if n:
                            pe.wait_ge(S["a1_sd"], 2 * p + 1)
                        for b in range(2):
                            last = mm(bank(4 + b), block64[:, :], root[:, b * BANK:(b + 1) * BANK], start=True, stop=True)
                        last.then_inc(S["a1_ss"], 1)
                        for t in range(4 * n, 4 * n + 4):
                            for c in range(KD):
                                last = mm(bank(6 + n, P, (t % 4) * P), uT[:, c, t * P:(t + 1) * P], ring[5][:, c, :], start=(c == 0), stop=(c == KD - 1))
                        last.then_inc(S["a1_v"], 1)

                    def scores(t):
                        nk = (t + 1) * P
                        if t == 0:
                            pe.wait_ge(S["a1_qn"], 2 * p + 2)
                        else:
                            pe.wait_ge(S["a1_max"], 16 * p + 2 * t)
                        for k0 in range(0, nk, BANK):
                            k1 = min(nk, k0 + BANK)
                            for a in range(2):
                                r = slice(a * HD, (a + 1) * HD)
                                last = mm(bank(2 * a + k0 // BANK, k1 - k0), qT1[r, t * P:(t + 1) * P], kT1[r, k0:k1], start=True, stop=True)
                        last.then_inc(S["a1_s"], 1)

                    def turn_probs(u):
                        pe.wait_ge(S["a1_e"], 16 * p + u + 1)
                        for j in range(u // 2 + 1):
                            last = turn(bank(4 + j // 4, P, (j % 4) * P), E1[u % 3][:, j * P:(j + 1) * P])
                        last.then_inc(S["a1_t"], 1)

                    def values(u):
                        t, a = u // 2, u % 2
                        pe.wait_ge(S["a1_pt_lo"], 16 * p + u + 1)
                        if u >= 8:
                            pe.wait_ge(S["a1_pt_hi"], 8 * p + u - 7)
                        if u >= 2:
                            pe.wait_ge(S["a1_y"], 16 * p + u - 1 + CREDIT)
                        else:
                            pe.wait_ge(S["a1_vs"], 2 * p + 2)
                        for j in range(t + 1):
                            last = mm(bank(6 + a, HD), PT1[u % 2][:, j, :], V1[:, j, a * HD:(a + 1) * HD], start=(j == 0), stop=(j == t))
                        last.then_inc(S["a1_o"], 1)

                    scores(0)
                    for t in range(NT):
                        if t + 1 < NT:
                            scores(t + 1)
                        for u in (2 * t, 2 * t + 1):
                            if u:
                                values(u - 1)
                            turn_probs(u)
                    values(15)
                for t in range(NT):
                    pe.wait_ge(S["a1_yn"], t + 1)
                    if t >= 2:
                        pe.wait_ge(S["a1_mix" if t % 2 else "a1_mixd"], 4 * (t // 2))
                    for fi in range(4):
                        last = turn(bank(4 + t % 2, P, fi * P), y_tok[:, t, fi * P:(fi + 1) * P])
                    last.then_inc(S["a1_yt"], 1)
                pe.wait_ge(S["cn_n"], DC // P)
                pe.wait_ge(S["a1_mix"], 2 * NT)
                pe.wait_ge(S["a1_mixd"], 2 * NT)
                with pe.Fori(0, KD // 2) as i:
                    for j in range(2):
                        pe.wait_ge(ring_ld[j], 16 * (DC // P) + 16 * i + 16)
                        pe.wait_ge(S["wo_x"], 2 * i + j - 1 + 2 * CREDIT)
                        project(ring[j], mixT, 2 * j, 2, BANK).then_inc(S["wo_z"], 1)
                norm_sum(pe, 1, 2, BANK)
                pe.wait_ge(N["h"], 2 * KD)
                with pe.Fori(0, NF // 2) as i:
                    for j in range(2):
                        pe.wait_ge(S["up_h"], 2 * i + j - 1 + 2 * CREDIT)
                        pe.wait_ge(ring_ld[2 + 2 * j], 16 * (DC // P) + 16 * i + 16)
                        project(ring[2 + 2 * j], uT, 4 * j, 2, BANK).then_inc(S["up_g"], 1)
                        pe.wait_ge(ring_ld[3 + 2 * j], 16 * (DC // P) + 16 * i + 16)
                        project(ring[3 + 2 * j], uT, 4 * j + 2, 2, BANK).then_inc(S["up_u"], 1)
                pe.wait_ge(S["up_h"], NF + 2 * CREDIT)
                with pe.Fori(0, KD // 2) as i:
                    for j in range(2):
                        pe.wait_ge(ring_ld[3 * j], 16 * (DC // P + (NF // 2 if j else KD // 2)) + 16 * i + 16)
                        pe.wait_ge(S["dn_x"], 2 * i + j - 1 + 2 * CREDIT)
                        for c in range(NF):
                            for b in range(2):
                                last = mm(bank(2 * j + b), down_w[j][:, c, :], hid[:, c, b * BANK:(b + 1) * BANK], start=(c == 0), stop=(c == NF - 1))
                        last.then_inc(S["dn_z"], 1)
                norm_sum(pe, 2, 3, CH)

        nc.clear_and_free_semaphores(list(first_sems.values()))
        nc.all_engine_barrier()
        S.update({n: sem(n) for n in second_block})
        gate_ld = [sem(f"gate_ld{j}") for j in range(EK)]
        up_ld = [sem(f"up_ld{j}") for j in range(EK)]
        down_ld = sem("down_ld")
        row_st = [sem(f"row_st{j}") for j in range(4)]

        with nc.Block() as block:
            @block.sync
            def _(sp):
                w_in2 = A["w_in_2"]
                with sp.Fori(1, HEADS) as h:
                    for j, (c, done, k) in enumerate(((QA, "aa_q", 1), (KA, "aa_k", 1), (VA, "aa_v", 3))):
                        sp.wait_ge(S[done], k * h)
                        load(sp, j, cols(w_in2, c + h))
                load(sp, 3, cols(w_in2, VB))
                load(sp, 4, cols(w_in2, KB))
                sp.wait_ge(S["as_t"], 2 * (NT + 1))
                sp.dma_start(cos[:, :], A["cos"]).then_inc(S["rope_ld"], 16)
                sp.dma_start(sin[:, :], A["sin"]).then_inc(S["rope_ld"], 16)
                for g in range(KV):
                    n0 = g * (GROUP + 1)
                    if g:
                        sp.wait_ge(S["ob_v"], 3 * g)
                        load(sp, 3, cols(w_in2, VB + g))
                        sp.wait_ge(S["ob_z"], n0)
                        load(sp, 4, cols(w_in2, KB + g))
                    for j in range(GROUP):
                        if n0 + j:
                            sp.wait_ge(S["ob_z"], n0 + j + (1 if j else 0))
                        load(sp, 5, cols(w_in2, QB + (g * GROUP + j)))
                w_a, w_b = A["w_branch_a_2"], A["w_branch_b_2"]
                sp.wait_ge(S["aa_v"], 3 * HEADS)
                load(sp, 0, cols(w_in2, GA))
                load(sp, 1, cols(w_a, 0))
                load(sp, 2, cols(w_in2, GB))
                sp.wait_ge(S["ob_v"], 3 * KV)
                load(sp, 3, cols(w_b, 0))
                with sp.Fori(1, KD) as d:
                    for j, (w, c, done) in enumerate(((w_in2, GA, "mg_ga"), (w_a, 0, "mg_ya"),
                                                      (w_in2, GB, "mg_gb"), (w_b, 0, "mg_yb"))):
                        sp.wait_ge(S[done], d)
                        load(sp, j, cols(w, c + d))
                w_out2 = A["w_out_2"]
                sp.wait_ge(S["ob_z"], KV * (GROUP + 1))
                load(sp, 4, cols(w_out2, 0))
                load(sp, 5, cols(w_out2, 1))
                sp.wait_ge(S["mg_yb"], KD)
                sp.wait_ge(S["keep_st"], 16)
                sp.dma_start(xT[:, :, :], x_keep).then_inc(S["keep_ld"], 16)
                with sp.Fori(1, KD // 2) as i:
                    for j in range(2):
                        sp.wait_ge(S["w2_z"], 2 * i - 1 + j)
                        load(sp, 4 + j, cols(w_out2, i * 2 + j))
                sp.wait_ge(S["w2_z"], KD)
                sp.dma_start(router[:, :, :], A["w_router_2"][0].rearrange("(c p) n -> p c n", p=P)).then_inc(S["router_ld"], 16)
                wg, wu, wd = A["w_gate_2"], A["w_up_2"], A["w_down_2"][0]

                def expert_cols(w, e, j):
                    return w[bass.ds(e, 1), j].rearrange("a p c n -> p (a c) n")

                def expert_rows(w, e, j):
                    return w[bass.ds(e, 1), j * P:(j + 1) * P, :].rearrange("a p n -> p (a n)")

                for j in range(EK):
                    sp.dma_start(w_gate[:, j, :, :], expert_cols(wg, 0, j)).then_inc(gate_ld[j], 16)
                    sp.dma_start(w_up[:, j, :, :], expert_cols(wu, 0, j)).then_inc(up_ld[j], 16)
                for j in range(EK):
                    sp.dma_start(w_down[:, j, :], expert_rows(wd, 0, j)).then_inc(down_ld, 16)
                for t in range(NT + 1):
                    rows = P if t < NT else META
                    r0 = META + t * P if t < NT else 0
                    sp.wait_ge(S["hr_c"], 2 * (t + 1))
                    sp.dma_start(h_rows[r0:r0 + rows, :], h_row[t % 2][0:rows, :]).then_inc(row_st[t % 2], 16)
                    sp.wait_ge(S["ur_c"], 2 * (t + 1))
                    sp.dma_start(u_rows[r0:r0 + rows, :], u_row[t % 2][0:rows, :]).then_inc(row_st[2 + t % 2], 16)
                with sp.Fori(1, NE) as e:
                    for j in range(EK):
                        sp.wait_ge(S["ex_g"], e * EK - (EK - 1) + j)
                        sp.dma_start(w_gate[:, j, :, :], expert_cols(wg, e, j)).then_inc(gate_ld[j], 16)
                        sp.wait_ge(S["ex_u"], e * EK - (EK - 1) + j)
                        sp.dma_start(w_up[:, j, :, :], expert_cols(wu, e, j)).then_inc(up_ld[j], 16)
                    sp.wait_ge(S["ex_y"], 3 * e)
                    for j in range(EK):
                        sp.dma_start(w_down[:, j, :], expert_rows(wd, e, j)).then_inc(down_ld, 16)
                sp.wait_ge(S["ur_t"], 2 * (NT + 1))
                sp.dma_start(g_fin[:, :], A["g_final_2"].rearrange("(a n) -> a n", a=1).broadcast_to([P, D])).then_inc(S["gfin_ld"], 16)
                sp.wait_ge(S["ex_add_a"], 16 * NE)
                sp.wait_ge(S["ex_add_b"], 16 * NE)
                for t in range(NT):
                    sp.dma_start(fin[t][:, :], h_rows[META + t * P:META + (t + 1) * P, :]).then_inc(xin_lds[t], 16)
                for t in range(NT):
                    sp.wait_ge(S["fin_o"], t + 1)
                    sp.dma_start(out[0, t * P:(t + 1) * P, :], fin[t][:, :]).then_inc(S["fin_st"], 16)
                sp.wait_ge(S["fin_st"], 16 * NT)

            @block.gpsimd
            def _(pool):
                pool.wait_ge(S["dist_ld"], 16)
                with pool.Fori(0, HEADS) as h:
                    pool.wait_ge(S["aa_max"], h * (2 * NT + 2) + CREDIT)
                    seen(pool)
                    pool.tensor_scalar(biasH[:, :], biasH[:, :], 0.5, None, ALU.mult).then_inc(S["aa_bias"], 1)
                for g in range(KV):
                    with pool.Fori(0, GROUP) as j:
                        pool.wait_ge(S["ob_q"], g * (GROUP + 1) + 2 + j)
                        pool.wait_ge(S["bb_s"], (g * GROUP + j) * (NT + 1) + CREDIT)
                        seen(pool)
                        pool.tensor_copy(qs[:, :], q_grp[:, bass.ds(j, 1), :].rearrange("p a n -> p (a n)")).then_inc(S["bb_qs"], 1)
                pool.sem_inc(S["ex_free"], CREDIT)
                pool.wait_ge(S["tk_c"], 4)
                for j in range(4):
                    pool.wait_ge(row_st[j], 16 * ((NT + 2 - j % 2) // 2))

                def gather(e):
                    for r in range(2):
                        pool.tensor_copy(pick_g[r][:, :], pick[r][:, bass.ds(e, 1)]).then_inc(S["ex_pick_g"], 1)
                    pool.wait_ge(S["ex_pick_g"], e * 2 + 2)
                    seen(pool)
                    for r, done in enumerate(("ex_xa", "ex_xb")):
                        pool.indirect_dma_start(xs[r][:, :], None, u_rows, bass.IndirectOffsetOnAxis(ap=pick_g[r][:, :], axis=0)).then_inc(S[done], 16)

                def scatter(e):
                    for r in range(2):
                        pool.tensor_copy(pick_s[r][:, :], pick[r][:, bass.ds(e, 1)]).then_inc(S["ex_pick_s"], 1)
                    pool.wait_ge(S["ex_pick_s"], e * 2 + 2)
                    for r, (rows, done) in enumerate((("ex_ra", "ex_add_a"), ("ex_rb", "ex_add_b"))):
                        pool.wait_ge(S[rows], e * 2 + 2 + CREDIT)
                        seen(pool)
                        pool.indirect_dma_start(h_rows, bass.IndirectOffsetOnAxis(ap=pick_s[r][:, :], axis=0), y_row[r][:, :], None,
                                                compute_op=ALU.add).then_inc(S[done], 16)
                    pool.wait_ge(S["ex_add_a"], e * 16 + 16)
                    pool.wait_ge(S["ex_add_b"], e * 16 + 16)
                    pool.sem_inc(S["ex_free"], 1)

                gather(0)
                with pool.Fori(0, NE - 1) as e:
                    pool.wait_ge(S["ex_xt"], e * 3 + 3)
                    gather(e + 1)
                    scatter(e)
                scatter(NE - 1)

            @block.scalar
            def _(act):
                act.wait_ge(S["as_init"], 1)
                with act.Fori(0, HEADS) as h:
                    act.wait_ge(S["aa_q"], h + 1)
                    act.activation(thirds(qTa[:, :]), banks(0, 3, CH), ACT.Copy, scale=HD ** -0.5).then_inc(S["aa_qs"], 1)
                    for n in range(2):
                        act.wait_ge(S["aa_v"], 3 * h + n + 1)
                        act.activation(Va[:, 4 * n:4 * n + 4, :], bank(6 + n).rearrange("p (t n) -> p t n", n=P), ACT.Copy).then_inc(S["aa_vs"], 1)
                    act.wait_ge(S["aa_v"], 3 * h + 3)
                    act.activation(Va[0:META, NT, :], bank(0, P, 0, META), ACT.Copy).then_inc(S["aa_vs"], 1)

                    def take_pt(t):
                        m = P if t < NT else META
                        act.wait_ge(S["aa_t"], 9 * h + t + 1)
                        if t >= 2:
                            act.wait_ge(S["aa_o"], 9 * h + t - 1)
                        act.activation(PTa[t % 2][:, 0:NT, 0:m], wide(5, NT * P).rearrange("p (j n) -> p j n", n=P)[:, :, 0:m], ACT.Copy).then_inc(S["aa_pt"], 1)
                        act.activation(PTa[t % 2][0:META, NT, 0:m], bank(7, m, 256, META), ACT.Copy).then_inc(S["aa_pt9"], 1)

                    def square(t):
                        m = P if t < NT else META
                        act.wait_ge(S["aa_y"], 9 * h + t + 1 + CREDIT)
                        act.activation(junk[0:m, :], o_tok[0:m, t, bass.ds(h * P, P)], ACT.Square,
                                       accum_out=ss2[0:m, t, bass.ds(h, 1)]).then_inc(S["aa_ssq"], 1)
                        act.wait_ge(S["aa_ssq"], 9 * h + t + 1)

                    for t in range(NT + 1):
                        m = P if t < NT else META
                        for k in range(2):
                            act.wait_ge(S["aa_max"], 18 * h + 2 * t + k + 1 + CREDIT)
                            e = EA[t % 2][k]
                            act.activation(e[0:m, :], e[0:m, :], ACT.Exp, scale=-1.0, bias=small[0:m, 8 + 2 * (t % 2) + k:9 + 2 * (t % 2) + k],
                                           accum_out=small[0:m, 12 + 2 * (t % 2) + k:13 + 2 * (t % 2) + k]).then_inc(S["aa_e"], 1)
                        if t >= 1:
                            take_pt(t - 1)
                        if t >= 3:
                            square(t - 3)
                    take_pt(NT)
                    for t in range(NT - 2, NT + 1):
                        square(t)
                act.wait_ge(S["aa_ssq"], 9 * HEADS)
                act.activation(rs2[:, :, :], ss2[:, :, :], ACT.Sqrt, scale=1.0 / P, bias=eps[:, :]).then_inc(S["as_sd"], 1)
                for t in range(NT + 1):
                    m = P if t < NT else META
                    act.wait_ge(S["as_t"], 2 * t + 1)
                    act.activation(oaT[:, 0:4, t * P:t * P + m], bank(4 * (t % 2)).rearrange("p (c n) -> p c n", n=P)[:, :, 0:m], ACT.Copy,
                                   scale=g_heads[:, G_SUBI:G_SUBI + 1]).then_inc(S["as_o"], 1)
                    act.wait_ge(S["as_t"], 2 * t + 2)
                    act.activation(oaT[:, 4:8, t * P:t * P + m], bank(4 * (t % 2) + 1).rearrange("p (c n) -> p c n", n=P)[:, :, 0:m], ACT.Copy,
                                   scale=g_heads[:, G_SUBI:G_SUBI + 1]).then_inc(S["as_o"], 1)
                for g in range(KV):
                    v0, z0 = 3 * g, g * (GROUP + 1)
                    for n in range(2):
                        act.wait_ge(S["ob_v"], v0 + n + 1)
                        act.activation(Vb[:, 4 * n:4 * n + 4, :], bank(6 + n).rearrange("p (t n) -> p t n", n=P), ACT.Copy).then_inc(S["ob_vs"], 1)
                    act.wait_ge(S["ob_v"], v0 + 3)
                    act.activation(Vb[0:META, NT, :], bank(5, P, 0, META), ACT.Copy).then_inc(S["ob_vs"], 1)

                    def raw(n):
                        i = z0 + n
                        gain = g_heads[:, G_QNS:G_QNS + 1] if n else gains[:, G_KN:G_KN + 1]
                        act.wait_ge(S["ob_z"], i + 1)
                        if i >= 1:
                            act.wait_ge(S["ob_ss"], i)
                            act.wait_ge(S["ob_m"], i)
                            act.wait_ge(S["ob_sw"], i)
                        act.activation(thirds(acc[:, :]), banks(3 * (n % 2), 3, CH), ACT.Copy, scale=gain).then_inc(S["ob_raw"], 1)
                        act.activation(thirds(sq[0][:, :]), banks(3 * (n % 2), 3, CH), ACT.Square).then_inc(S["ob_sq"], 1)

                    def root(n):
                        i = z0 + n
                        act.wait_ge(S["ob_ss"], i + 1)
                        if i >= 1:
                            act.wait_ge(S["ob_r"], i)
                        act.activation(sd[:, 0:T1], wide(6, T1), ACT.Sqrt, scale=1.0 / HB, bias=eps[:, :]).then_inc(S["ob_sd"], 1)
                        act.activation(sd[:, T1:T2], bank(3 * (n % 2) + 2, META, 384), ACT.Sqrt, scale=1.0 / HB, bias=eps[:, :]).then_inc(S["ob_sd"], 1)

                    for n in range(GROUP + 1):
                        raw(n)
                        root(n)
                    with act.Fori(0, GROUP) as j:
                        def head(j):
                            return (g * GROUP + j) * 9

                        def take_pt(t):
                            m = P if t < NT else META
                            act.wait_ge(S["bb_t"], head(j) + t + 1)
                            if t >= 2:
                                act.wait_ge(S["bb_o"], head(j) + t - 1)
                            act.activation(PTb[t % 2][:, 0:NT, 0:m], wide(5, NT * P).rearrange("p (j n) -> p j n", n=P)[:, :, 0:m], ACT.Copy).then_inc(S["bb_pt"], 1)
                            act.activation(PTb[t % 2][0:META, NT, 0:m], bank(7, m, 256, META), ACT.Copy).then_inc(S["bb_pt9"], 1)

                        for t in range(NT + 1):
                            m = P if t < NT else META
                            act.wait_ge(S["bb_max"], head(j) + t + 1)
                            act.activation(EB[t % 2][0:m, :], EB[t % 2][0:m, :], ACT.Exp, scale=-1.0, bias=small[0:m, 24 + t % 2:25 + t % 2],
                                           accum_out=small[0:m, 26 + t % 2:27 + t % 2]).then_inc(S["bb_e"], 1)
                            if t >= 1:
                                take_pt(t - 1)
                        take_pt(NT)
                with act.Fori(0, KD) as d:
                    for k, (z, done, used) in enumerate((("mg_ga", "mg_sa", "mg_ma"), ("mg_gb", "mg_sb", "mg_mb"))):
                        act.wait_ge(S[z], d + 1)
                        act.wait_ge(S[used], d + CREDIT)
                        act.activation(thirds(sq[k][:, :]), banks(0, 3, CH), ACT.Sigmoid).then_inc(S[done], 1)
                act.wait_ge(S["w2_x"], KD + 2 * CREDIT)
                norm_root(act, 3, TP, xT, 3, CH)
                act.wait_ge(S["lg_sub"], 1)
                act.activation(aff[:, :, :], aff[:, :, :], ACT.Exp).then_inc(S["lg_e"], 1)
                for t in range(NT + 1):
                    rows = P if t < NT else META
                    for buf, first, src, done, st in ((h_row, 6, "hr_t", "hr_c", 0), (u_row, 2, "ur_t", "ur_c", 2)):
                        if t >= 2:
                            act.wait_ge(row_st[st + t % 2], 16 * (t // 2))
                        for n in range(2):
                            act.wait_ge(S[src], 2 * t + n + 1)
                            act.activation(buf[t % 2][0:rows, n * BANK:(n + 1) * BANK], bank(first + n, BANK, 0, rows), ACT.Copy).then_inc(S[done], 1)
                act.sem_inc(S["ex_rb"], CREDIT)
                with act.Fori(0, NE) as e:
                    for j in range(EK):
                        act.wait_ge(S["ex_g"], e * EK + j + 1)
                        act.wait_ge(S["ex_h"], e * EK + j - 1 + 2 * CREDIT)
                        act.activation(silu_e[j % 2][:, :], bank(3 + 2 * (j % 2), CAP), ACT.Silu).then_inc(S["ex_s"], 1)
                    act.wait_ge(S["ex_free"], e + CREDIT)
                    for n in range(2):
                        act.wait_ge(S["ex_r"], e * 2 + n + 1)
                        seen(act)
                        act.activation(y_row[1][:, n * BANK:(n + 1) * BANK], bank(5 + n, BANK, 0, REST), ACT.Copy,
                                       scale=weight[1][:, bass.ds(e, 1)]).then_inc(S["ex_rb"], 1)
                for t in range(NT):
                    act.wait_ge(xin_lds[t], 32)
                    act.activation(fin_sq[:, :], fin[t][:, :], ACT.Square, accum_out=fin_s[:, 0, t:t + 1]).then_inc(S["fin_q"], 1)
                    act.wait_ge(S["fin_q"], t + 1)
                    act.activation(fin_s[:, 1, t:t + 1], fin_s[:, 0, t:t + 1], ACT.Sqrt, scale=1.0 / D, bias=eps[:, :]).then_inc(S["fin_sd"], 1)

            @block.vector
            def _(dve):
                for n in ("aa_max", "aa_y", "mg_ma", "mg_mb", "ex_ra"):
                    dve.sem_inc(S[n], CREDIT)
                for n in ("ex_h", "w2_x"):
                    dve.sem_inc(S[n], 2 * CREDIT)
                dve.memset(kmeta[:, :], 0.0).then_inc(S["as_init"], 1)
                dve.wait_ge(S["as_init"], 2)
                with dve.Fori(0, HEADS) as h:
                    dve.wait_ge(S["aa_k"], h + 1)
                    dve.tensor_copy(thirds(kTa[:, :]), banks(3, 3, CH)).then_inc(S["aa_ks"], 1)
                    for k in range(2):
                        half = slice(k * HD, (k + 1) * HD)
                        dve.tensor_copy(kmeta[half, k * META:(k + 1) * META], PS[half, 5, T1 - 2 * CH:T2 - 2 * CH]).then_inc(S["aa_ks"], 1)
                    dve.wait_ge(S["aa_bias"], h + 1)

                    def scores(t):
                        m = P if t < NT else META
                        dve.wait_ge(S["aa_s"], 9 * h + t + 1)
                        if t >= 2:
                            dve.wait_ge(S["aa_t"], 9 * h + t - 1)
                        seen(dve)
                        for k in range(2):
                            e = EA[t % 2][k]
                            low = small[0:m, 8 + 2 * (t % 2) + k:9 + 2 * (t % 2) + k]
                            part = small[0:m, 16 + k:17 + k]
                            bias = biasH[:, T1 - P - t * P:2 * T1 - P - t * P] if t < NT else zero[0:m, :].broadcast_to([m, T1])
                            dve.tensor_tensor_reduce(e[0:m, 0:T1], wide(2 * k, T1, m), bias, -1.0, BIG, ALU.add, ALU.min, part).then_inc(S["aa_part"], 1)
                            dve.wait_ge(S["aa_part"], 18 * h + 2 * t + k + 1)
                            seen(dve)
                            dve.tensor_tensor_reduce(e[0:m, T1:T2], bank(4, META, META * k, m), zero[0:m, :].broadcast_to([m, META]), -1.0, part,
                                                     ALU.add, ALU.min, low).then_inc(S["aa_max"], 1)

                    def combine(t):
                        m = P if t < NT else META
                        den = [small[0:m, 12 + 2 * (t % 2) + k:13 + 2 * (t % 2) + k] for k in range(2)]
                        r2, c2, r1 = small[0:m, 40 + t % 2:41 + t % 2], small[0:m, 42 + t % 2:43 + t % 2], small[0:m, 20 + t % 3:21 + t % 3]
                        dve.wait_ge(S["aa_e"], 18 * h + 2 * t + 2)
                        dve.reciprocal(r2, den[1]).then_inc(S["aa_sm"], 1)
                        dve.reciprocal(r1, den[0]).then_inc(S["aa_sm"], 1)
                        dve.wait_ge(S["aa_sm"], 27 * h + 3 * t + 2)
                        dve.tensor_scalar(c2, den[0], r2, lam_sm[0:m, 4:5], ALU.mult, ALU.mult).then_inc(S["aa_sm"], 1)
                        dve.wait_ge(S["aa_sm"], 27 * h + 3 * t + 3)
                        dve.scalar_tensor_tensor(EA[t % 2][0][0:m, :], EA[t % 2][1][0:m, :], c2, EA[t % 2][0][0:m, :], ALU.mult, ALU.add).then_inc(S["aa_c"], 1)

                    def result(t):
                        m = P if t < NT else META
                        dve.wait_ge(S["aa_o"], 9 * h + t + 1)
                        dve.tensor_scalar(o_tok[0:m, t, bass.ds(h * P, P)], bank(7, P, 0, m), small[0:m, 20 + t % 3:21 + t % 3], None, ALU.mult).then_inc(S["aa_y"], 1)

                    for t in range(NT + 1):
                        scores(t)
                        if t >= 2:
                            result(t - 2)
                        combine(t)
                    result(NT - 1)
                    result(NT)
                dve.wait_ge(S["as_sd"], 1)
                dve.reciprocal(ss2[:, :, :], rs2[:, :, :]).then_inc(S["as_r"], 1)
                dve.wait_ge(S["as_r"], 1)
                for t in range(NT + 1):
                    m = P if t < NT else META
                    o3 = o_tok[0:m, t, :].rearrange("p (h n) -> p h n", n=P)
                    dve.tensor_tensor(o3, o3, ss2[0:m, t, :].unsqueeze(2).broadcast_to([m, HEADS, P]), ALU.mult).then_inc(S["as_n"], 1)
                dve.wait_ge(S["rope_ld"], 32)
                for g in range(KV):
                    z0 = g * (GROUP + 1)
                    for n in range(GROUP + 1):
                        i = z0 + n
                        dst = q_grp[:, n - 1, :] if n else kTb[:, :]
                        dve.wait_ge(S["ob_raw"], i + 1)
                        if i:
                            dve.wait_ge(S["ob_q"], i)
                        if g and n == 0:
                            dve.wait_ge(S["bb_t"], g * GROUP * (NT + 1))
                        dve.tensor_tensor(sq[1][:, 0:T2], acc[:, 0:T2], cos[:, :], ALU.mult).then_inc(S["ob_m"], 1)
                        dve.wait_ge(S["ob_sd"], 2 * i + 2)
                        dve.reciprocal(rs[:, 0:T2], sd[:, 0:T2]).then_inc(S["ob_r"], 1)
                        dve.wait_ge(S["ob_sw"], i + 1)
                        for k in range(3):
                            w = min(CH, T2 - k * CH)
                            c = slice(k * CH, k * CH + w)
                            if i and k == 0:
                                dve.wait_ge(S["ob_m3"], i)
                            ins = dve.tensor_tensor(swapped[:, c], bank(3 * (n % 2) + k, w), sin[:, c], ALU.mult)
                            ins.then_inc(S["ob_m2"], 1)
                        dve.wait_ge(S["ob_m2"], 3 * i + 3)
                        dve.wait_ge(S["ob_m"], i + 1)
                        dve.tensor_tensor(swapped[:, :], swapped[:, :], sq[1][:, 0:T2], ALU.add).then_inc(S["ob_m3"], 1)
                        dve.wait_ge(S["ob_m3"], i + 1)
                        dve.wait_ge(S["ob_r"], i + 1)
                        dve.tensor_tensor(dst, swapped[:, :], rs[:, 0:T2], ALU.mult).then_inc(S["ob_q"], 1)
                    with dve.Fori(0, GROUP) as j:
                        def head(j):
                            return (g * GROUP + j) * 9

                        def scores(t):
                            m = P if t < NT else META
                            e = EB[t % 2]
                            part, low = small[0:m, 28 + t % 2:29 + t % 2], small[0:m, 24 + t % 2:25 + t % 2]
                            dve.wait_ge(S["bb_s"], head(j) + t + 1 + CREDIT)
                            if t >= 2:
                                dve.wait_ge(S["bb_t"], head(j) + t - 1)
                            seen(dve)
                            dve.tensor_tensor_reduce(e[0:m, 0:T1], wide(2 * (t % 2), T1, m), zero[0:m, :].broadcast_to([m, T1]), -1.0, BIG, ALU.add, ALU.min,
                                                     part).then_inc(S["bb_part"], 1)
                            dve.wait_ge(S["bb_part"], head(j) + t + 1)
                            seen(dve)
                            dve.tensor_tensor_reduce(e[0:m, T1:T2], bank(4, META, META * (t % 2), m), zero[0:m, :].broadcast_to([m, META]), -1.0, part,
                                                     ALU.add, ALU.min, low).then_inc(S["bb_max"], 1)

                        def divide(t):
                            m = P if t < NT else META
                            r = small[0:m, 30 + t % 2:31 + t % 2]
                            dve.wait_ge(S["bb_e"], head(j) + t + 1)
                            dve.reciprocal(r, small[0:m, 26 + t % 2:27 + t % 2]).then_inc(S["bb_rd"], 1)
                            dve.wait_ge(S["bb_rd"], head(j) + t + 1)
                            dve.tensor_scalar(EB[t % 2][0:m, :], EB[t % 2][0:m, :], r, None, ALU.mult).then_inc(S["bb_p"], 1)

                        def result(t):
                            m = P if t < NT else META
                            dve.wait_ge(S["bb_o"], head(j) + t + 1)
                            dve.tensor_copy(obT[:, bass.ds(g * GROUP + j, 1), t * P:t * P + m].rearrange("p a n -> p (a n)"), bank(7, m)).then_inc(S["bb_ob"], 1)

                        for t in range(NT + 1):
                            scores(t)
                            if t >= 2:
                                result(t - 2)
                            divide(t)
                        result(NT - 1)
                        result(NT)
                dve.memset(oaT[:, :, T2:TP], 0.0).then_inc(S["pad_set"], 1)
                dve.memset(obT[:, :, T2:TP], 0.0).then_inc(S["pad_set"], 1)
                with dve.Fori(0, KD) as d:
                    m = mergedT[:, bass.ds(d, 1), :].rearrange("p a (n w) -> p (a n) w", w=CH)
                    dve.wait_ge(S["mg_sa"], d + 1)
                    dve.wait_ge(S["mg_ya"], d + 1)
                    dve.tensor_tensor(m, thirds(sq[0][:, :]), banks(3, 3, CH), ALU.mult).then_inc(S["mg_ma"], 1)
                    dve.wait_ge(S["mg_sb"], d + 1)
                    dve.wait_ge(S["mg_yb"], d + 1)
                    dve.tensor_tensor(thirds(acc[:, :]), thirds(sq[1][:, :]), banks(3, 3, CH), ALU.mult).then_inc(S["mg_mb"], 1)
                    dve.wait_ge(S["mg_mb"], d + 1 + CREDIT)
                    dve.wait_ge(S["mg_ma"], d + 1 + CREDIT)
                    dve.tensor_tensor(m, m, thirds(acc[:, :]), ALU.add).then_inc(S["mg_tmp"], 1)
                dve.wait_ge(S["keep_ld"], 16)
                with dve.Fori(0, KD // 2) as i:
                    for j in range(2):
                        dve.wait_ge(S["w2_z"], 2 * i + j + 1)
                        residual(dve, 2 * i + j, 3 * j, 3, CH, "w2_x", None)
                dve.wait_ge(S["w2_x"], KD + 2 * CREDIT)
                norm_apply(dve, 3, TP, xT, uT)
                dve.memset(aff[:, :, :], 0.0).then_inc(S["lg_set"], 1)
                dve.wait_ge(S["lg_set"], 1)
                dve.wait_ge(S["lg_z"], 1)
                dve.tensor_copy(aff[:, 0:NT, :], bank(0, NT * NE).rearrange("p (t n) -> p t n", n=NE)).then_inc(S["lg_c"], 1)
                dve.tensor_copy(aff[0:META, NT, :], bank(0, NE, NT * NE, META)).then_inc(S["lg_c"], 1)
                dve.wait_ge(S["lg_c"], 2)
                row_max, row_sum = small[:, 32:32 + NT + 1], small[:, 48:48 + NT + 1]
                dve.tensor_reduce(row_max, aff[:, :, :], AX, ALU.max).then_inc(S["lg_max"], 1)
                dve.wait_ge(S["lg_max"], 1)
                dve.tensor_tensor(aff[:, :, :], aff[:, :, :], row_max.unsqueeze(2).broadcast_to([P, NT + 1, NE]), ALU.subtract).then_inc(S["lg_sub"], 1)
                dve.wait_ge(S["lg_e"], 1)
                dve.tensor_reduce(row_sum, aff[:, :, :], AX, ALU.add).then_inc(S["lg_sum"], 1)
                dve.wait_ge(S["lg_sum"], 1)
                dve.reciprocal(row_max, row_sum).then_inc(S["lg_r"], 1)
                dve.wait_ge(S["lg_r"], 1)
                dve.tensor_tensor(aff[:, :, :], aff[:, :, :], row_max.unsqueeze(2).broadcast_to([P, NT + 1, NE]), ALU.mult).then_inc(S["lg_aff"], 1)
                for n in range(2):
                    dve.wait_ge(S["lg_t"], n + 1)
                    dve.tensor_copy(affT[:, META + n * BANK:META + (n + 1) * BANK], bank(n, BANK, 0, NE)).then_inc(S["lg_tc"], 1)
                dve.wait_ge(S["lg_t"], 3)
                dve.tensor_copy(affT[:, 0:META], bank(4, META, 0, NE)).then_inc(S["lg_tc"], 1)
                dve.wait_ge(S["lg_tc"], 3)
                for r in range(ROUNDS):
                    e8 = slice(8 * r, 8 * r + 8)
                    dve.max(best[:, e8], affT[:, :]).then_inc(S["tk_max"], 1)
                    dve.wait_ge(S["tk_max"], r + 1)
                    dve.max_index(where[:, e8], best[:, e8], affT[:, :]).then_inc(S["tk_idx"], 1)
                    if r < ROUNDS - 1:
                        dve.wait_ge(S["tk_idx"], r + 1)
                        dve.match_replace(affT[:, :], best[:, e8], affT[:, :], -1.0).then_inc(S["tk_rep"], 1)
                        dve.wait_ge(S["tk_rep"], r + 1)
                dve.wait_ge(S["tk_idx"], ROUNDS)
                dve.tensor_copy(where_f[:, :], where[:, :]).then_inc(S["tk_f"], 1)
                dve.wait_ge(S["tk_t"], 1)
                for r, rows in enumerate((P, REST)):
                    dve.tensor_copy(pick[r][:, :], bank(0, NE, 2 * r * NE, rows)).then_inc(S["tk_c"], 1)
                    dve.tensor_copy(weight[r][:, :], bank(0, NE, (2 * r + 1) * NE, rows)).then_inc(S["tk_c"], 1)
                dve.wait_ge(S["tk_c"], 4)
                with dve.Fori(0, NE) as e:
                    for n, (c, k) in enumerate(((0, 3), (3, 3), (6, 2))):
                        dve.wait_ge(S["ex_xt"], e * 3 + n + 1)
                        dve.tensor_copy(xsT[:, c:c + k, :], bank(n, k * CAP).rearrange("p (c n) -> p c n", n=CAP)).then_inc(S["ex_xc"], 1)
                    for j in range(EK):
                        dve.wait_ge(S["ex_s"], e * EK + j + 1)
                        dve.wait_ge(S["ex_u"], e * EK + j + 1)
                        dve.tensor_tensor(hidT[:, j, :], silu_e[j % 2][:, :], bank(4 + 2 * (j % 2), CAP), ALU.mult).then_inc(S["ex_h"], 1)
                    for n, (b, c, k) in enumerate(((7, 0, 3), (0, 3, 3), (1, 6, 2))):
                        dve.wait_ge(S["ex_y"], e * 3 + n + 1)
                        dve.tensor_copy(yT[:, c:c + k, :], bank(b, k * CAP).rearrange("p (c n) -> p c n", n=CAP)).then_inc(S["ex_yt"], 1)
                    dve.wait_ge(S["ex_free"], e + CREDIT)
                    for n in range(2):
                        dve.wait_ge(S["ex_r"], e * 2 + n + 1)
                        dve.tensor_scalar(y_row[0][:, n * BANK:(n + 1) * BANK], bank(3 + n), weight[0][:, bass.ds(e, 1)], None, ALU.mult).then_inc(S["ex_ra"], 1)
                dve.wait_ge(S["gfin_ld"], 16)
                for t in range(NT):
                    dve.wait_ge(S["fin_sd"], t + 1)
                    dve.reciprocal(fin_s[:, 2, t:t + 1], fin_s[:, 1, t:t + 1]).then_inc(S["fin_r"], 1)
                    dve.wait_ge(S["fin_r"], t + 1)
                    dve.scalar_tensor_tensor(fin[t][:, :], fin[t][:, :], fin_s[:, 2, t:t + 1], g_fin[:, :], ALU.mult, ALU.mult).then_inc(S["fin_o"], 1)

            @block.tensor
            def _(pe):
                pe.sem_inc(S["bb_s"], CREDIT)
                pe.wait_ge(N["h"], 3 * KD)
                before = [DC // P + KD // 2 + KD // 2, DC // P + KD // 2, DC // P + NF // 2]
                with pe.Fori(0, HEADS) as h:
                    pe.wait_ge(ring_ld[0], 16 * h + 16 * before[0] + 16)
                    project(ring[0], uT, 0, 3, CH).then_inc(S["aa_q"], 1)
                    pe.wait_ge(ring_ld[1], 16 * h + 16 * before[1] + 16)
                    project(ring[1], uT, 3, 3, CH).then_inc(S["aa_k"], 1)
                    pe.wait_ge(ring_ld[2], 16 * h + 16 * before[2] + 16)
                    for n in range(3):
                        if n == 1:
                            pe.wait_ge(S["aa_y"], 9 * h + CREDIT)
                        if n == 2:
                            pe.wait_ge(S["aa_qs"], h + 1)
                        for t in range(4 * n, min(4 * n + 4, NT + 1)):
                            m = P if t < NT else META
                            for c in range(KD):
                                last = mm(bank(6 + n if n < 2 else 0, P, (t % 4) * P, m), uT[:, c, t * P:t * P + m], ring[2][:, c, :],
                                          start=(c == 0), stop=(c == KD - 1))
                        last.then_inc(S["aa_v"], 1)

                    def scores(t):
                        m = P if t < NT else META
                        if t == 0:
                            pe.wait_ge(S["aa_ks"], 3 * h + 3)
                            pe.wait_ge(S["aa_vs"], 3 * h + 3)
                        else:
                            pe.wait_ge(S["aa_max"], 18 * h + 2 * t + CREDIT)
                        if m < P:
                            seen(pe)
                        for k0 in (0, BANK):
                            for a in range(2):
                                r = slice(a * HD, (a + 1) * HD)
                                mm(bank(2 * a + k0 // BANK, BANK, 0, m), qTa[r, t * P:t * P + m], kTa[r, k0:k0 + BANK], start=True, stop=True)
                        last = mm(bank(4, 2 * META, 0, m), qTa[:, t * P:t * P + m], kmeta[:, :], start=True, stop=True)
                        last.then_inc(S["aa_s"], 1)

                    def turn_probs(t):
                        m = P if t < NT else META
                        e = EA[t % 2][0]
                        pe.wait_ge(S["aa_c"], 9 * h + t + 1)
                        if m < P:
                            seen(pe)
                        for j in range(NT):
                            turn(bank(5 + j // 4, m, (j % 4) * P), e[0:m, j * P:(j + 1) * P], m)
                        if t >= 1:
                            pe.wait_ge(S["aa_y"], 9 * h + t + CREDIT)
                            if m < P:
                                seen(pe)
                        turn(bank(7, m, 256, META), e[0:m, T1:T2], m).then_inc(S["aa_t"], 1)

                    def values(t):
                        m = P if t < NT else META
                        pe.wait_ge(S["aa_pt"], 9 * h + t + 1)
                        pe.wait_ge(S["aa_pt9"], 9 * h + t + 1)
                        for j in range(NT):
                            mm(bank(7, P, 0, m), PTa[t % 2][:, j, 0:m], Va[:, j, :], start=(j == 0), stop=False)
                        mm(bank(7, P, 0, m), PTa[t % 2][0:META, NT, 0:m], Va[0:META, NT, :], start=False, stop=True).then_inc(S["aa_o"], 1)

                    scores(0)
                    for t in range(NT + 1):
                        if t < NT:
                            scores(t + 1)
                        if t >= 1:
                            values(t - 1)
                        turn_probs(t)
                    values(NT)
                for t in range(NT + 1):
                    m = P if t < NT else META
                    pe.wait_ge(S["as_n"], t + 1)
                    for half in range(2):
                        if t >= 2:
                            pe.wait_ge(S["as_o"], 2 * (t - 2) + half + 1)
                        for c in range(4):
                            last = turn(bank(4 * (t % 2) + half, m, c * P), o_tok[0:m, t, (4 * half + c) * P:(4 * half + c + 1) * P], m)
                        last.then_inc(S["as_t"], 1)
                before = [DC // P + NF // 2 + KD // 2, DC // P + NF // 2, DC // P + NF // 2]
                pe.wait_ge(S["as_o"], 2 * (NT + 1))
                for g in range(KV):
                    z0 = g * (GROUP + 1)
                    pe.wait_ge(ring_ld[3], 16 * (before[0] + g + 1))
                    if g:
                        pe.wait_ge(S["bb_ob"], g * GROUP * (NT + 1))
                    for n in range(3):
                        for t in range(4 * n, min(4 * n + 4, NT + 1)):
                            m = P if t < NT else META
                            for c in range(KD):
                                last = mm(bank(6 + n if n < 2 else 5, P, (t % 4) * P, m), uT[:, c, t * P:t * P + m], ring[3][:, c, :],
                                          start=(c == 0), stop=(c == KD - 1))
                        last.then_inc(S["ob_v"], 1)

                    def normed(n):
                        i = z0 + n
                        first = 3 * (n % 2)
                        pe.wait_ge(S["ob_sq"], i + 1)
                        if n == 0:
                            pe.wait_ge(S["ob_vs"], 3 * g + 3)
                        else:
                            pe.wait_ge(S["ob_sd"], 2 * i)
                        for b in range(2):
                            mm(bank(6 + b), ones[:, :], sq[0][:, b * BANK:(b + 1) * BANK], start=True, stop=True)
                        mm(bank(first + 2, META, 384), ones[:, :], sq[0][:, T1:T2], start=True, stop=True).then_inc(S["ob_ss"], 1)
                        pe.wait_ge(S["ob_raw"], i + 1)
                        pe.wait_ge(S["ob_sd"], 2 * i + 2)
                        for b in range(3):
                            last = mm(bank(first + b, CH), swap[:, :], acc[:, b * CH:(b + 1) * CH], start=True, stop=True)
                        last.then_inc(S["ob_sw"], 1)

                    for n in range(GROUP + 1):
                        i = z0 + n
                        if n == 0:
                            pe.wait_ge(ring_ld[4], 16 * (before[1] + g + 1))
                        else:
                            pe.wait_ge(ring_ld[5], 16 * (before[2] + g * GROUP + n))
                        if n == 1:
                            pe.wait_ge(S["ob_vs"], 3 * g + 3)
                        if n >= 2:
                            pe.wait_ge(S["ob_m2"], 3 * (i - 1))
                        project(ring[5 if n else 4], uT, 3 * (n % 2), 3, CH).then_inc(S["ob_z"], 1)
                        if n:
                            normed(n - 1)
                    normed(GROUP)
                    with pe.Fori(0, GROUP) as j:
                        def head(j):
                            return (g * GROUP + j) * 9

                        def scores(t):
                            m = P if t < NT else META
                            if t == 0:
                                pe.wait_ge(S["bb_qs"], g * GROUP + j + 1)
                                pe.wait_ge(S["ob_q"], z0 + GROUP + 1)
                            if t >= 2:
                                pe.wait_ge(S["bb_max"], head(j) + t - 1)
                            for k0 in (0, BANK):
                                mm(bank(2 * (t % 2) + k0 // BANK, BANK, 0, m), qs[:, t * P:t * P + m], kTb[:, k0:k0 + BANK], start=True, stop=True)
                            if t >= 1:
                                pe.wait_ge(S["bb_max"], head(j) + t)
                            mm(bank(4, META, META * (t % 2), m), qs[:, t * P:t * P + m], kTb[:, T1:T2], start=True, stop=True).then_inc(S["bb_s"], 1)

                        def turn_probs(t):
                            m = P if t < NT else META
                            pe.wait_ge(S["bb_p"], head(j) + t + 1)
                            if m < P:
                                seen(pe)
                            for i in range(NT):
                                turn(bank(5 + i // 4, m, (i % 4) * P), EB[t % 2][0:m, i * P:(i + 1) * P], m)
                            if t >= 1:
                                pe.wait_ge(S["bb_ob"], head(j) + t)
                                if m < P:
                                    seen(pe)
                            turn(bank(7, m, 256, META), EB[t % 2][0:m, T1:T2], m).then_inc(S["bb_t"], 1)

                        def values(t):
                            m = P if t < NT else META
                            pe.wait_ge(S["bb_pt"], head(j) + t + 1)
                            pe.wait_ge(S["bb_pt9"], head(j) + t + 1)
                            for i in range(NT):
                                mm(bank(7, m), Vb[:, i, :], PTb[t % 2][:, i, 0:m], start=(i == 0), stop=False)
                            mm(bank(7, m), Vb[0:META, NT, :], PTb[t % 2][0:META, NT, 0:m], start=False, stop=True).then_inc(S["bb_o"], 1)

                        scores(0)
                        for t in range(NT + 1):
                            if t < NT:
                                scores(t + 1)
                            if t >= 1:
                                values(t - 1)
                            turn_probs(t)
                        values(NT)
                before = [DC // P + KD + HEADS, DC // P + KD // 2 + HEADS, DC // P + NF // 2 + HEADS, DC // P + NF // 2 + KD // 2 + KV]
                pe.wait_ge(S["bb_ob"], HEADS * (NT + 1))
                pe.wait_ge(S["pad_set"], 3)
                with pe.Fori(0, KD) as d:
                    for k, (src, z, first, free) in enumerate(((uT, "mg_ga", 0, None), (oaT, "mg_ya", 3, "mg_mb"), (uT, "mg_gb", 0, "mg_sa"), (obT, "mg_yb", 3, "mg_ma"))):
                        pe.wait_ge(ring_ld[k], 16 * d + 16 * before[k] + 16)
                        if k == 0:
                            pe.wait_ge(S["mg_mb"], d + CREDIT)
                        elif k == 1:
                            pe.wait_ge(S["mg_mb"], d + CREDIT)
                        elif k == 2:
                            pe.wait_ge(S["mg_sa"], d + 1)
                        else:
                            pe.wait_ge(S["mg_ma"], d + 1 + CREDIT)
                        project(ring[k], src, first, 3, CH).then_inc(S[z], 1)
                before = [DC // P + NF // 2 + KV, DC // P + NF // 2 + KV * GROUP]
                pe.wait_ge(S["mg_tmp"], KD)
                with pe.Fori(0, KD // 2) as i:
                    for j in range(2):
                        pe.wait_ge(ring_ld[4 + j], 16 * i + 16 * before[j] + 16)
                        pe.wait_ge(S["w2_x"], 2 * i + j - 1 + 2 * CREDIT)
                        project(ring[4 + j], mergedT, 3 * j, 3, CH).then_inc(S["w2_z"], 1)
                norm_sum(pe, 3, 3, CH)
                pe.wait_ge(S["router_ld"], 16)
                pe.wait_ge(N["h"], 4 * KD)
                for t in range(NT + 1):
                    m = P if t < NT else META
                    for c in range(KD):
                        last = mm(bank(0, NE, t * NE, m), uT[:, c, t * P:t * P + m], router[:, c, :], start=(c == 0), stop=(c == KD - 1))
                last.then_inc(S["lg_z"], 1)

                def rows(t):
                    m = P if t < NT else META
                    for src, first, done, free in ((xT, 6, "hr_t", "hr_c"), (uT, 2, "ur_t", "ur_c")):
                        for n in range(2):
                            if t:
                                pe.wait_ge(S[free], 2 * (t - 1) + n + 1)
                            for c in range(4):
                                last = turn(bank(first + n, P, c * P, m), src[:, 4 * n + c, t * P:t * P + m])
                            last.then_inc(S[done], 1)

                for t in range(3):
                    rows(t)
                pe.wait_ge(S["lg_aff"], 1)
                for t in range(NT + 1):
                    m = P if t < NT else META
                    last = turn(bank(t // 4 if t < NT else 4, m, (t % 4) * P, NE), aff[0:m, t, :], m)
                    if t in (3, 7, 8):
                        last.then_inc(S["lg_t"], 1)
                for t in range(3, NT + 1):
                    rows(t)
                pe.wait_ge(S["tk_f"], 1)
                for r, (c, n) in enumerate(((0, P), (P, REST))):
                    for k, src in enumerate((where_f, best)):
                        last = turn(bank(0, NE, (2 * r + k) * NE, n), src[:, c:c + n], NE)
                last.then_inc(S["tk_t"], 1)
                pe.wait_ge(S["tk_c"], 4)
                pe.wait_ge(S["ur_c"], 2 * (NT + 1))
                pe.wait_ge(S["hr_c"], 2 * (NT + 1))
                with pe.Fori(0, NE) as e:
                    pe.wait_ge(S["ex_xa"], 16 * e + 16)
                    pe.wait_ge(S["ex_xb"], 16 * e + 16)
                    for c in range(KD):
                        turn(bank(c // 3, P, (c % 3) * CAP), xs[0][:, c * P:(c + 1) * P])
                        last = turn(bank(c // 3, REST, (c % 3) * CAP + P), xs[1][:, c * P:(c + 1) * P], REST)
                        if c in (2, 5, 7):
                            last.then_inc(S["ex_xt"], 1)
                    pe.wait_ge(S["ex_xc"], e * 3 + 3)
                    for j in range(EK):
                        if j == 0:
                            pe.wait_ge(S["ex_ra"], e * 2 + CREDIT)
                            pe.wait_ge(S["ex_rb"], e * 2 + CREDIT)
                        if j >= 2:
                            pe.wait_ge(S["ex_h"], e * EK + j - 1 + 2 * CREDIT)
                        for w, b, ld, done in ((w_gate, 3, gate_ld, "ex_g"), (w_up, 4, up_ld, "ex_u")):
                            pe.wait_ge(ld[j], 16 * e + 16)
                            for c in range(KD):
                                last = mm(bank(b + 2 * (j % 2), CAP), w[:, j, c, :], xsT[:, c, :], start=(c == 0), stop=(c == KD - 1))
                            last.then_inc(S[done], 1)
                    pe.wait_ge(S["ex_h"], e * EK + EK + 2 * CREDIT)
                    pe.wait_ge(down_ld, EK * 16 * e + EK * 16)
                    for c in range(KD):
                        b = (7, 0, 1)[c // 3]
                        for j in range(EK):
                            last = mm(bank(b, CAP, (c % 3) * CAP), w_down[:, j, c * P:(c + 1) * P], hidT[:, j, :], start=(j == 0), stop=(j == EK - 1))
                        if c in (2, 5, 7):
                            last.then_inc(S["ex_y"], 1)
                    for n in range(2):
                        pe.wait_ge(S["ex_yt"], e * 3 + 2 + n)
                        for c in range(4):
                            turn(bank(3 + n, P, c * P), yT[:, 4 * n + c, 0:P])
                            last = turn(bank(5 + n, P, c * P, REST), yT[:, 4 * n + c, P:CAP])
                        last.then_inc(S["ex_r"], 1)



def layout(inputs):
    a = {n: np.asarray(v) for n, v in inputs.items()}

    def by_column_tile(w):
        lead, k, n = w.shape[:-2], w.shape[-2], w.shape[-1]
        w = w.reshape(*lead, k // P, P, n // P, P)
        r = len(lead)
        return w.transpose(*range(r), r + 2, r + 1, r, r + 3)

    def by_feature(g):
        return g.reshape(-1, P).T

    vectors = [by_feature(a[n][0]) for n in ("g_mix", "g_ffn", "g_mix_2", "g_ffn_2")]
    vectors += [by_feature(a["conv_w"][0, k]) for k in range(3)]
    vectors += [by_feature(a["g_conv_out"][0]), by_feature(a["g_attn_out"][0])]
    vectors += [np.tile(a[n][0], 2)[:, None] for n in ("g_q", "g_k")]
    vectors += [a[n][0][:, None] for n in ("g_subln_2", "g_qnorm_2", "g_knorm_2")]
    out = {"vectors": np.concatenate(vectors, 1)}
    for n in ("w_in", "w_out", "w_gate", "w_up", "w_down", "w_in_2", "w_branch_a_2", "w_branch_b_2", "w_out_2", "w_gate_2", "w_up_2"):
        out[n] = by_column_tile(a[n][0])
    for n in ("x", "meta_tokens_2", "lambda_q1_2", "lambda_k1_2", "lambda_q2_2", "lambda_k2_2", "w_router_2", "w_down_2", "g_final_2"):
        out[n] = a[n]
    return {n: np.ascontiguousarray(v) for n, v in (out | host_constants()).items()}


def kernel(**inputs):
    import concourse.bacc as bacc
    from concourse.bass_utils import run_bass_kernel_spmd as run

    nc = bacc.Bacc("TRN2", target_bir_lowering=False, num_devices=1)
    arrays, aps = {}, {}
    for name, a in layout(inputs).items():
        arrays[f"in_{name}"] = a
        aps[name] = nc.dram_tensor(f"in_{name}", a.shape, mybir.dt.from_np(a.dtype), kind="ExternalInput").ap()
    out = nc.dram_tensor("out", (1, T1, D), F32, kind="ExternalOutput").ap()
    build(nc, aps, out)
    r = run(nc, [arrays], core_ids=[0])
    return r.results[0]["out"]
```

```python
from contextlib import ExitStack

import concourse.bass as bass
import numpy as np
from concourse import mybir

F32 = mybir.dt.float32
F32R = mybir.dt.float32r
U32 = mybir.dt.uint32
ALU = mybir.AluOpType
ACT = mybir.ActivationFunctionType
AX = mybir.AxisListType.X

P = 128
D = 1024
KD = D // P
T1 = 1024
META = 16
T2 = T1 + META
CH = 348
TP = 3 * CH
NT = T1 // P
BANK = 512
EPS = 1e-6

DC = 512
DCT = DC // P
HD = 64
FF = 2816
NF = FF // P
HALF = KD // 2
W_OUT0 = 6 * DCT
UP0 = W_OUT0 + KD
DOWN0 = UP0 + 2 * NF
TILES = DOWN0 + NF
QA, KA, VA, QB, KB, VB, GA, GB = 0, 8, 16, 24, 32, 34, 36, 44
HEADS = 8
KV = 2
GROUP = HEADS // KV
HB = 128
NE = 16
EF = 512
EK = EF // P
CAP = 2 * T2 // NE
REST = CAP - P
ROUNDS = -(-CAP // 8)
LAM_INIT = 0.8 - 0.6 * float(np.exp(-0.3 * 0))
BIG = 3.0e38
MASKED = -1.0e30
CREDIT = 1

NORM_GAINS = [n * KD for n in range(4)]
CONV_W = 4 * KD
G_CONV = CONV_W + 3 * DCT
G_ATTN = G_CONV + DCT
G_Q, G_K, G_SUB, G_QN, G_KN = range(G_ATTN + DCT, G_ATTN + DCT + 5)
GAINS = G_KN + 1


def host_constants():
    eye = np.eye(P, dtype=np.float32)
    ones = np.ones((P, P), np.float32)
    block = np.kron(np.eye(2), np.ones((HD, HD))).astype(np.float32)
    swap = np.zeros((P, P), np.float32)
    for half in (0, 64):
        for i in range(32):
            swap[half + 32 + i, half + i] = -1.0
            swap[half + i, half + 32 + i] = 1.0
    delta = np.arange(P)[:, None] - (np.arange(T1)[None, :] - (T1 - P))
    count = np.zeros(delta.shape, np.float32)
    for window, dil in ((128, 1), (512, 4), (2048, 16)):
        count += (delta >= 0) & (delta % dil == 0) & (delta <= window)
    log_count = np.where(count > 0, np.log(np.maximum(count, 1)), MASKED).astype(np.float32)
    neg_dist = -np.abs(np.arange(P)[:, None] - (np.arange(2 * T1 - P)[None, :] - (T1 - P))).astype(np.float32)
    half = HB // 2
    inv = (np.float32(10000.0) ** (-np.arange(0, half, 2, dtype=np.float32) / np.float32(half))).astype(np.float32)
    tok = np.arange(T1)
    row = np.concatenate([tok // 64, np.zeros(META, int)]).astype(np.float32)
    col = np.concatenate([tok % 64, np.zeros(META, int)]).astype(np.float32)
    ang_r, ang_c = inv[:, None] * row[None], inv[:, None] * col[None]
    ang = np.concatenate([ang_r, ang_r, ang_c, ang_c], 0)
    cos = np.cos(ang).astype(np.float32)
    sin = np.sin(ang).astype(np.float32)
    return {"eye": eye, "ones": ones, "block": block, "swap": swap, "log_count": log_count, "neg_dist": neg_dist,
            "cos": cos, "sin": sin}


def build(nc, A, out):
    ctx = ExitStack()
    with ctx:
        base = [-(-nc.sbuf_base // 64) * 64]

        def at(name, shape, offset, dt=F32):
            return nc.alloc_sbuf_tensor_at(name, shape, dt, offset=offset)

        def size(shape):
            return 4 * int(np.prod(shape[1:]))

        def put(name, shape, dt=F32):
            t = at(name, shape, base[0], dt)
            base[0] += -(-size(shape) // 32) * 32
            return t

        class Overlay:

            def __init__(self, start, end):
                self.at, self.end = start, end

            def put(self, name, shape, dt=F32):
                t = at(name, shape, self.at, dt)
                self.at += -(-size(shape) // 32) * 32
                assert self.at <= self.end, (name, self.at, self.end)
                return t

        def sem(name):
            return ctx.enter_context(nc.semaphore(name))

        eye = put("eye_sb", [P, P])
        ones = put("ones_sb", [P, P])
        block64 = put("block_sb", [P, P])
        swap = put("swap_sb", [P, P])
        gains = put("gains_sb", [P, GAINS])
        g_heads = put("g_heads_sb", [P, 3])
        G_Q8, G_SUBI, G_QNS = range(3)
        lams = put("lams_sb", [P, 4, HD])
        lam_sm = put("lam_small", [P, 8])
        eps = put("eps_sb", [P, 1])
        zero = put("zero_sb", [P, 1])
        small = put("small_sb", [P, 64])
        ring0 = base[0]
        ring = [put(f"ring{j}", [P, KD, P]) for j in range(6)]
        w_raw = ring[0:2]
        w_hi = [at(f"w_hi{j}", [P, KD, P], ring0 + (2 + j) * 4096, F32R) for j in range(2)]
        w_lo = [at(f"w_lo{j}", [P, KD, P], ring0 + (4 + j) * 4096, F32R) for j in range(2)]
        uT_at = base[0]
        uT = put("uT", [P, KD, TP])
        norm0 = base[0]
        sq = [put(f"sq{j}", [P, TP]) for j in range(2)]
        acc = put("acc", [P, TP])
        sd = put("sd", [P, TP])
        rs = put("rs", [P, TP])
        xT_at = base[0]
        xT = put("xT", [P, KD, TP])
        scratch = base[0]
        top = nc.sbuf_usable_end
        yT_at = (top - 4 * KD * TP) // 32 * 32

        u_hi = at("u_hi", [P, KD, T1], uT_at, F32R)
        u_lo = at("u_lo", [P, KD, T1], yT_at, F32R)
        o = Overlay(scratch, yT_at)
        x_in = o.put("x_in", [P, NT, D])
        meta_in = o.put("meta_in", [META, D])
        o = Overlay(xT_at, yT_at)
        qT1 = o.put("qT1", [P, T1])
        kT1 = o.put("kT1", [P, T1])
        V1 = o.put("V1", [P, NT, P])
        E1 = [o.put(f"E1_{j}", [P, T1]) for j in range(4)]
        PT1 = [o.put(f"PT1_{j}", [P, 4, P]) for j in range(4)]
        convT = o.put("convT", [P, DCT, T1])
        y_tok = o.put("y_tok", [P, NT, DC])
        u_sb = o.put("u_sb", [P, T1])
        gated = o.put("gated", [P, 2 + T1])
        conv_acc = o.put("conv_acc", [P, T1])
        conv_sq = o.put("conv_sq", [P, T1])
        ss1 = o.put("ss1", [P, 2 * NT])
        bias1 = o.put("bias1", [P, T1])
        vT1 = u_sb
        tmp = [at(f"tmp{j}", [P, T1], scratch + j * 4096) for j in range(2)]
        hid = at("hid", [P, NF, T1], xT_at)
        assert xT_at + 4 * NF * T1 <= yT_at
        hid_hi = [at(f"hid_hi{j}", [P, T1], uT_at + j * 8192, F32R) for j in range(4)]
        hid_lo = [at(f"hid_lo{j}", [P, T1], uT_at + j * 8192 + 4096, F32R) for j in range(4)]
        silu1 = sq
        x2T = at("x2T", [P, KD, TP], yT_at)

        oaT = at("oaT", [P, HEADS, TP], xT_at)
        o = Overlay(scratch, top)
        o_tok = o.put("o_tok", [P, NT + 1, D])
        biasH = o.put("biasH", [P, 2 * T1 - P])
        kmeta = o.put("kmeta", [P, 2 * META])
        qTa = o.put("qTa", [P, TP])
        kTa = o.put("kTa", [P, TP])
        q_parts = [o.put(f"q_parts{k}", [P, TP], F32R) for k in range(2)]
        Va = o.put("Va", [P, NT + 1, P])
        EA = [[o.put(f"EA{j}{m}", [P, T2]) for m in range(2)] for j in range(2)]
        PTa = [o.put(f"PTa{j}", [P, NT + 1, P]) for j in range(2)]
        ss2 = at("ss2", [P, NT + 1, HEADS], norm0)
        junk = at("junk", [P, P], norm0 + 512)
        rs2 = at("rs2", [P, NT + 1, HEADS], norm0 + 1024 + 512)
        o = Overlay(norm0 + 2048, xT_at)
        k_lead = [o.put(f"k_lead{k}", [P, TP], F32R) for k in range(2)]
        k_rest = [o.put(f"k_rest{k}", [P, TP], F32R) for k in range(2)]
        meta_a = o.put("meta_a", [P, NT + 1, 2, META])
        low_a = o.put("low_a", [P, NT + 1, 2])
        o = Overlay(scratch, top)
        obT = o.put("obT", [P, HEADS, TP])
        ob_end = o.at
        q_grp = o.put("q_grp", [P, GROUP, T2])
        swapped = o.put("swapped", [P, T2])
        cos = o.put("cos_sb", [P, T2])
        sin = o.put("sin_sb", [P, T2])
        kTb = o.put("kTb", [P, T2])
        Vb = o.put("Vb", [P, NT + 1, HB])
        qs = o.put("qs", [P, T2])
        meta_b = o.put("meta_b", [P, NT + 1, META])
        low_b = o.put("low_b", [P, NT + 1])
        EB = [o.put(f"EB{j}", [P, T2]) for j in range(2)]
        PTb = [o.put(f"PTb{j}", [P, NT + 1, P]) for j in range(2)]
        o = Overlay(ob_end, top)
        mergedT = o.put("mergedT", [P, KD, TP])
        h_row = [at(f"h_row{j}", [P, D], ring0 + j * 4096) for j in range(2)]
        u_row = [at(f"u_row{j}", [P, D], ring0 + 8192 + j * 4096) for j in range(2)]
        o = Overlay(scratch, top)
        w_gate = o.put("w_gate_sb", [P, EK, KD, P])
        w_up = o.put("w_up_sb", [P, EK, KD, P])
        w_down = o.put("w_down_sb", [P, EK, D])
        xs = [o.put("xs_a", [P, D]), o.put("xs_b", [REST, D])]
        xsT = o.put("xsT", [P, KD, CAP])
        hidT = o.put("hidT", [P, EK, CAP])
        silu_e = [o.put(f"silu_e{j}", [P, CAP]) for j in range(2)]
        yT = o.put("yT", [P, KD, CAP])
        y_row = [o.put("y_row_a", [P, D]), o.put("y_row_b", [REST, D])]
        router = o.put("router_sb", [P, KD, NE])
        aff = o.put("aff", [P, NT + 1, NE])
        affT = o.put("affT", [NE, T2])
        best = o.put("best", [NE, 8 * ROUNDS])
        where = o.put("where", [NE, 8 * ROUNDS], U32)
        where_f = o.put("where_f", [NE, 8 * ROUNDS])
        pick = [o.put("pick_a", [P, NE], U32), o.put("pick_b", [REST, NE], U32)]
        pick_g = [o.put("pick_g_a", [P, 1], U32), o.put("pick_g_b", [REST, 1], U32)]
        pick_s = [o.put("pick_s_a", [P, 1], U32), o.put("pick_s_b", [REST, 1], U32)]
        weight = [o.put("weight_a", [P, NE]), o.put("weight_b", [REST, NE])]
        fin = [at(f"fin{j}", [P, D], xT_at + j * 4096) for j in range(NT)]
        g_fin = at("g_fin", [P, D], uT_at)
        fin_sq = at("fin_sq", [P, D], uT_at + 4096)
        fin_s = at("fin_s", [P, 3, NT], uT_at + 8192)

        PS = ctx.enter_context(nc.psum_tensor("PS", [P, 8, BANK], F32))

        def bank(b, n=BANK, start=0, rows=P):
            return PS[0:rows, b, start:start + n]

        def banks(b, n, width):
            return PS[:, b:b + n, 0:width]

        def wide(b, n, rows=P):
            return PS[0:rows, :, :].rearrange("p b n -> p (b n)")[:, b * BANK:b * BANK + n]

        def thirds(t):
            return t.rearrange("p (n w) -> p n w", w=CH)

        x_keep = nc.dram_tensor("x_keep", (P, KD, TP), F32, kind="Internal").ap()
        h_rows = nc.dram_tensor("h_rows", (T2, D), F32, kind="Internal").ap()
        u_rows = nc.dram_tensor("u_rows", (T2, D), F32, kind="Internal").ap()

        def cols(w, tile):
            return w[bass.ds(tile, 1)].rearrange("a p c n -> p (a c) n")

        lasting = """seen eye_ld const_ld gain_ld lam_ld eps_set pad_set gain_set lam_dot lam_exp lam_done dist_ld keep_st keep_ld as_init""".split()
        first_block = """meta_ld bias_ld x_t x_act x_dve w_ld0 w_ld1 w_rounded w_split w_used n_hi n_lo
            conv_u conv_a conv_k conv_y mix_sq mix_acc cn_sum cn_sd cn_r cn_n cn_hi cn_lo
            a1_sq a1_ss a1_sd a1_r a1_qn a1_vf a1_vt a1_vs a1_s a1_max a1_e a1_t a1_pt_d a1_pt_a a1_o a1_y a1_rd
            a1_ysq a1_ysd a1_yr a1_yn a1_yt a1_hi a1_lo wo_x up_s up_h hid_hi hid_lo dn_z dn_x""".split()
        second_block = """aa_bias aa_q aa_k aa_v aa_qs aa_qh aa_ql aa_kh aa_ks aa_vs aa_s aa_mt aa_ms aa_max aa_e aa_sm aa_c aa_t aa_pt aa_pt9 aa_o aa_y aa_ssq as_sd
            as_r as_n as_t as_o ob_v ob_vs ob_z ob_raw ob_sq ob_ss ob_sd ob_r ob_sw ob_m ob_m2 ob_m3 ob_q rope_ld bb_qs bb_s bb_mt bb_ms
            bb_max bb_e bb_rd bb_p bb_t bb_pt bb_pt9 bb_o bb_ob mg_ga mg_ya mg_gb mg_yb mg_sa mg_sb mg_ma mg_mb mg_tmp w2_z w2_x
            router_ld lg_z router_step    lg_e    lg_t  hr_t hr_c ur_t ur_c tk_max tk_idx
            tk_rep tk_f tk_t tk_c ex_pick_g ex_pick_s ex_xa ex_xb ex_xt ex_xc ex_g ex_u ex_s ex_h ex_y ex_yt ex_r ex_ra ex_rb
            ex_add_a ex_add_b ex_free gfin_ld fin_q fin_sd fin_r fin_o fin_st""".split()
        S = {n: sem(n) for n in lasting}
        first_sems = {n: nc.alloc_semaphore(name=n) for n in first_block}
        S.update(first_sems)
        ring_ld = [sem(f"ring_ld{j}") for j in range(6)]
        xin_lds = [sem(f"xin_ld{j}") for j in range(NT)]
        N = {s: sem(f"norm_{s}") for s in ("sq", "acc", "ss", "sd", "r", "h")}

        def load(sp, j, src):
            sp.dma_start(ring[j][:, :, :], src).then_inc(ring_ld[j], 16)

        def norm_root(act, k, width, src, n_banks, w):
            for c in range(KD):
                if c >= 2:
                    act.wait_ge(N["acc"], k * KD + c - 1)
                act.activation(sq[c % 2][:, 0:width], src[:, c, 0:width], ACT.Square).then_inc(N["sq"], 1)
            act.wait_ge(N["ss"], k + 1)
            act.activation(sd[:, 0:width].rearrange("p (n w) -> p n w", w=w), banks(0, n_banks, w), ACT.Sqrt,
                           scale=1.0 / D, bias=eps[:, :]).then_inc(N["sd"], 1)

        def norm_total(dve, k, width):
            for c in range(KD):
                dve.wait_ge(N["sq"], k * KD + c + 1)
                if c == 0:
                    dve.tensor_copy(acc[:, 0:width], sq[0][:, 0:width]).then_inc(N["acc"], 1)
                else:
                    dve.wait_ge(N["acc"], k * KD + c)
                    dve.tensor_tensor(acc[:, 0:width], acc[:, 0:width], sq[c % 2][:, 0:width], ALU.add).then_inc(N["acc"], 1)
            dve.wait_ge(N["sd"], k + 1)
            dve.reciprocal(rs[:, 0:width], sd[:, 0:width]).then_inc(N["r"], 1)
            dve.wait_ge(N["r"], k + 1)

        def normed(dve, k, dst, src, c, width):
            return dve.scalar_tensor_tensor(dst, src[:, c, 0:width], gains[:, NORM_GAINS[k] + c:NORM_GAINS[k] + c + 1], rs[:, 0:width],
                                            ALU.mult, ALU.mult)

        def norm_apply(dve, k, width, src, dst):
            norm_total(dve, k, width)
            for c in range(KD):
                normed(dve, k, dst[:, c, 0:width], src, c, width).then_inc(N["h"], 1)

        def norm_split(dve, k, src):
            norm_total(dve, k, T1)
            for c in range(KD + 1):
                if c < KD:
                    if c >= 2:
                        dve.wait_ge(S["n_lo"], k * KD + c - 1)
                    normed(dve, k, tmp[c % 2][:, :], src, c, T1).then_inc(N["h"], 1)
                if c:
                    dve.wait_ge(S["n_hi"], k * KD + c)
                    dve.tensor_tensor(u_lo[:, c - 1, :], tmp[(c - 1) % 2][:, :], u_hi[:, c - 1, :], ALU.subtract).then_inc(S["n_lo"], 1)

        def norm_round(act, k):
            for c in range(KD):
                act.wait_ge(N["h"], k * KD + c + 1)
                act.activation(u_hi[:, c, :], tmp[c % 2][:, :], ACT.Copy).then_inc(S["n_hi"], 1)

        def seen(engine):
            engine.sem_inc(S["seen"], 1)

        mm = nc.tensor.matmul

        def turn(out, in_, k=P):
            return nc.tensor.transpose(out, in_, eye[0:k, 0:k])

        def project(w, src, first, n, width):
            for c in range(KD):
                for b in range(n):
                    last = mm(bank(first + b, width), w[:, c, :], src[:, c, b * width:(b + 1) * width], start=(c == 0), stop=(c == KD - 1))
            return last

        def project_split(pe, j, n, first, hi, lo, ready=None):
            pe.wait_ge(S["w_split"], n + 1)
            for c in range(KD):
                if ready is not None:
                    ready(c)
                for k, (w, src) in enumerate(((w_hi, hi), (w_hi, lo), (w_lo, hi))):
                    for b in range(2):
                        last = mm(bank(first + b), w[j][:, c, :], src[:, c, b * BANK:(b + 1) * BANK], start=(c == 0 and k == 0),
                                  stop=(c == KD - 1 and k == 2))
            return last

        def total(first, n, width, src):
            for b in range(n):
                last = mm(bank(first + b, width), ones[:, :], src[:, b * width:(b + 1) * width], start=True, stop=True)
            return last

        def norm_sum(pe, k, n, width):
            pe.wait_ge(N["acc"], (k + 1) * KD)
            total(0, n, width, acc).then_inc(N["ss"], 1)

        def residual(dve, d, first, n, w, done, count):
            x = xT[:, bass.ds(d, 1), 0:n * w].rearrange("p a (n w) -> p (a n) w", w=w)
            dve.tensor_tensor(x, x, banks(first, n, w), ALU.add).then_inc(S[done], 1)

        chunks = [(t, kc) for t in range(NT) for kc in range(t // 4 + 1)]
        turns = [(u, kc) for u in range(2 * NT) for kc in range(u // 8 + 1)]
        NS, NU = len(chunks), len(turns)
        last_chunk = {t: chunks.index((t, t // 4)) for t in range(NT)}
        last_turn = {u: turns.index((u, u // 8)) for u in range(2 * NT)}
        ahead = [[] for _ in turns]
        coming = 2
        for step, (u, kc) in enumerate(turns):
            t, upto = u // 2, (u // 2 + 1, u % 2)
            if u % 2 and t + 2 <= 4:
                upto = (t + 2, 0)
            while kc == 0 and coming < NS and chunks[coming] <= upto:
                ahead[step].append(coming)
                coming += 1
        assert coming == NS

        def tile_done(n):
            return n + 1 + 2 * CREDIT

        with nc.Block() as block:
            @block.sync
            def _(sp):
                for t in range(NT):
                    sp.dma_start(x_in[:, t, :], A["x"][0, t * P:(t + 1) * P, :]).then_inc(xin_lds[t], 16)
                    if t == 0:
                        sp.dma_start(eye[:, :], A["eye"]).then_inc(S["eye_ld"], 16)
                sp.dma_start(meta_in[:, :], A["meta_tokens_2"]).then_inc(S["meta_ld"], 16)

                def tile(n):
                    return A["stream"][bass.ds(n, 1)].rearrange("a p c n -> p (a c) n")

                for j in range(2):
                    sp.dma_start(w_raw[j][:, :, :], tile(j)).then_inc(S[f"w_ld{j}"], 16)
                sp.dma_start(ones[:, :], A["ones"]).then_inc(S["const_ld"], 16)
                sp.dma_start(block64[:, :], A["block"]).then_inc(S["const_ld"], 16)
                sp.dma_start(swap[:, :], A["swap"]).then_inc(S["const_ld"], 16)
                with sp.Fori(1, TILES // 2) as i:
                    for j in range(2):
                        sp.wait_ge(S["w_split"], 2 * i + j - 1)
                        sp.dma_start(w_raw[j][:, :, :], tile(2 * i + j)).then_inc(S[f"w_ld{j}"], 16)
                w_in2 = A["w_in_2"]
                sp.wait_ge(S["w_split"], TILES)
                sp.wait_ge(S["w_used"], tile_done(TILES - 1))
                for j, c in enumerate((QA, KA, VA)):
                    load(sp, j, cols(w_in2, c))
                sp.dma_start(biasH[:, :], A["neg_dist"]).then_inc(S["dist_ld"], 16)
                sp.wait_ge(S["dn_x"], KD)
                sp.dma_start(x_keep, x2T[:, :, :]).then_inc(S["keep_st"], 16)

            @block.gpsimd
            def _(pool):
                pool.memset(eps[:, :], EPS).then_inc(S["eps_set"], 1)
                pool.memset(zero[:, :], 0.0).then_inc(S["eps_set"], 1)
                pool.memset(xT[:, :, T2:TP], 0.0).then_inc(S["pad_set"], 1)
                with pool.Fori(0, TILES // 2) as i:
                    for j in range(2):
                        pool.wait_ge(S[f"w_ld{j}"], 16 * i + 16)
                        pool.wait_ge(S["w_used"], tile_done(2 * i + j - 2))
                        seen(pool)
                        pool.tensor_copy(w_hi[j][:, :, :], w_raw[j][:, :, :]).then_inc(S["w_rounded"], 1)
                        pool.wait_ge(S["w_rounded"], 2 * i + j + 1)
                        pool.tensor_tensor(w_lo[j][:, :, :], w_raw[j][:, :, :], w_hi[j][:, :, :], ALU.subtract).then_inc(S["w_split"], 1)

            @block.scalar
            def _(act):
                act.dma_start(gains[:, :], A["vectors"]).then_inc(S["gain_ld"], 16)
                for n, g in enumerate(("lambda_q1_2", "lambda_k1_2", "lambda_q2_2", "lambda_k2_2")):
                    act.dma_start(lams[:, n, :], A[g].broadcast_to([P, HD])).then_inc(S["lam_ld"], 16)
                act.dma_start(bias1[:, :], A["log_count"]).then_inc(S["bias_ld"], 16)

                for t in range(NT):
                    act.wait_ge(S["x_t"], 2 * t + 2)
                    act.activation(xT[:, 4:8, t * P:(t + 1) * P], bank(2 * (t % 4) + 1).rearrange("p (c n) -> p c n", n=P), ACT.Copy).then_inc(S["x_act"], 1)
                act.wait_ge(S["x_t"], 2 * NT + 2)
                act.activation(xT[:, 4:8, T1:T2], bank(1, 4 * META).rearrange("p (c n) -> p c n", n=META), ACT.Copy).then_inc(S["x_act"], 1)
                act.wait_ge(S["x_act"], NT + 1)
                act.wait_ge(S["x_dve"], NT + 1)
                act.wait_ge(S["pad_set"], 1)
                act.dma_start(x_keep, xT[:, :, :]).then_inc(S["keep_st"], 16)
                act.wait_ge(S["eps_set"], 2)
                norm_root(act, 0, T1, xT, 2, BANK)
                norm_round(act, 0)
                act.wait_ge(S["keep_st"], 16)
                with act.Fori(0, DCT) as p:
                    act.wait_ge(S["w_used"], tile_done(6 * p))
                    act.activation(u_sb[:, :], wide(0, T1), ACT.Copy).then_inc(S["conv_u"], 1)
                    act.wait_ge(S["conv_y"], p + 1)
                    act.wait_ge(S["mix_acc"], p + 1)
                    act.activation(conv_sq[:, :], convT[:, bass.ds(p, 1), :].rearrange("p a n -> p (a n)"), ACT.Square).then_inc(S["mix_sq"], 1)
                    for n in range(2):
                        act.wait_ge(S["w_used"], tile_done(6 * p + 3 + n))
                        act.activation(sq[n][:, 0:T1], wide(2 * n, T1), ACT.Square).then_inc(S["a1_sq"], 1)
                    for n, buf in ((0, sd), (1, acc)):
                        act.wait_ge(S["a1_ss"], 2 * p + n + 1)
                        act.activation(buf[:, 0:T1], wide(4, T1), ACT.Sqrt, scale=1.0 / HD, bias=eps[:, :]).then_inc(S["a1_sd"], 1)
                    act.wait_ge(S["w_used"], tile_done(6 * p + 5))
                    act.wait_ge(S["conv_a"], p + 1)
                    act.activation(vT1[:, :], wide(6, T1), ACT.Copy).then_inc(S["a1_vf"], 1)
                    for n in range(2):
                        act.wait_ge(S["a1_vt"], 2 * p + n + 1)
                        act.activation(V1[:, 4 * n:4 * n + 4, :], bank(6 + n).rearrange("p (t n) -> p t n", n=P), ACT.Copy).then_inc(S["a1_vs"], 1)

                    def exp(u):
                        nk = (u // 2 + 1) * P
                        act.wait_ge(S["a1_max"], 2 * NS * p + 2 * last_chunk[u // 2] + u % 2 + 1)
                        if u >= 4:
                            act.wait_ge(S["a1_rd"], 16 * p + u - 3)
                        act.activation(E1[u % 4][:, 0:nk], E1[u % 4][:, 0:nk], ACT.Exp, scale=-1.0, bias=small[:, u % 4:u % 4 + 1],
                                       accum_out=small[:, 4 + u % 4:5 + u % 4]).then_inc(S["a1_e"], 1)

                    for u in range(4):
                        exp(u)
                    for step, (u, kc) in enumerate(turns):
                        if step % 2:
                            n = min(u // 2 + 1 - 4 * kc, 4)
                            act.wait_ge(S["a1_t"], NU * p + step + 1)
                            if step >= 4:
                                act.wait_ge(S["a1_o"], NU * p + step - 3)
                            act.activation(PT1[step % 4][:, 0:n, :], bank(4 + step % 3, n * P).rearrange("p (j n) -> p j n", n=P), ACT.Copy).then_inc(S["a1_pt_a"], 1)
                        for s in ahead[step]:
                            t = chunks[s][0]
                            if last_chunk[t] == s:
                                exp(2 * t)
                                exp(2 * t + 1)
                act.wait_ge(S["a1_o"], NU * DCT)
                act.dma_start(xT[:, :, :], x_keep).then_inc(S["keep_ld"], 16)
                for t in range(NT):
                    act.wait_ge(S["a1_y"], 16 * DCT + CREDIT)
                    act.activation(sq[0][:, 0:DC], y_tok[:, t, :], ACT.Square, accum_out=ss1[:, t:t + 1]).then_inc(S["a1_ysq"], 1)
                    act.wait_ge(S["a1_ysq"], t + 1)
                act.activation(ss1[:, NT:2 * NT], ss1[:, 0:NT], ACT.Sqrt, scale=1.0 / DC, bias=eps[:, :]).then_inc(S["a1_ysd"], 1)
                act.wait_ge(S["cn_sum"], 1)
                act.activation(sd[:, 0:T1], wide(0, T1), ACT.Sqrt, scale=1.0 / DC, bias=eps[:, :]).then_inc(S["cn_sd"], 1)
                for i in range(DCT):
                    act.wait_ge(S["cn_n"], i + 1)
                    act.activation(u_hi[:, i, :], convT[:, i, :], ACT.Copy).then_inc(S["cn_hi"], 1)
                for f in range(DCT):
                    act.wait_ge(S["a1_yt"], f + 1)
                    act.activation(u_hi[:, DCT + f, :], wide(2 * ((f + 1) % 4), T1), ACT.Copy, scale=gains[:, G_ATTN + f:G_ATTN + f + 1]).then_inc(S["a1_hi"], 1)
                act.wait_ge(S["wo_x"], KD + 4 * CREDIT)
                act.dma_start(x_keep, xT[:, :, :]).then_inc(S["keep_st"], 16)
                norm_root(act, 1, T1, xT, 2, BANK)
                norm_round(act, 1)
                with act.Fori(0, NF // 2) as i:
                    for j in range(2):
                        act.wait_ge(S["w_used"], tile_done(UP0 + 4 * i + 2 * j))
                        act.wait_ge(S["up_h"], 2 * i + j - 1 + 2 * CREDIT)
                        act.activation(silu1[j][:, 0:T1], wide(4 * j, T1), ACT.Silu).then_inc(S["up_s"], 1)
                act.wait_ge(S["w_used"], tile_done(DOWN0 - 1))
                act.dma_start(x2T[:, :, :], x_keep).then_inc(S["keep_ld"], 16)
                act.wait_ge(S["up_h"], NF + 2 * CREDIT)

                def round_tile(m, c):
                    act.wait_ge(S["w_used"], tile_done(DOWN0 + m - 2))
                    for k in range(2):
                        act.activation(hid_hi[2 * slot + k][:, :], hid[:, bass.ds(c + k, 1), :].rearrange("p a n -> p (a n)"), ACT.Copy).then_inc(S["hid_hi"], 1)

                with act.Fori(0, NF // 4) as i:
                    for slot in range(2):
                        round_tile(2 * i + slot, 4 * i + 2 * slot)
                slot = 0
                round_tile(NF // 2 - 1, NF - 2)
                slot = 1
                round_tile(NF // 2, 0)
                with act.Fori(0, NF // 4) as i:
                    for slot in range(2):
                        round_tile(NF // 2 + 1 + 2 * i + slot, 4 * i + 2 * slot + 2)
                act.wait_ge(S["dn_x"], KD)
                norm_root(act, 2, TP, x2T, 3, CH)
                act.wait_ge(S["lam_dot"], 2)
                act.activation(lam_sm[:, 2:4], lam_sm[:, 0:2], ACT.Exp).then_inc(S["lam_exp"], 1)

            @block.vector
            def _(dve):
                dve.sem_inc(S["a1_y"], CREDIT)
                dve.sem_inc(S["wo_x"], 4 * CREDIT)
                dve.sem_inc(S["up_h"], 2 * CREDIT)
                for t in range(NT):
                    dve.wait_ge(S["x_t"], 2 * t + 1)
                    dve.tensor_copy(xT[:, 0:4, t * P:(t + 1) * P], bank(2 * (t % 4)).rearrange("p (c n) -> p c n", n=P)).then_inc(S["x_dve"], 1)
                dve.wait_ge(S["x_t"], 2 * NT + 1)
                dve.tensor_copy(xT[:, 0:4, T1:T2], bank(0, 4 * META).rearrange("p (c n) -> p c n", n=META)).then_inc(S["x_dve"], 1)
                dve.wait_ge(S["gain_ld"], 16)
                for dst, src, k in ((G_Q8, G_Q, HD ** -0.5), (G_SUBI, G_SUB, 1.0 - LAM_INIT), (G_QNS, G_QN, HB ** -0.5)):
                    dve.tensor_scalar(g_heads[:, dst:dst + 1], gains[:, src:src + 1], float(k), None, ALU.mult).then_inc(S["gain_set"], 1)
                dve.wait_ge(S["x_t"], 2 * NT + 2)
                norm_split(dve, 0, xT)
                dve.wait_ge(S["n_lo"], KD)
                dve.wait_ge(S["keep_st"], 16)
                dve.memset(conv_acc[:, :], 0.0).then_inc(S["mix_acc"], 1)
                dve.memset(gated[:, 0:2], 0.0).then_inc(S["conv_k"], 1)
                dve.wait_ge(S["bias_ld"], 16)
                dve.wait_ge(S["gain_set"], 3)
                with dve.Fori(0, DCT) as p:
                    k0 = p * 3 + 1
                    dve.wait_ge(S["w_used"], tile_done(6 * p + 2))
                    dve.wait_ge(S["conv_u"], p + 1)
                    dve.wait_ge(S["conv_k"], k0)
                    dve.tensor_tensor(gated[:, 2:2 + T1], wide(4, T1), u_sb[:, :], ALU.mult).then_inc(S["conv_a"], 1)
                    dve.wait_ge(S["conv_a"], p + 1)
                    conv = convT[:, bass.ds(p, 1), :].rearrange("p a n -> p (a n)")
                    for k in range(3):
                        w = gains[:, bass.ds(CONV_W + (2 - k) * DCT + p, 1)]
                        src = gated[:, 2 - k:2 - k + T1]
                        if k == 0:
                            dve.tensor_scalar(conv, src, w, None, ALU.mult).then_inc(S["conv_k"], 1)
                        else:
                            dve.wait_ge(S["conv_k"], k0 + k)
                            dve.scalar_tensor_tensor(conv, src, w, conv, ALU.mult, ALU.add).then_inc(S["conv_k"], 1)
                    dve.wait_ge(S["conv_k"], k0 + 3)
                    dve.tensor_tensor(conv, wide(2, T1), conv, ALU.mult).then_inc(S["conv_y"], 1)
                    dve.wait_ge(S["mix_sq"], p + 1)
                    dve.wait_ge(S["mix_acc"], p + 1)
                    dve.tensor_tensor(conv_acc[:, :], conv_acc[:, :], conv_sq[:, :], ALU.add).then_inc(S["mix_acc"], 1)
                    for n, (dst, root, gain) in enumerate(((qT1, sd, g_heads[:, G_Q8:G_Q8 + 1]), (kT1, acc, gains[:, G_K:G_K + 1]))):
                        if n:
                            dve.wait_ge(S["a1_qn"], 2 * p + 1)
                        dve.wait_ge(S["a1_sd"], 2 * p + n + 1)
                        dve.reciprocal(rs[:, 0:T1], root[:, 0:T1]).then_inc(S["a1_r"], 1)
                        dve.wait_ge(S["a1_r"], 2 * p + n + 1)
                        dve.scalar_tensor_tensor(dst[:, :], wide(2 * n, T1), gain, rs[:, 0:T1], ALU.mult, ALU.mult).then_inc(S["a1_qn"], 1)

                    def scores(s):
                        t, kc = chunks[s]
                        k0, k1 = kc * BANK, min((kc + 1) * BANK, (t + 1) * P)
                        for a in range(2):
                            u = 2 * t + a
                            part, low = small[:, 20 + u % 4:21 + u % 4], small[:, u % 4:u % 4 + 1]
                            if a == 0:
                                dve.wait_ge(S["a1_s"], NS * p + s + 1)
                            if u >= 4 and kc == 0:
                                dve.wait_ge(S["a1_t"], NU * p + last_turn[u - 4] + 1)
                            if kc:
                                dve.wait_ge(S["a1_max"], 2 * NS * p + 2 * (s - 1) + a + 1)
                            seen(dve)
                            dve.tensor_tensor_reduce(E1[u % 4][:, k0:k1], bank(2 * (s % 2) + a, k1 - k0), bias1[:, T1 - (t + 1) * P + k0:T1 - (t + 1) * P + k1],
                                                     -1.0, part if kc else BIG, ALU.add, ALU.min, low if s == last_chunk[t] else part).then_inc(S["a1_max"], 1)

                    def result(u):
                        dve.wait_ge(S["a1_e"], 16 * p + u + 1)
                        dve.reciprocal(small[:, 16 + u % 4:17 + u % 4], small[:, 4 + u % 4:5 + u % 4]).then_inc(S["a1_rd"], 1)
                        dve.wait_ge(S["a1_rd"], 16 * p + u + 1)
                        dve.wait_ge(S["a1_o"], NU * p + last_turn[u] + 1)
                        dve.tensor_scalar(y_tok[:, u // 2, bass.ds(p * P + (u % 2) * HD, HD)], bank(7, HD), small[:, 16 + u % 4:17 + u % 4],
                                          None, ALU.mult).then_inc(S["a1_y"], 1)

                    scores(0)
                    scores(1)
                    for step in range(NU + 3):
                        if step >= 3 and step - 3 in last_turn.values():
                            result(turns[step - 3][0])
                        if step >= NU:
                            continue
                        u, kc = turns[step]
                        for s in ahead[step]:
                            scores(s)
                        if step % 2 == 0:
                            n = min(u // 2 + 1 - 4 * kc, 4)
                            dve.wait_ge(S["a1_t"], NU * p + step + 1)
                            if step >= 4:
                                dve.wait_ge(S["a1_o"], NU * p + step - 3)
                            dve.tensor_copy(PT1[step % 4][:, 0:n, :], bank(4 + step % 3, n * P).rearrange("p (j n) -> p j n", n=P)).then_inc(S["a1_pt_d"], 1)
                dve.wait_ge(S["a1_y"], 16 * DCT + CREDIT)
                dve.wait_ge(S["a1_ysd"], 1)
                dve.reciprocal(ss1[:, 0:NT], ss1[:, NT:2 * NT]).then_inc(S["a1_yr"], 1)
                dve.wait_ge(S["a1_yr"], 1)
                for t in range(NT):
                    dve.tensor_scalar(y_tok[:, t, :], y_tok[:, t, :], ss1[:, t:t + 1], None, ALU.mult).then_inc(S["a1_yn"], 1)
                dve.wait_ge(S["cn_sd"], 1)
                dve.reciprocal(rs[:, 0:T1], sd[:, 0:T1]).then_inc(S["cn_r"], 1)
                dve.wait_ge(S["cn_r"], 1)
                for i in range(DCT):
                    dve.scalar_tensor_tensor(convT[:, i, :], convT[:, i, :], gains[:, G_CONV + i:G_CONV + i + 1], rs[:, 0:T1], ALU.mult, ALU.mult).then_inc(S["cn_n"], 1)
                for i in range(DCT):
                    dve.wait_ge(S["cn_hi"], i + 1)
                    dve.tensor_tensor(u_lo[:, i, :], convT[:, i, :], u_hi[:, i, :], ALU.subtract).then_inc(S["cn_lo"], 1)
                for f in range(DCT):
                    dve.wait_ge(S["a1_hi"], f + 1)
                    dve.scalar_tensor_tensor(u_lo[:, DCT + f, :], wide(2 * ((f + 1) % 4), T1), gains[:, G_ATTN + f:G_ATTN + f + 1], u_hi[:, DCT + f, :],
                                             ALU.mult, ALU.subtract).then_inc(S["a1_lo"], 1)
                dve.wait_ge(S["keep_ld"], 16)
                with dve.Fori(0, KD // 4) as i:
                    for j in range(4):
                        dve.wait_ge(S["w_used"], tile_done(W_OUT0 + 4 * i + j))
                        residual(dve, 4 * i + j, 2 * j, 2, BANK, "wo_x", None)
                dve.wait_ge(S["wo_x"], KD + 4 * CREDIT)
                norm_split(dve, 1, xT)
                dve.wait_ge(S["keep_st"], 32)
                dve.wait_ge(S["n_lo"], 2 * KD)
                with dve.Fori(0, NF // 2) as i:
                    for j in range(2):
                        dve.wait_ge(S["up_s"], 2 * i + j + 1)
                        dve.wait_ge(S["w_used"], tile_done(UP0 + 4 * i + 2 * j + 1))
                        dve.tensor_tensor(hid[:, bass.ds(2 * i + j, 1), :].rearrange("p a n -> p (a n)"), silu1[j][:, 0:T1], wide(4 * j + 2, T1), ALU.mult).then_inc(S["up_h"], 1)

                def rest_tile(m, c):
                    for k in range(2):
                        dve.wait_ge(S["hid_hi"], 2 * m + k + 1)
                        dve.tensor_tensor(hid_lo[2 * slot + k][:, :], hid[:, bass.ds(c + k, 1), :].rearrange("p a n -> p (a n)"), hid_hi[2 * slot + k][:, :],
                                          ALU.subtract).then_inc(S["hid_lo"], 1)

                def add_half(o):
                    dve.wait_ge(S["keep_ld"], 32)
                    for d in range(HALF):
                        if d < HALF - 1:
                            dve.wait_ge(S["dn_z"], (HALF - 1) * o + d + 1)
                        else:
                            dve.wait_ge(S["w_used"], tile_done(DOWN0 + (o + 1) * (NF // 2) - 1))
                        x = x2T[:, o * HALF + d, 0:T1]
                        dve.tensor_tensor(x, x, wide(2 * d, T1), ALU.add).then_inc(S["dn_x"], 1)

                with dve.Fori(0, NF // 4) as i:
                    for slot in range(2):
                        rest_tile(2 * i + slot, 4 * i + 2 * slot)
                slot = 0
                rest_tile(NF // 2 - 1, NF - 2)
                slot = 1
                rest_tile(NF // 2, 0)
                add_half(0)
                with dve.Fori(0, NF // 4) as i:
                    for slot in range(2):
                        rest_tile(NF // 2 + 1 + 2 * i + slot, 4 * i + 2 * slot + 2)
                add_half(1)
                dve.wait_ge(S["dn_x"], KD)
                norm_apply(dve, 2, TP, x2T, uT)
                dve.wait_ge(S["lam_ld"], 64)
                for n in range(2):
                    dve.tensor_tensor_reduce(junk[:, n * HD:(n + 1) * HD], lams[:, 2 * n, :], lams[:, 2 * n + 1, :], 1.0, 0.0, ALU.mult, ALU.add,
                                             lam_sm[:, n:n + 1]).then_inc(S["lam_dot"], 1)
                dve.wait_ge(S["lam_exp"], 1)
                dve.tensor_scalar(lam_sm[:, 4:5], lam_sm[:, 3:4], lam_sm[:, 2:3], -LAM_INIT, ALU.subtract, ALU.add).then_inc(S["lam_done"], 1)
                dve.wait_ge(S["lam_done"], 1)
                dve.memset(ss2[:, :, :], 1.0).then_inc(S["as_init"], 1)

            @block.tensor
            def _(pe):
                pe.sem_inc(S["w_used"], 2 * CREDIT)
                pe.wait_ge(S["eye_ld"], 16)
                for t in range(NT):
                    pe.wait_ge(xin_lds[t], 16)
                    for half in range(2):
                        if t >= 4:
                            pe.wait_ge(S["x_act" if half else "x_dve"], t - 3)
                        for c in range(4):
                            last = turn(bank(2 * (t % 4) + half, P, c * P), x_in[:, t, (4 * half + c) * P:(4 * half + c + 1) * P])
                        last.then_inc(S["x_t"], 1)
                pe.wait_ge(S["meta_ld"], 16)
                for half in range(2):
                    pe.wait_ge(S["x_act" if half else "x_dve"], 5)
                    for c in range(4):
                        last = turn(bank(half, META, c * META), meta_in[:, (4 * half + c) * P:(4 * half + c + 1) * P], META)
                    last.then_inc(S["x_t"], 1)
                pe.wait_ge(S["const_ld"], 48)
                pe.wait_ge(S["x_dve"], NT + 1)
                norm_sum(pe, 0, 2, BANK)
                pe.wait_ge(N["sd"], 1)
                with pe.Fori(0, DCT) as p:
                    for j in range(3):
                        project_split(pe, j % 2, 6 * p + j, 2 * j, u_hi, u_lo, None if j else lambda c: pe.wait_ge(S["n_lo"], c + 1)).then_inc(S["w_used"], 1)
                    pe.wait_ge(S["conv_u"], p + 1)
                    project_split(pe, 1, 6 * p + 3, 0, u_hi, u_lo).then_inc(S["w_used"], 1)
                    pe.wait_ge(S["conv_y"], p + 1)
                    project_split(pe, 0, 6 * p + 4, 2, u_hi, u_lo).then_inc(S["w_used"], 1)

                    def head_sums(n):
                        pe.wait_ge(S["a1_sq"], 2 * p + n + 1)
                        if n:
                            pe.wait_ge(S["a1_sd"], 2 * p + 1)
                        for b in range(2):
                            last = mm(bank(4 + b), block64[:, :], sq[n][:, b * BANK:(b + 1) * BANK], start=True, stop=True)
                        last.then_inc(S["a1_ss"], 1)

                    head_sums(0)
                    pe.wait_ge(S["a1_y"], 16 * p + CREDIT)
                    project_split(pe, 1, 6 * p + 5, 6, u_hi, u_lo).then_inc(S["w_used"], 1)
                    head_sums(1)
                    pe.wait_ge(S["a1_vf"], p + 1)
                    for n in range(2):
                        for t in range(4):
                            last = turn(bank(6 + n, P, t * P), vT1[:, (4 * n + t) * P:(4 * n + t + 1) * P])
                        last.then_inc(S["a1_vt"], 1)

                    def scores(s):
                        t, kc = chunks[s]
                        k0, k1 = kc * BANK, min((kc + 1) * BANK, (t + 1) * P)
                        if s == 0:
                            pe.wait_ge(S["a1_qn"], 2 * p + 2)
                        if s >= 2:
                            pe.wait_ge(S["a1_max"], 2 * NS * p + 2 * (s - 2) + 2)
                        for a in range(2):
                            r = slice(a * HD, (a + 1) * HD)
                            last = mm(bank(2 * (s % 2) + a, k1 - k0), qT1[r, t * P:(t + 1) * P], kT1[r, k0:k1], start=True, stop=True)
                        last.then_inc(S["a1_s"], 1)

                    def taken(step):
                        pe.wait_ge(S["a1_pt_a" if step % 2 else "a1_pt_d"], NU // 2 * p + step // 2 + 1)

                    def turn_probs(step):
                        u, kc = turns[step]
                        if kc == 0:
                            pe.wait_ge(S["a1_e"], 16 * p + u + 1)
                        if step >= 3:
                            taken(step - 3)
                        elif step == 2:
                            pe.wait_ge(S["a1_vs"], 2 * p + 1)
                        for j in range(4 * kc, min(4 * kc + 4, u // 2 + 1)):
                            last = turn(bank(4 + step % 3, P, (j % 4) * P), E1[u % 4][:, j * P:(j + 1) * P])
                        last.then_inc(S["a1_t"], 1)

                    def values(step):
                        u, kc = turns[step]
                        t, a = u // 2, u % 2
                        taken(step)
                        if step == 0:
                            pe.wait_ge(S["a1_vs"], 2 * p + 2)
                        elif kc == 0:
                            pe.wait_ge(S["a1_y"], 16 * p + u + CREDIT)
                        for j in range(4 * kc, min(4 * kc + 4, t + 1)):
                            last = mm(bank(7, HD), PT1[step % 4][:, j % 4, :], V1[:, j, a * HD:(a + 1) * HD], start=(j == 0), stop=(j == t))
                        last.then_inc(S["a1_o"], 1)

                    scores(0)
                    scores(1)
                    for step in range(NU):
                        for s in ahead[step]:
                            scores(s)
                        turn_probs(step)
                        if step >= 2:
                            values(step - 2)
                    values(NU - 2)
                    values(NU - 1)
                pe.wait_ge(S["mix_acc"], DCT + 1)
                total(0, 2, BANK, conv_acc).then_inc(S["cn_sum"], 1)
                pe.wait_ge(S["a1_yn"], NT)
                for f in range(DCT):
                    b = 2 * ((f + 1) % 4)
                    if b == 0:
                        pe.wait_ge(S["cn_sd"], 1)
                    for t in range(NT):
                        last = turn(bank(b + t // 4, P, (t % 4) * P), y_tok[:, t, f * P:(f + 1) * P])
                    last.then_inc(S["a1_yt"], 1)
                pe.wait_ge(S["cn_lo"], DCT)
                pe.wait_ge(S["a1_lo"], DCT)
                with pe.Fori(0, KD // 4) as i:
                    for j in range(4):
                        pe.wait_ge(S["wo_x"], 4 * i + j - 3 + 4 * CREDIT)
                        project_split(pe, j % 2, W_OUT0 + 4 * i + j, 2 * j, u_hi, u_lo).then_inc(S["w_used"], 1)
                norm_sum(pe, 1, 2, BANK)
                with pe.Fori(0, NF // 2) as i:
                    for j in range(2):
                        pe.wait_ge(S["up_h"], 2 * i + j - 1 + 2 * CREDIT)
                        ready = None if j else lambda c: pe.wait_ge(S["n_lo"], KD + c + 1)
                        project_split(pe, 0, UP0 + 4 * i + 2 * j, 4 * j, u_hi, u_lo, ready).then_inc(S["w_used"], 1)
                        project_split(pe, 1, UP0 + 4 * i + 2 * j + 1, 4 * j + 2, u_hi, u_lo).then_inc(S["w_used"], 1)

                def down_tile(m, o, first=False, end=False):
                    pe.wait_ge(S["w_split"], DOWN0 + m + 1)
                    order = [(k, d) for d in range(HALF) for k in range(2)] if end else [(k, d) for k in range(2) for d in range(HALF)]
                    for n, (k, d) in enumerate(order):
                        if n == 0 or (not end and d == 0):
                            pe.wait_ge(S["hid_lo"], 2 * m + k + 1 + (1 if end else 0))
                        if first and o and k == 0:
                            pe.wait_ge(S["dn_x"], d + 1)
                        for q, (w, src) in enumerate(((w_hi, hid_hi), (w_hi, hid_lo), (w_lo, hid_hi))):
                            for b in range(2):
                                last = mm(bank(2 * d + b), w[slot][:, k * HALF + d, :], src[2 * slot + k][:, b * BANK:(b + 1) * BANK],
                                          start=(first and k == 0 and q == 0), stop=(end and k == 1 and q == 2))
                        if end and k == 1 and d < HALF - 1:
                            last.then_inc(S["dn_z"], 1)
                    last.then_inc(S["w_used"], 1)

                pe.wait_ge(S["up_h"], NF + 2 * CREDIT)
                for o in range(2):
                    m0 = o * (NF // 2)
                    slot = m0 % 2
                    down_tile(m0, o, first=True)
                    with pe.Fori(0, NF // 4 - 1) as i:
                        for j in range(2):
                            slot = (m0 + 1 + j) % 2
                            down_tile(m0 + 1 + 2 * i + j, o)
                    slot = (m0 + 1) % 2
                    down_tile(m0 + NF // 2 - 2, o)
                    slot = m0 % 2
                    down_tile(m0 + NF // 2 - 1, o, end=True)
                norm_sum(pe, 2, 3, CH)

        nc.clear_and_free_semaphores(list(first_sems.values()))
        nc.all_engine_barrier()
        S.update({n: sem(n) for n in second_block})
        gate_ld = [sem(f"gate_ld{j}") for j in range(EK)]
        up_ld = [sem(f"up_ld{j}") for j in range(EK)]
        down_ld = sem("down_ld")
        row_st = [sem(f"row_st{j}") for j in range(4)]

        with nc.Block() as block:
            @block.sync
            def _(sp):
                w_in2 = A["w_in_2"]
                with sp.Fori(1, HEADS) as h:
                    for j, (c, done, k) in enumerate(((QA, "aa_q", 1), (KA, "aa_k", 1), (VA, "aa_v", 3))):
                        sp.wait_ge(S[done], k * h)
                        load(sp, j, cols(w_in2, c + h))
                load(sp, 3, cols(w_in2, VB))
                load(sp, 4, cols(w_in2, KB))
                sp.wait_ge(S["as_t"], 2 * (NT + 1))
                sp.dma_start(cos[:, :], A["cos"]).then_inc(S["rope_ld"], 16)
                sp.dma_start(sin[:, :], A["sin"]).then_inc(S["rope_ld"], 16)
                for g in range(KV):
                    n0 = g * (GROUP + 1)
                    if g:
                        sp.wait_ge(S["ob_v"], 3 * g)
                        load(sp, 3, cols(w_in2, VB + g))
                        sp.wait_ge(S["ob_z"], n0)
                        load(sp, 4, cols(w_in2, KB + g))
                    for j in range(GROUP):
                        if n0 + j:
                            sp.wait_ge(S["ob_z"], n0 + j + (1 if j else 0))
                        load(sp, 5, cols(w_in2, QB + (g * GROUP + j)))
                w_a, w_b = A["w_branch_a_2"], A["w_branch_b_2"]
                sp.wait_ge(S["aa_v"], 3 * HEADS)
                load(sp, 0, cols(w_in2, GA))
                load(sp, 1, cols(w_a, 0))
                load(sp, 2, cols(w_in2, GB))
                sp.wait_ge(S["ob_v"], 3 * KV)
                load(sp, 3, cols(w_b, 0))
                with sp.Fori(1, KD) as d:
                    for j, (w, c, done) in enumerate(((w_in2, GA, "mg_ga"), (w_a, 0, "mg_ya"),
                                                      (w_in2, GB, "mg_gb"), (w_b, 0, "mg_yb"))):
                        sp.wait_ge(S[done], d)
                        load(sp, j, cols(w, c + d))
                w_out2 = A["w_out_2"]
                sp.wait_ge(S["ob_z"], KV * (GROUP + 1))
                load(sp, 4, cols(w_out2, 0))
                load(sp, 5, cols(w_out2, 1))
                sp.wait_ge(S["mg_yb"], KD)
                sp.wait_ge(S["keep_st"], 48)
                sp.dma_start(xT[:, :, :], x_keep).then_inc(S["keep_ld"], 16)
                with sp.Fori(1, KD // 2) as i:
                    for j in range(2):
                        sp.wait_ge(S["w2_z"], 2 * i - 1 + j)
                        load(sp, 4 + j, cols(w_out2, i * 2 + j))
                sp.wait_ge(S["w2_z"], KD)
                sp.dma_start(router[:, :, :], A["w_router_2"][0].rearrange("(c p) n -> p c n", p=P)).then_inc(S["router_ld"], 16)
                wg, wu, wd = A["w_gate_2"], A["w_up_2"], A["w_down_2"][0]

                def expert_cols(w, e, j):
                    return w[bass.ds(e, 1), j].rearrange("a p c n -> p (a c) n")

                def expert_rows(w, e, j):
                    return w[bass.ds(e, 1), j * P:(j + 1) * P, :].rearrange("a p n -> p (a n)")

                for j in range(EK):
                    sp.dma_start(w_gate[:, j, :, :], expert_cols(wg, 0, j)).then_inc(gate_ld[j], 16)
                    sp.dma_start(w_up[:, j, :, :], expert_cols(wu, 0, j)).then_inc(up_ld[j], 16)
                for j in range(EK):
                    sp.dma_start(w_down[:, j, :], expert_rows(wd, 0, j)).then_inc(down_ld, 16)
                for t in range(NT + 1):
                    rows = P if t < NT else META
                    r0 = META + t * P if t < NT else 0
                    sp.wait_ge(S["hr_c"], 2 * (t + 1))
                    sp.dma_start(h_rows[r0:r0 + rows, :], h_row[t % 2][0:rows, :]).then_inc(row_st[t % 2], 16)
                    sp.wait_ge(S["ur_c"], 2 * (t + 1))
                    sp.dma_start(u_rows[r0:r0 + rows, :], u_row[t % 2][0:rows, :]).then_inc(row_st[2 + t % 2], 16)
                with sp.Fori(1, NE) as e:
                    for j in range(EK):
                        sp.wait_ge(S["ex_g"], e * EK - (EK - 1) + j)
                        sp.dma_start(w_gate[:, j, :, :], expert_cols(wg, e, j)).then_inc(gate_ld[j], 16)
                        sp.wait_ge(S["ex_u"], e * EK - (EK - 1) + j)
                        sp.dma_start(w_up[:, j, :, :], expert_cols(wu, e, j)).then_inc(up_ld[j], 16)
                    sp.wait_ge(S["ex_y"], 3 * e)
                    for j in range(EK):
                        sp.dma_start(w_down[:, j, :], expert_rows(wd, e, j)).then_inc(down_ld, 16)
                sp.wait_ge(S["ur_t"], 2 * (NT + 1))
                sp.dma_start(g_fin[:, :], A["g_final_2"].rearrange("(a n) -> a n", a=1).broadcast_to([P, D])).then_inc(S["gfin_ld"], 16)
                sp.wait_ge(S["ex_add_a"], 16 * NE)
                sp.wait_ge(S["ex_add_b"], 16 * NE)
                for t in range(NT):
                    sp.dma_start(fin[t][:, :], h_rows[META + t * P:META + (t + 1) * P, :]).then_inc(xin_lds[t], 16)
                for t in range(NT):
                    sp.wait_ge(S["fin_o"], t + 1)
                    sp.dma_start(out[0, t * P:(t + 1) * P, :], fin[t][:, :]).then_inc(S["fin_st"], 16)
                sp.wait_ge(S["fin_st"], 16 * NT)

            @block.gpsimd
            def _(pool):
                pool.wait_ge(S["dist_ld"], 16)
                with pool.Fori(0, HEADS) as h:
                    pool.wait_ge(S["aa_max"], h * (2 * NT + 2) + CREDIT)
                    seen(pool)
                    pool.tensor_scalar(biasH[:, :], biasH[:, :], 0.5, None, ALU.mult).then_inc(S["aa_bias"], 1)
                for g in range(KV):
                    with pool.Fori(0, GROUP) as j:
                        pool.wait_ge(S["ob_q"], g * (GROUP + 1) + 2 + j)
                        pool.wait_ge(S["bb_s"], (g * GROUP + j) * (NT + 1) + CREDIT)
                        seen(pool)
                        pool.tensor_copy(qs[:, :], q_grp[:, bass.ds(j, 1), :].rearrange("p a n -> p (a n)")).then_inc(S["bb_qs"], 1)
                pool.sem_inc(S["ex_free"], CREDIT)
                pool.wait_ge(S["tk_c"], 4)
                for j in range(4):
                    pool.wait_ge(row_st[j], 16 * ((NT + 2 - j % 2) // 2))

                def gather(e):
                    for r in range(2):
                        pool.tensor_copy(pick_g[r][:, :], pick[r][:, bass.ds(e, 1)]).then_inc(S["ex_pick_g"], 1)
                    pool.wait_ge(S["ex_pick_g"], e * 2 + 2)
                    seen(pool)
                    for r, done in enumerate(("ex_xa", "ex_xb")):
                        pool.indirect_dma_start(xs[r][:, :], None, u_rows, bass.IndirectOffsetOnAxis(ap=pick_g[r][:, :], axis=0)).then_inc(S[done], 16)

                def scatter(e):
                    for r in range(2):
                        pool.tensor_copy(pick_s[r][:, :], pick[r][:, bass.ds(e, 1)]).then_inc(S["ex_pick_s"], 1)
                    pool.wait_ge(S["ex_pick_s"], e * 2 + 2)
                    for r, (rows, done) in enumerate((("ex_ra", "ex_add_a"), ("ex_rb", "ex_add_b"))):
                        pool.wait_ge(S[rows], e * 2 + 2 + CREDIT)
                        seen(pool)
                        pool.indirect_dma_start(h_rows, bass.IndirectOffsetOnAxis(ap=pick_s[r][:, :], axis=0), y_row[r][:, :], None,
                                                compute_op=ALU.add).then_inc(S[done], 16)
                    pool.wait_ge(S["ex_add_a"], e * 16 + 16)
                    pool.wait_ge(S["ex_add_b"], e * 16 + 16)
                    pool.sem_inc(S["ex_free"], 1)

                gather(0)
                with pool.Fori(0, NE - 1) as e:
                    pool.wait_ge(S["ex_xt"], e * 3 + 3)
                    gather(e + 1)
                    scatter(e)
                scatter(NE - 1)

            @block.scalar
            def _(act):
                act.wait_ge(S["as_init"], 1)
                act.wait_ge(S["keep_st"], 48)
                with act.Fori(0, HEADS) as h:
                    act.wait_ge(S["aa_q"], h + 1)
                    act.activation(thirds(qTa[:, :]), banks(0, 3, CH), ACT.Copy, scale=HD ** -0.5).then_inc(S["aa_qs"], 1)
                    act.wait_ge(S["aa_qs"], h + 1)
                    for k in range(2):
                        half = slice(k * HD, (k + 1) * HD)
                        act.activation(q_parts[k][half, :], qTa[half, :], ACT.Copy).then_inc(S["aa_qh"], 1)
                    act.wait_ge(S["aa_ks"], 7 * h + 1)
                    for k in range(2):
                        for n in (k, 1 - k):
                            act.activation(k_lead[k][n * HD:(n + 1) * HD, :], kTa[k * HD:(k + 1) * HD, :], ACT.Copy).then_inc(S["aa_kh"], 1)
                    for n in range(2):
                        act.wait_ge(S["aa_v"], 3 * h + n + 1)
                        act.activation(Va[:, 4 * n:4 * n + 4, :], bank(6 + n).rearrange("p (t n) -> p t n", n=P), ACT.Copy).then_inc(S["aa_vs"], 1)
                    act.wait_ge(S["aa_v"], 3 * h + 3)
                    act.activation(Va[0:META, NT, :], bank(0, P, 0, META), ACT.Copy).then_inc(S["aa_vs"], 1)

                    def take_pt(t):
                        m = P if t < NT else META
                        act.wait_ge(S["aa_t"], 9 * h + t + 1)
                        if t >= 2:
                            act.wait_ge(S["aa_o"], 9 * h + t - 1)
                        act.activation(PTa[t % 2][:, 0:NT, 0:m], wide(5, NT * P).rearrange("p (j n) -> p j n", n=P)[:, :, 0:m], ACT.Copy).then_inc(S["aa_pt"], 1)
                        act.activation(PTa[t % 2][0:META, NT, 0:m], bank(7, m, 256, META), ACT.Copy).then_inc(S["aa_pt9"], 1)

                    def square(t):
                        m = P if t < NT else META
                        act.wait_ge(S["aa_y"], 9 * h + t + 1 + CREDIT)
                        act.activation(junk[0:m, :], o_tok[0:m, t, bass.ds(h * P, P)], ACT.Square,
                                       accum_out=ss2[0:m, t, bass.ds(h, 1)]).then_inc(S["aa_ssq"], 1)
                        act.wait_ge(S["aa_ssq"], 9 * h + t + 1)

                    def exp(t, k):
                        m = P if t < NT else META
                        act.wait_ge(S["aa_max"], 18 * h + 2 * t + k + 1 + CREDIT)
                        e = EA[t % 2][k]
                        act.activation(e[0:m, :], e[0:m, :], ACT.Exp, scale=-1.0, bias=small[0:m, 8 + 2 * (t % 2) + k:9 + 2 * (t % 2) + k],
                                       accum_out=small[0:m, 12 + 2 * (t % 2) + k:13 + 2 * (t % 2) + k]).then_inc(S["aa_e"], 1)

                    def result(t):
                        m = P if t < NT else META
                        act.wait_ge(S["aa_o"], 9 * h + t + 1)
                        seen(act)
                        act.activation(o_tok[0:m, t, bass.ds(h * P, P)], bank(7, P, 0, m), ACT.Copy, scale=small[0:m, 20 + t % 3:21 + t % 3]).then_inc(S["aa_y"], 1)

                    for t in range(NT + 1):
                        exp(t, 0)
                        if t >= 2:
                            result(t - 2)
                        exp(t, 1)
                        if t >= 1:
                            take_pt(t - 1)
                        if t >= 3:
                            square(t - 3)
                    result(NT - 1)
                    take_pt(NT)
                    square(NT - 2)
                    result(NT)
                    for t in range(NT - 1, NT + 1):
                        square(t)
                act.wait_ge(S["aa_ssq"], 9 * HEADS)
                act.activation(rs2[:, :, :], ss2[:, :, :], ACT.Sqrt, scale=1.0 / P, bias=eps[:, :]).then_inc(S["as_sd"], 1)
                for t in range(NT + 1):
                    m = P if t < NT else META
                    act.wait_ge(S["as_t"], 2 * t + 1)
                    act.activation(oaT[:, 0:4, t * P:t * P + m], bank(4 * (t % 2)).rearrange("p (c n) -> p c n", n=P)[:, :, 0:m], ACT.Copy,
                                   scale=g_heads[:, G_SUBI:G_SUBI + 1]).then_inc(S["as_o"], 1)
                    act.wait_ge(S["as_t"], 2 * t + 2)
                    act.activation(oaT[:, 4:8, t * P:t * P + m], bank(4 * (t % 2) + 1).rearrange("p (c n) -> p c n", n=P)[:, :, 0:m], ACT.Copy,
                                   scale=g_heads[:, G_SUBI:G_SUBI + 1]).then_inc(S["as_o"], 1)
                for g in range(KV):
                    v0, z0 = 3 * g, g * (GROUP + 1)
                    def raw(n):
                        i = z0 + n
                        gain = g_heads[:, G_QNS:G_QNS + 1] if n else gains[:, G_KN:G_KN + 1]
                        act.wait_ge(S["ob_z"], i + 1)
                        if i >= 1:
                            act.wait_ge(S["ob_ss"], i)
                            act.wait_ge(S["ob_m"], i)
                            act.wait_ge(S["ob_sw"], i)
                        act.activation(thirds(acc[:, :]), banks(3 * (n % 2), 3, CH), ACT.Copy, scale=gain).then_inc(S["ob_raw"], 1)
                        act.activation(thirds(sq[0][:, :]), banks(3 * (n % 2), 3, CH), ACT.Square).then_inc(S["ob_sq"], 1)

                    def root(n):
                        i = z0 + n
                        act.wait_ge(S["ob_ss"], i + 1)
                        if i >= 1:
                            act.wait_ge(S["ob_r"], i)
                        act.activation(sd[:, 0:T1], wide(6, T1), ACT.Sqrt, scale=1.0 / HB, bias=eps[:, :]).then_inc(S["ob_sd"], 1)
                        act.activation(sd[:, T1:T2], bank(3 * (n % 2) + 2, META, 384), ACT.Sqrt, scale=1.0 / HB, bias=eps[:, :]).then_inc(S["ob_sd"], 1)

                    for n in range(GROUP + 1):
                        raw(n)
                        root(n)
                    for n in range(2):
                        act.wait_ge(S["ob_v"], v0 + n + 1)
                        act.activation(Vb[:, 4 * n:4 * n + 4, :], bank(6 + n).rearrange("p (t n) -> p t n", n=P), ACT.Copy).then_inc(S["ob_vs"], 1)
                    act.wait_ge(S["ob_v"], v0 + 3)
                    act.activation(Vb[0:META, NT, :], bank(5, P, 0, META), ACT.Copy).then_inc(S["ob_vs"], 1)
                    with act.Fori(0, GROUP) as j:
                        def head(j):
                            return (g * GROUP + j) * 9

                        def take_pt(t):
                            m = P if t < NT else META
                            act.wait_ge(S["bb_t"], head(j) + t + 1)
                            if t >= 2:
                                act.wait_ge(S["bb_o"], head(j) + t - 1)
                            act.activation(PTb[t % 2][:, 0:NT, 0:m], wide(5, NT * P).rearrange("p (j n) -> p j n", n=P)[:, :, 0:m], ACT.Copy).then_inc(S["bb_pt"], 1)
                            act.activation(PTb[t % 2][0:META, NT, 0:m], bank(7, m, 256, META), ACT.Copy).then_inc(S["bb_pt9"], 1)

                        for t in range(NT + 1):
                            m = P if t < NT else META
                            act.wait_ge(S["bb_max"], head(j) + t + 1)
                            act.activation(EB[t % 2][0:m, :], EB[t % 2][0:m, :], ACT.Exp, scale=-1.0, bias=small[0:m, 24 + t % 2:25 + t % 2],
                                           accum_out=small[0:m, 26 + t % 2:27 + t % 2]).then_inc(S["bb_e"], 1)
                            if t >= 1:
                                take_pt(t - 1)
                        take_pt(NT)
                with act.Fori(0, KD) as d:
                    for k, (z, done, used) in enumerate((("mg_ga", "mg_sa", "mg_ma"), ("mg_gb", "mg_sb", "mg_mb"))):
                        act.wait_ge(S[z], d + 1)
                        act.wait_ge(S[used], d + CREDIT)
                        act.activation(thirds(sq[k][:, :]), banks(0, 3, CH), ACT.Sigmoid).then_inc(S[done], 1)
                act.wait_ge(S["w2_x"], KD + 2 * CREDIT)
                norm_root(act, 3, TP, xT, 3, CH)
                act.wait_ge(S["router_step"], 5)
                act.activation(aff[:, :, :], aff[:, :, :], ACT.Exp).then_inc(S["lg_e"], 1)
                for t in range(NT + 1):
                    rows = P if t < NT else META
                    for buf, first, src, done, st in ((h_row, 6, "hr_t", "hr_c", 0), (u_row, 2, "ur_t", "ur_c", 2)):
                        if t >= 2:
                            act.wait_ge(row_st[st + t % 2], 16 * (t // 2))
                        for n in range(2):
                            act.wait_ge(S[src], 2 * t + n + 1)
                            act.activation(buf[t % 2][0:rows, n * BANK:(n + 1) * BANK], bank(first + n, BANK, 0, rows), ACT.Copy).then_inc(S[done], 1)
                act.sem_inc(S["ex_rb"], CREDIT)
                with act.Fori(0, NE) as e:
                    for j in range(EK):
                        act.wait_ge(S["ex_g"], e * EK + j + 1)
                        act.wait_ge(S["ex_h"], e * EK + j - 1 + 2 * CREDIT)
                        act.activation(silu_e[j % 2][:, :], bank(3 + 2 * (j % 2), CAP), ACT.Silu).then_inc(S["ex_s"], 1)
                    act.wait_ge(S["ex_free"], e + CREDIT)
                    for n in range(2):
                        act.wait_ge(S["ex_r"], e * 2 + n + 1)
                        seen(act)
                        act.activation(y_row[1][:, n * BANK:(n + 1) * BANK], bank(5 + n, BANK, 0, REST), ACT.Copy,
                                       scale=weight[1][:, bass.ds(e, 1)]).then_inc(S["ex_rb"], 1)
                for t in range(NT):
                    act.wait_ge(xin_lds[t], 32)
                    act.activation(fin_sq[:, :], fin[t][:, :], ACT.Square, accum_out=fin_s[:, 0, t:t + 1]).then_inc(S["fin_q"], 1)
                    act.wait_ge(S["fin_q"], t + 1)
                    act.activation(fin_s[:, 1, t:t + 1], fin_s[:, 0, t:t + 1], ACT.Sqrt, scale=1.0 / D, bias=eps[:, :]).then_inc(S["fin_sd"], 1)

            @block.vector
            def _(dve):
                for n in ("aa_max", "aa_y", "mg_ma", "mg_mb", "ex_ra"):
                    dve.sem_inc(S[n], CREDIT)
                for n in ("ex_h", "w2_x"):
                    dve.sem_inc(S[n], 2 * CREDIT)
                dve.wait_ge(S["keep_st"], 48)
                dve.memset(kmeta[:, :], 0.0).then_inc(S["as_init"], 1)
                dve.wait_ge(S["as_init"], 2)
                with dve.Fori(0, HEADS) as h:
                    for k in range(2):
                        half, other = slice(k * HD, (k + 1) * HD), slice((1 - k) * HD, (2 - k) * HD)
                        dve.wait_ge(S["aa_qh"], 2 * h + k + 1)
                        dve.tensor_tensor(q_parts[k][other, :], qTa[half, :], q_parts[k][half, :], ALU.subtract).then_inc(S["aa_ql"], 1)
                    dve.wait_ge(S["aa_k"], h + 1)
                    dve.tensor_copy(thirds(kTa[:, :]), banks(3, 3, CH)).then_inc(S["aa_ks"], 1)
                    dve.wait_ge(S["aa_ks"], 7 * h + 1)
                    for k in range(2):
                        half = slice(k * HD, (k + 1) * HD)
                        dve.tensor_copy(kmeta[half, k * META:(k + 1) * META], kTa[half, T1:T2]).then_inc(S["aa_ks"], 1)
                    for k in range(2):
                        for n in range(2):
                            half = slice(k * HD, (k + 1) * HD)
                            if n == 0:
                                dve.wait_ge(S["aa_kh"], 4 * h + 2 * k + 1)
                            dve.tensor_tensor(k_rest[k][n * HD:(n + 1) * HD, :], kTa[half, :], k_lead[k][half, :], ALU.subtract).then_inc(S["aa_ks"], 1)
                    dve.wait_ge(S["aa_bias"], h + 1)

                    dve.wait_ge(S["aa_mt"], h + 1)
                    for m, tiles in ((P, slice(0, NT)), (META, slice(NT, NT + 1))):
                        n = tiles.stop - tiles.start
                        dve.tensor_scalar(meta_a[0:m, tiles, :, :].rearrange("p t k n -> p (t k n)"), bank(4, n * 2 * META, tiles.start * 2 * META, m), -1.0, None,
                                          ALU.mult).then_inc(S["aa_ms"], 1)
                    dve.wait_ge(S["aa_ms"], 4 * h + 2)
                    for m, tiles in ((P, slice(0, NT)), (META, slice(NT, NT + 1))):
                        dve.tensor_reduce(low_a[0:m, tiles, :].rearrange("p t k -> p (t k)"), meta_a[0:m, tiles, :, :].rearrange("p t k n -> p (t k) n"), AX,
                                          ALU.min).then_inc(S["aa_ms"], 1)
                    dve.wait_ge(S["aa_ms"], 4 * h + 4)

                    def scores(t, k):
                        m = P if t < NT else META
                        low = small[0:m, 8 + 2 * (t % 2) + k:9 + 2 * (t % 2) + k]
                        bias = biasH[:, T1 - P - t * P:2 * T1 - P - t * P] if t < NT else zero[0:m, :].broadcast_to([m, T1])
                        if t >= 2 and k == 0:
                            dve.wait_ge(S["aa_t"], 9 * h + t - 1)
                        if k == 0:
                            dve.tensor_copy(EA[t % 2][0][0:m, T1:T2], meta_a[0:m, t, 0, :])
                            dve.tensor_copy(EA[t % 2][1][0:m, T1:T2], meta_a[0:m, t, 1, :])
                        dve.wait_ge(S["aa_s"], 18 * h + 2 * t + k + 1)
                        seen(dve)
                        dve.tensor_tensor_reduce(EA[t % 2][k][0:m, 0:T1], wide(2 * k, T1, m), bias, -1.0, low_a[0:m, t, k:k + 1], ALU.add, ALU.min,
                                                 low).then_inc(S["aa_max"], 1)

                    def columns(t):
                        m = P if t < NT else META
                        den = [small[0:m, 12 + 2 * (t % 2) + k:13 + 2 * (t % 2) + k] for k in range(2)]
                        return den, small[0:m, 40 + t % 2:41 + t % 2], small[0:m, 42 + t % 2:43 + t % 2], small[0:m, 20 + t % 3:21 + t % 3]

                    def sums(t):
                        den, r2, c2, r1 = columns(t)
                        if t >= 3:
                            dve.wait_ge(S["aa_y"], 9 * h + t - 2 + CREDIT)
                        dve.wait_ge(S["aa_e"], 18 * h + 2 * t + 2)
                        dve.reciprocal(r2, den[1]).then_inc(S["aa_sm"], 1)
                        dve.reciprocal(r1, den[0]).then_inc(S["aa_sm"], 1)

                    def combine(t):
                        m = P if t < NT else META
                        den, r2, c2, r1 = columns(t)
                        dve.wait_ge(S["aa_sm"], 27 * h + 3 * t + 2)
                        dve.tensor_scalar(c2, den[0], r2, lam_sm[0:m, 4:5], ALU.mult, ALU.mult).then_inc(S["aa_sm"], 1)
                        dve.wait_ge(S["aa_sm"], 27 * h + 3 * t + 3)
                        dve.scalar_tensor_tensor(EA[t % 2][0][0:m, :], EA[t % 2][1][0:m, :], c2, EA[t % 2][0][0:m, :], ALU.mult, ALU.add).then_inc(S["aa_c"], 1)

                    scores(0, 0)
                    scores(0, 1)
                    for t in range(NT + 1):
                        if t < NT:
                            scores(t + 1, 0)
                        sums(t)
                        combine(t)
                        if t < NT:
                            scores(t + 1, 1)
                dve.wait_ge(S["as_sd"], 1)
                dve.reciprocal(ss2[:, :, :], rs2[:, :, :]).then_inc(S["as_r"], 1)
                dve.wait_ge(S["as_r"], 1)
                for t in range(NT + 1):
                    m = P if t < NT else META
                    o3 = o_tok[0:m, t, :].rearrange("p (h n) -> p h n", n=P)
                    dve.tensor_tensor(o3, o3, ss2[0:m, t, :].unsqueeze(2).broadcast_to([m, HEADS, P]), ALU.mult).then_inc(S["as_n"], 1)
                dve.wait_ge(S["rope_ld"], 32)
                for g in range(KV):
                    z0 = g * (GROUP + 1)
                    for n in range(GROUP + 1):
                        i = z0 + n
                        dst = q_grp[:, n - 1, :] if n else kTb[:, :]
                        dve.wait_ge(S["ob_raw"], i + 1)
                        if i:
                            dve.wait_ge(S["ob_q"], i)
                        if g and n == 0:
                            dve.wait_ge(S["bb_t"], g * GROUP * (NT + 1))
                        dve.tensor_tensor(sq[1][:, 0:T2], acc[:, 0:T2], cos[:, :], ALU.mult).then_inc(S["ob_m"], 1)
                        dve.wait_ge(S["ob_sd"], 2 * i + 2)
                        dve.reciprocal(rs[:, 0:T2], sd[:, 0:T2]).then_inc(S["ob_r"], 1)
                        dve.wait_ge(S["ob_sw"], i + 1)
                        for k in range(3):
                            w = min(CH, T2 - k * CH)
                            c = slice(k * CH, k * CH + w)
                            if i and k == 0:
                                dve.wait_ge(S["ob_m3"], i)
                            ins = dve.tensor_tensor(swapped[:, c], bank(3 * (n % 2) + k, w), sin[:, c], ALU.mult)
                            ins.then_inc(S["ob_m2"], 1)
                        dve.wait_ge(S["ob_m2"], 3 * i + 3)
                        dve.wait_ge(S["ob_m"], i + 1)
                        dve.tensor_tensor(swapped[:, :], swapped[:, :], sq[1][:, 0:T2], ALU.add).then_inc(S["ob_m3"], 1)
                        dve.wait_ge(S["ob_m3"], i + 1)
                        dve.wait_ge(S["ob_r"], i + 1)
                        dve.tensor_tensor(dst, swapped[:, :], rs[:, 0:T2], ALU.mult).then_inc(S["ob_q"], 1)
                    with dve.Fori(0, GROUP) as j:
                        def head(j):
                            return (g * GROUP + j) * 9

                        n_head = g * GROUP + j
                        dve.wait_ge(S["bb_mt"], n_head + 1)
                        for m, tiles in ((P, slice(0, NT)), (META, slice(NT, NT + 1))):
                            n = tiles.stop - tiles.start
                            dve.tensor_scalar(meta_b[0:m, tiles, :].rearrange("p t n -> p (t n)"), bank(4, n * META, tiles.start * META, m), -1.0, None,
                                              ALU.mult).then_inc(S["bb_ms"], 1)
                        dve.wait_ge(S["bb_ms"], 4 * n_head + 2)
                        for m, tiles in ((P, slice(0, NT)), (META, slice(NT, NT + 1))):
                            dve.tensor_reduce(low_b[0:m, tiles], meta_b[0:m, tiles, :], AX, ALU.min).then_inc(S["bb_ms"], 1)
                        dve.wait_ge(S["bb_ms"], 4 * n_head + 4)

                        def scores(t):
                            m = P if t < NT else META
                            e = EB[t % 2]
                            if t >= 2:
                                dve.wait_ge(S["bb_t"], head(j) + t - 1)
                            dve.tensor_copy(e[0:m, T1:T2], meta_b[0:m, t, :])
                            dve.wait_ge(S["bb_s"], head(j) + t + 1 + CREDIT)
                            seen(dve)
                            dve.tensor_tensor_reduce(e[0:m, 0:T1], wide(2 * (t % 2), T1, m), zero[0:m, :].broadcast_to([m, T1]), -1.0, low_b[0:m, t:t + 1], ALU.add, ALU.min,
                                                     small[0:m, 24 + t % 2:25 + t % 2]).then_inc(S["bb_max"], 1)

                        def divide(t):
                            m = P if t < NT else META
                            r = small[0:m, 30 + t % 2:31 + t % 2]
                            dve.wait_ge(S["bb_e"], head(j) + t + 1)
                            dve.reciprocal(r, small[0:m, 26 + t % 2:27 + t % 2]).then_inc(S["bb_rd"], 1)
                            dve.wait_ge(S["bb_rd"], head(j) + t + 1)
                            dve.tensor_scalar(EB[t % 2][0:m, :], EB[t % 2][0:m, :], r, None, ALU.mult).then_inc(S["bb_p"], 1)

                        def result(t):
                            m = P if t < NT else META
                            dve.wait_ge(S["bb_o"], head(j) + t + 1)
                            dve.tensor_copy(obT[:, bass.ds(g * GROUP + j, 1), t * P:t * P + m].rearrange("p a n -> p (a n)"), bank(7, m)).then_inc(S["bb_ob"], 1)

                        scores(0)
                        for t in range(NT + 1):
                            if t < NT:
                                scores(t + 1)
                            divide(t)
                            if t >= 1:
                                result(t - 1)
                        result(NT)
                dve.memset(oaT[:, :, T2:TP], 0.0).then_inc(S["pad_set"], 1)
                dve.memset(obT[:, :, T2:TP], 0.0).then_inc(S["pad_set"], 1)
                with dve.Fori(0, KD) as d:
                    m = mergedT[:, bass.ds(d, 1), :].rearrange("p a (n w) -> p (a n) w", w=CH)
                    dve.wait_ge(S["mg_sa"], d + 1)
                    dve.wait_ge(S["mg_ya"], d + 1)
                    dve.tensor_tensor(m, thirds(sq[0][:, :]), banks(3, 3, CH), ALU.mult).then_inc(S["mg_ma"], 1)
                    dve.wait_ge(S["mg_sb"], d + 1)
                    dve.wait_ge(S["mg_yb"], d + 1)
                    dve.tensor_tensor(thirds(acc[:, :]), thirds(sq[1][:, :]), banks(3, 3, CH), ALU.mult).then_inc(S["mg_mb"], 1)
                    dve.wait_ge(S["mg_mb"], d + 1 + CREDIT)
                    dve.wait_ge(S["mg_ma"], d + 1 + CREDIT)
                    dve.tensor_tensor(m, m, thirds(acc[:, :]), ALU.add).then_inc(S["mg_tmp"], 1)
                dve.wait_ge(S["keep_ld"], 48)
                with dve.Fori(0, KD // 2) as i:
                    for j in range(2):
                        dve.wait_ge(S["w2_z"], 2 * i + j + 1)
                        residual(dve, 2 * i + j, 3 * j, 3, CH, "w2_x", None)
                dve.wait_ge(S["w2_x"], KD + 2 * CREDIT)
                norm_apply(dve, 3, TP, xT, uT)
                dve.memset(aff[:, :, :], 0.0).then_inc(S["router_step"], 1)
                dve.wait_ge(S["router_step"], 1)
                dve.wait_ge(S["lg_z"], 1)
                dve.tensor_copy(aff[:, 0:NT, :], bank(0, NT * NE).rearrange("p (t n) -> p t n", n=NE)).then_inc(S["router_step"], 1)
                dve.tensor_copy(aff[0:META, NT, :], bank(0, NE, NT * NE, META)).then_inc(S["router_step"], 1)
                dve.wait_ge(S["router_step"], 3)
                row_max, row_sum = small[:, 32:32 + NT + 1], small[:, 48:48 + NT + 1]
                dve.tensor_reduce(row_max, aff[:, :, :], AX, ALU.max).then_inc(S["router_step"], 1)
                dve.wait_ge(S["router_step"], 4)
                dve.tensor_tensor(aff[:, :, :], aff[:, :, :], row_max.unsqueeze(2).broadcast_to([P, NT + 1, NE]), ALU.subtract).then_inc(S["router_step"], 1)
                dve.wait_ge(S["lg_e"], 1)
                dve.tensor_reduce(row_sum, aff[:, :, :], AX, ALU.add).then_inc(S["router_step"], 1)
                dve.wait_ge(S["router_step"], 6)
                dve.reciprocal(row_max, row_sum).then_inc(S["router_step"], 1)
                dve.wait_ge(S["router_step"], 7)
                dve.tensor_tensor(aff[:, :, :], aff[:, :, :], row_max.unsqueeze(2).broadcast_to([P, NT + 1, NE]), ALU.mult).then_inc(S["router_step"], 1)
                for n in range(2):
                    dve.wait_ge(S["lg_t"], n + 1)
                    dve.tensor_copy(affT[:, META + n * BANK:META + (n + 1) * BANK], bank(n, BANK, 0, NE)).then_inc(S["router_step"], 1)
                dve.wait_ge(S["lg_t"], 3)
                dve.tensor_copy(affT[:, 0:META], bank(4, META, 0, NE)).then_inc(S["router_step"], 1)
                dve.wait_ge(S["router_step"], 11)
                for r in range(ROUNDS):
                    e8 = slice(8 * r, 8 * r + 8)
                    dve.max(best[:, e8], affT[:, :]).then_inc(S["tk_max"], 1)
                    dve.wait_ge(S["tk_max"], r + 1)
                    dve.max_index(where[:, e8], best[:, e8], affT[:, :]).then_inc(S["tk_idx"], 1)
                    if r < ROUNDS - 1:
                        dve.wait_ge(S["tk_idx"], r + 1)
                        dve.match_replace(affT[:, :], best[:, e8], affT[:, :], -1.0).then_inc(S["tk_rep"], 1)
                        dve.wait_ge(S["tk_rep"], r + 1)
                dve.wait_ge(S["tk_idx"], ROUNDS)
                dve.tensor_copy(where_f[:, :], where[:, :]).then_inc(S["tk_f"], 1)
                dve.wait_ge(S["tk_t"], 1)
                for r, rows in enumerate((P, REST)):
                    dve.tensor_copy(pick[r][:, :], bank(0, NE, 2 * r * NE, rows)).then_inc(S["tk_c"], 1)
                    dve.tensor_copy(weight[r][:, :], bank(0, NE, (2 * r + 1) * NE, rows)).then_inc(S["tk_c"], 1)
                dve.wait_ge(S["tk_c"], 4)
                with dve.Fori(0, NE) as e:
                    for n, (c, k) in enumerate(((0, 3), (3, 3), (6, 2))):
                        dve.wait_ge(S["ex_xt"], e * 3 + n + 1)
                        dve.tensor_copy(xsT[:, c:c + k, :], bank(n, k * CAP).rearrange("p (c n) -> p c n", n=CAP)).then_inc(S["ex_xc"], 1)
                    for j in range(EK):
                        dve.wait_ge(S["ex_s"], e * EK + j + 1)
                        dve.wait_ge(S["ex_u"], e * EK + j + 1)
                        dve.tensor_tensor(hidT[:, j, :], silu_e[j % 2][:, :], bank(4 + 2 * (j % 2), CAP), ALU.mult).then_inc(S["ex_h"], 1)
                    for n, (b, c, k) in enumerate(((7, 0, 3), (0, 3, 3), (1, 6, 2))):
                        dve.wait_ge(S["ex_y"], e * 3 + n + 1)
                        dve.tensor_copy(yT[:, c:c + k, :], bank(b, k * CAP).rearrange("p (c n) -> p c n", n=CAP)).then_inc(S["ex_yt"], 1)
                    dve.wait_ge(S["ex_free"], e + CREDIT)
                    for n in range(2):
                        dve.wait_ge(S["ex_r"], e * 2 + n + 1)
                        dve.tensor_scalar(y_row[0][:, n * BANK:(n + 1) * BANK], bank(3 + n), weight[0][:, bass.ds(e, 1)], None, ALU.mult).then_inc(S["ex_ra"], 1)
                dve.wait_ge(S["gfin_ld"], 16)
                for t in range(NT):
                    dve.wait_ge(S["fin_sd"], t + 1)
                    dve.reciprocal(fin_s[:, 2, t:t + 1], fin_s[:, 1, t:t + 1]).then_inc(S["fin_r"], 1)
                    dve.wait_ge(S["fin_r"], t + 1)
                    dve.scalar_tensor_tensor(fin[t][:, :], fin[t][:, :], fin_s[:, 2, t:t + 1], g_fin[:, :], ALU.mult, ALU.mult).then_inc(S["fin_o"], 1)

            @block.tensor
            def _(pe):
                pe.sem_inc(S["bb_s"], CREDIT)
                pe.wait_ge(N["h"], 3 * KD)
                before = [0, 0, 0]
                with pe.Fori(0, HEADS) as h:
                    pe.wait_ge(ring_ld[0], 16 * h + 16 * before[0] + 16)
                    project(ring[0], uT, 0, 3, CH).then_inc(S["aa_q"], 1)
                    pe.wait_ge(ring_ld[1], 16 * h + 16 * before[1] + 16)
                    project(ring[1], uT, 3, 3, CH).then_inc(S["aa_k"], 1)
                    pe.wait_ge(ring_ld[2], 16 * h + 16 * before[2] + 16)
                    for n in range(3):
                        if n == 1:
                            pe.wait_ge(S["aa_y"], 9 * h + CREDIT)
                        if n == 2:
                            pe.wait_ge(S["aa_qs"], h + 1)
                            pe.wait_ge(S["aa_ql"], 2 * h + 2)
                        for t in range(4 * n, min(4 * n + 4, NT + 1)):
                            m = P if t < NT else META
                            for c in range(KD):
                                last = mm(bank(6 + n if n < 2 else 0, P, (t % 4) * P, m), uT[:, c, t * P:t * P + m], ring[2][:, c, :],
                                          start=(c == 0), stop=(c == KD - 1))
                        last.then_inc(S["aa_v"], 1)

                    pe.wait_ge(S["aa_ks"], 7 * h + 3)
                    for t in range(NT + 1):
                        m = P if t < NT else META
                        if m < P:
                            seen(pe)
                        last = mm(bank(4, 2 * META, t * 2 * META, m), qTa[:, t * P:t * P + m], kmeta[:, :], start=True, stop=True)
                    last.then_inc(S["aa_mt"], 1)

                    def scores(t):
                        m = P if t < NT else META
                        if t == 0:
                            pe.wait_ge(S["aa_ks"], 7 * h + 7)
                            pe.wait_ge(S["aa_vs"], 3 * h + 3)
                        for k in range(2):
                            if t:
                                pe.wait_ge(S["aa_max"], 18 * h + 2 * t + k - 1 + CREDIT)
                            if m < P:
                                seen(pe)
                            for keys, part in ((0, k_lead), (1, k_rest)):
                                for b in range(2):
                                    last = mm(bank(2 * k + b, BANK, 0, m), q_parts[k][:, t * P:t * P + m], part[k][:, b * BANK:(b + 1) * BANK],
                                              start=(keys == 0), stop=(keys == 1))
                            last.then_inc(S["aa_s"], 1)

                    def turn_probs(t):
                        m = P if t < NT else META
                        e = EA[t % 2][0]
                        pe.wait_ge(S["aa_c"], 9 * h + t + 1)
                        if m < P:
                            seen(pe)
                        for j in range(NT):
                            turn(bank(5 + j // 4, m, (j % 4) * P), e[0:m, j * P:(j + 1) * P], m)
                        if t >= 1:
                            pe.wait_ge(S["aa_y"], 9 * h + t + CREDIT)
                            if m < P:
                                seen(pe)
                        turn(bank(7, m, 256, META), e[0:m, T1:T2], m).then_inc(S["aa_t"], 1)

                    def values(t):
                        m = P if t < NT else META
                        pe.wait_ge(S["aa_pt"], 9 * h + t + 1)
                        pe.wait_ge(S["aa_pt9"], 9 * h + t + 1)
                        for j in range(NT):
                            mm(bank(7, P, 0, m), PTa[t % 2][:, j, 0:m], Va[:, j, :], start=(j == 0), stop=False)
                        mm(bank(7, P, 0, m), PTa[t % 2][0:META, NT, 0:m], Va[0:META, NT, :], start=False, stop=True).then_inc(S["aa_o"], 1)

                    scores(0)
                    for t in range(NT + 1):
                        if t < NT:
                            scores(t + 1)
                        if t >= 1:
                            values(t - 1)
                        turn_probs(t)
                    values(NT)
                for t in range(NT + 1):
                    m = P if t < NT else META
                    pe.wait_ge(S["as_n"], t + 1)
                    for half in range(2):
                        if t >= 2:
                            pe.wait_ge(S["as_o"], 2 * (t - 2) + half + 1)
                        for c in range(4):
                            last = turn(bank(4 * (t % 2) + half, m, c * P), o_tok[0:m, t, (4 * half + c) * P:(4 * half + c + 1) * P], m)
                        last.then_inc(S["as_t"], 1)
                before = [0, 0, 0]
                pe.wait_ge(S["as_o"], 2 * (NT + 1))
                for g in range(KV):
                    z0 = g * (GROUP + 1)
                    def normed(n):
                        i = z0 + n
                        first = 3 * (n % 2)
                        pe.wait_ge(S["ob_sq"], i + 1)
                        pe.wait_ge(S["ob_raw"], i + 1)
                        for b in range(3):
                            last = mm(bank(first + b, CH), swap[:, :], acc[:, b * CH:(b + 1) * CH], start=True, stop=True)
                        last.then_inc(S["ob_sw"], 1)
                        if n:
                            pe.wait_ge(S["ob_sd"], 2 * i)
                        for b in range(2):
                            mm(bank(6 + b), ones[:, :], sq[0][:, b * BANK:(b + 1) * BANK], start=True, stop=True)
                        mm(bank(first + 2, META, 384), ones[:, :], sq[0][:, T1:T2], start=True, stop=True).then_inc(S["ob_ss"], 1)

                    if g:
                        pe.wait_ge(S["bb_ob"], g * GROUP * (NT + 1))
                    for n in range(GROUP + 1):
                        i = z0 + n
                        if n == 0:
                            pe.wait_ge(ring_ld[4], 16 * (before[1] + g + 1))
                        else:
                            pe.wait_ge(ring_ld[5], 16 * (before[2] + g * GROUP + n))
                        if n >= 2:
                            pe.wait_ge(S["ob_m2"], 3 * (i - 1))
                        project(ring[5 if n else 4], uT, 3 * (n % 2), 3, CH).then_inc(S["ob_z"], 1)
                        if n:
                            normed(n - 1)
                    normed(GROUP)
                    pe.wait_ge(ring_ld[3], 16 * (before[0] + g + 1))
                    pe.wait_ge(S["ob_sd"], 2 * (z0 + GROUP + 1))
                    pe.wait_ge(S["ob_m2"], 3 * (z0 + GROUP))
                    for n in range(3):
                        for t in range(4 * n, min(4 * n + 4, NT + 1)):
                            m = P if t < NT else META
                            for c in range(KD):
                                last = mm(bank(6 + n if n < 2 else 5, P, (t % 4) * P, m), uT[:, c, t * P:t * P + m], ring[3][:, c, :],
                                          start=(c == 0), stop=(c == KD - 1))
                        last.then_inc(S["ob_v"], 1)

                    with pe.Fori(0, GROUP) as j:
                        def head(j):
                            return (g * GROUP + j) * 9

                        pe.wait_ge(S["ob_vs"], 3 * g + 3)
                        pe.wait_ge(S["bb_qs"], g * GROUP + j + 1)
                        pe.wait_ge(S["ob_q"], z0 + GROUP + 1)
                        for t in range(NT + 1):
                            m = P if t < NT else META
                            if m < P:
                                seen(pe)
                            last = mm(bank(4, META, t * META, m), qs[:, t * P:t * P + m], kTb[:, T1:T2], start=True, stop=True)
                        last.then_inc(S["bb_mt"], 1)

                        def scores(t):
                            m = P if t < NT else META
                            if t >= 2:
                                pe.wait_ge(S["bb_max"], head(j) + t - 1)
                            if m < P:
                                seen(pe)
                            for b in range(2):
                                last = mm(bank(2 * (t % 2) + b, BANK, 0, m), qs[:, t * P:t * P + m], kTb[:, b * BANK:(b + 1) * BANK], start=True, stop=True)
                            last.then_inc(S["bb_s"], 1)

                        def turn_probs(t):
                            m = P if t < NT else META
                            pe.wait_ge(S["bb_p"], head(j) + t + 1)
                            if m < P:
                                seen(pe)
                            for i in range(NT):
                                turn(bank(5 + i // 4, m, (i % 4) * P), EB[t % 2][0:m, i * P:(i + 1) * P], m)
                            if t >= 1:
                                pe.wait_ge(S["bb_ob"], head(j) + t)
                                if m < P:
                                    seen(pe)
                            turn(bank(7, m, 256, META), EB[t % 2][0:m, T1:T2], m).then_inc(S["bb_t"], 1)

                        def values(t):
                            m = P if t < NT else META
                            pe.wait_ge(S["bb_pt"], head(j) + t + 1)
                            pe.wait_ge(S["bb_pt9"], head(j) + t + 1)
                            for i in range(NT):
                                mm(bank(7, m), Vb[:, i, :], PTb[t % 2][:, i, 0:m], start=(i == 0), stop=False)
                            mm(bank(7, m), Vb[0:META, NT, :], PTb[t % 2][0:META, NT, 0:m], start=False, stop=True).then_inc(S["bb_o"], 1)

                        scores(0)
                        scores(1)
                        for t in range(NT + 1):
                            if t + 2 <= NT:
                                scores(t + 2)
                            if t >= 1:
                                values(t - 1)
                            turn_probs(t)
                        values(NT)
                before = [HEADS, HEADS, HEADS, KV]
                pe.wait_ge(S["bb_ob"], HEADS * (NT + 1))
                pe.wait_ge(S["pad_set"], 3)
                with pe.Fori(0, KD) as d:
                    for k, (src, z, first, free) in enumerate(((uT, "mg_ga", 0, None), (oaT, "mg_ya", 3, "mg_mb"), (uT, "mg_gb", 0, "mg_sa"), (obT, "mg_yb", 3, "mg_ma"))):
                        pe.wait_ge(ring_ld[k], 16 * d + 16 * before[k] + 16)
                        if k == 0:
                            pe.wait_ge(S["mg_mb"], d + CREDIT)
                        elif k == 1:
                            pe.wait_ge(S["mg_mb"], d + CREDIT)
                        elif k == 2:
                            pe.wait_ge(S["mg_sa"], d + 1)
                        else:
                            pe.wait_ge(S["mg_ma"], d + 1 + CREDIT)
                        project(ring[k], src, first, 3, CH).then_inc(S[z], 1)
                before = [KV, KV * GROUP]
                pe.wait_ge(S["mg_tmp"], KD)
                with pe.Fori(0, KD // 2) as i:
                    for j in range(2):
                        pe.wait_ge(ring_ld[4 + j], 16 * i + 16 * before[j] + 16)
                        pe.wait_ge(S["w2_x"], 2 * i + j - 1 + 2 * CREDIT)
                        project(ring[4 + j], mergedT, 3 * j, 3, CH).then_inc(S["w2_z"], 1)
                norm_sum(pe, 3, 3, CH)
                pe.wait_ge(S["router_ld"], 16)
                pe.wait_ge(N["h"], 4 * KD)
                for t in range(NT + 1):
                    m = P if t < NT else META
                    for c in range(KD):
                        last = mm(bank(0, NE, t * NE, m), uT[:, c, t * P:t * P + m], router[:, c, :], start=(c == 0), stop=(c == KD - 1))
                last.then_inc(S["lg_z"], 1)

                def rows(t):
                    m = P if t < NT else META
                    for src, first, done, free in ((xT, 6, "hr_t", "hr_c"), (uT, 2, "ur_t", "ur_c")):
                        for n in range(2):
                            if t:
                                pe.wait_ge(S[free], 2 * (t - 1) + n + 1)
                            for c in range(4):
                                last = turn(bank(first + n, P, c * P, m), src[:, 4 * n + c, t * P:t * P + m])
                            last.then_inc(S[done], 1)

                for t in range(3):
                    rows(t)
                pe.wait_ge(S["router_step"], 8)
                for t in range(NT + 1):
                    m = P if t < NT else META
                    last = turn(bank(t // 4 if t < NT else 4, m, (t % 4) * P, NE), aff[0:m, t, :], m)
                    if t in (3, 7, 8):
                        last.then_inc(S["lg_t"], 1)
                for t in range(3, NT + 1):
                    rows(t)
                pe.wait_ge(S["tk_f"], 1)
                for r, (c, n) in enumerate(((0, P), (P, REST))):
                    for k, src in enumerate((where_f, best)):
                        last = turn(bank(0, NE, (2 * r + k) * NE, n), src[:, c:c + n], NE)
                last.then_inc(S["tk_t"], 1)
                pe.wait_ge(S["tk_c"], 4)
                pe.wait_ge(S["ur_c"], 2 * (NT + 1))
                pe.wait_ge(S["hr_c"], 2 * (NT + 1))
                with pe.Fori(0, NE) as e:
                    pe.wait_ge(S["ex_xa"], 16 * e + 16)
                    pe.wait_ge(S["ex_xb"], 16 * e + 16)
                    for c in range(KD):
                        turn(bank(c // 3, P, (c % 3) * CAP), xs[0][:, c * P:(c + 1) * P])
                        last = turn(bank(c // 3, REST, (c % 3) * CAP + P), xs[1][:, c * P:(c + 1) * P], REST)
                        if c in (2, 5, 7):
                            last.then_inc(S["ex_xt"], 1)
                    pe.wait_ge(S["ex_xc"], e * 3 + 3)
                    for j in range(EK):
                        if j == 0:
                            pe.wait_ge(S["ex_ra"], e * 2 + CREDIT)
                            pe.wait_ge(S["ex_rb"], e * 2 + CREDIT)
                        if j >= 2:
                            pe.wait_ge(S["ex_h"], e * EK + j - 1 + 2 * CREDIT)
                        for w, b, ld, done in ((w_gate, 3, gate_ld, "ex_g"), (w_up, 4, up_ld, "ex_u")):
                            pe.wait_ge(ld[j], 16 * e + 16)
                            for c in range(KD):
                                last = mm(bank(b + 2 * (j % 2), CAP), w[:, j, c, :], xsT[:, c, :], start=(c == 0), stop=(c == KD - 1))
                            last.then_inc(S[done], 1)
                    pe.wait_ge(S["ex_h"], e * EK + EK + 2 * CREDIT)
                    pe.wait_ge(down_ld, EK * 16 * e + EK * 16)
                    for c in range(KD):
                        b = (7, 0, 1)[c // 3]
                        for j in range(EK):
                            last = mm(bank(b, CAP, (c % 3) * CAP), w_down[:, j, c * P:(c + 1) * P], hidT[:, j, :], start=(j == 0), stop=(j == EK - 1))
                        if c in (2, 5, 7):
                            last.then_inc(S["ex_y"], 1)
                    for n in range(2):
                        pe.wait_ge(S["ex_yt"], e * 3 + 2 + n)
                        for c in range(4):
                            turn(bank(3 + n, P, c * P), yT[:, 4 * n + c, 0:P])
                            last = turn(bank(5 + n, P, c * P, REST), yT[:, 4 * n + c, P:CAP])
                        last.then_inc(S["ex_r"], 1)



def layout(inputs):
    a = {n: np.asarray(v) for n, v in inputs.items()}

    def by_column_tile(w):
        lead, k, n = w.shape[:-2], w.shape[-2], w.shape[-1]
        w = w.reshape(*lead, k // P, P, n // P, P)
        r = len(lead)
        return w.transpose(*range(r), r + 2, r + 1, r, r + 3)

    def by_feature(g):
        return g.reshape(-1, P).T

    vectors = [by_feature(a[n][0]) for n in ("g_mix", "g_ffn", "g_mix_2", "g_ffn_2")]
    vectors += [by_feature(a["conv_w"][0, k]) for k in range(3)]
    vectors += [by_feature(a["g_conv_out"][0]), by_feature(a["g_attn_out"][0])]
    vectors += [np.tile(a[n][0], 2)[:, None] for n in ("g_q", "g_k")]
    vectors += [a[n][0][:, None] for n in ("g_subln_2", "g_qnorm_2", "g_knorm_2")]
    out = {"vectors": np.concatenate(vectors, 1)}
    w_in, w_out, w_gate, w_up = (by_column_tile(a[n][0]) for n in ("w_in", "w_out", "w_gate", "w_up"))
    tiles = [w_in[k * DCT + i] for i in range(DCT) for k in range(6)]
    tiles += list(w_out)
    tiles += [w[i] for i in range(NF) for w in (w_gate, w_up)]
    down = a["w_down"][0].reshape(NF // 2, 2, P, 2, HALF, P).transpose(3, 0, 2, 1, 4, 5).reshape(NF, P, KD, P)
    out["stream"] = np.concatenate([np.stack(tiles), down])
    for n in ("w_in_2", "w_branch_a_2", "w_branch_b_2", "w_out_2", "w_gate_2", "w_up_2"):
        out[n] = by_column_tile(a[n][0])
    for n in ("x", "meta_tokens_2", "lambda_q1_2", "lambda_k1_2", "lambda_q2_2", "lambda_k2_2", "w_router_2", "w_down_2", "g_final_2"):
        out[n] = a[n]
    return {n: np.ascontiguousarray(v) for n, v in (out | host_constants()).items()}


def kernel(**inputs):
    import concourse.bacc as bacc
    from concourse.bass_utils import run_bass_kernel_spmd as run

    nc = bacc.Bacc("TRN2", target_bir_lowering=False, num_devices=1)
    arrays, aps = {}, {}
    for name, a in layout(inputs).items():
        arrays[f"in_{name}"] = a
        aps[name] = nc.dram_tensor(f"in_{name}", a.shape, mybir.dt.from_np(a.dtype), kind="ExternalInput").ap()
    out = nc.dram_tensor("out", (1, T1, D), F32, kind="ExternalOutput").ap()
    build(nc, aps, out)
    r = run(nc, [arrays], core_ids=[0])
    return r.results[0]["out"]
```

```python
from contextlib import ExitStack

import concourse.bass as bass
import numpy as np
from concourse import mybir

F32 = mybir.dt.float32
F32R = mybir.dt.float32r
U32 = mybir.dt.uint32
ALU = mybir.AluOpType
ACT = mybir.ActivationFunctionType
AX = mybir.AxisListType.X

P = 128
D = 1024
KD = D // P
T1 = 1024
META = 16
T2 = T1 + META
CH = 348
TP = 3 * CH
NT = T1 // P
BANK = 512
EPS = 1e-6

DC = 512
DCT = DC // P
HD = 64
FF = 2816
NF = FF // P
HALF = KD // 2
W_OUT0 = 6 * DCT
UP0 = W_OUT0 + KD
DOWN0 = UP0 + 2 * NF
TILES = DOWN0 + NF
HEADS = 8
KV = 2
GROUP = HEADS // KV
HB = 128
QA, KA, VA = 0, HEADS, 2 * HEADS
QB, KB, VB = 3 * HEADS, 4 * HEADS, 4 * HEADS + KV
GA, GB = VB + KV, VB + KV + KD
A0 = TILES
MG0 = A0 + 3 * HEADS
B0 = MG0 + 2 * KD
ITEMS = GROUP + 2
GB0 = B0 + KV * ITEMS
BR0 = GB0 + KD
OUT0 = BR0 + KD
ALL_TILES = OUT0 + KD
TAKEN = [TILES // 2 + 2 * HEADS, TILES // 2 + HEADS]
NE = 16
EF = 512
EK = EF // P
CAP = 2 * T2 // NE
REST = CAP - P
ROUNDS = -(-CAP // 8)
LATE = 2 * NE
LAM_INIT = 0.8 - 0.6 * float(np.exp(-0.3 * 0))
BIG = 3.0e38
MASKED = -1.0e30
CREDIT = 1

NORM_GAINS = [n * KD for n in range(4)]
CONV_W = 4 * KD
G_CONV = CONV_W + 3 * DCT
G_ATTN = G_CONV + DCT
G_Q, G_K, G_SUB, G_QN, G_KN = range(G_ATTN + DCT, G_ATTN + DCT + 5)
GAINS = G_KN + 1


def host_constants():
    eye = np.eye(P, dtype=np.float32)
    ones = np.ones((P, P), np.float32)
    block = np.kron(np.eye(2), np.ones((HD, HD))).astype(np.float32)
    swap = np.zeros((P, P), np.float32)
    for half in (0, 64):
        for i in range(32):
            swap[half + 32 + i, half + i] = -1.0
            swap[half + i, half + 32 + i] = 1.0
    delta = np.arange(P)[:, None] - (np.arange(T1)[None, :] - (T1 - P))
    count = np.zeros(delta.shape, np.float32)
    for window, dil in ((128, 1), (512, 4), (2048, 16)):
        count += (delta >= 0) & (delta % dil == 0) & (delta <= window)
    log_count = np.where(count > 0, np.log(np.maximum(count, 1)), MASKED).astype(np.float32)
    neg_dist = -np.abs(np.arange(P)[:, None] - (np.arange(2 * T1 - P)[None, :] - (T1 - P))).astype(np.float32)
    half = HB // 2
    inv = (np.float32(10000.0) ** (-np.arange(0, half, 2, dtype=np.float32) / np.float32(half))).astype(np.float32)
    tok = np.arange(T1)
    row = np.concatenate([tok // 64, np.zeros(META, int)]).astype(np.float32)
    col = np.concatenate([tok % 64, np.zeros(META, int)]).astype(np.float32)
    ang_r, ang_c = inv[:, None] * row[None], inv[:, None] * col[None]
    ang = np.concatenate([ang_r, ang_r, ang_c, ang_c], 0)
    cos = np.cos(ang).astype(np.float32)
    sin = np.sin(ang).astype(np.float32)
    return {"eye": eye, "ones": ones, "block": block, "swap": swap, "log_count": log_count, "neg_dist": neg_dist,
            "cos": cos, "sin": sin}


def build(nc, A, out):
    ctx = ExitStack()
    with ctx:
        base = [-(-nc.sbuf_base // 64) * 64]

        def at(name, shape, offset, dt=F32):
            return nc.alloc_sbuf_tensor_at(name, shape, dt, offset=offset)

        def size(shape):
            return 4 * int(np.prod(shape[1:]))

        def put(name, shape, dt=F32):
            t = at(name, shape, base[0], dt)
            base[0] += -(-size(shape) // 32) * 32
            return t

        class Overlay:

            def __init__(self, start, end):
                self.at, self.end = start, end

            def put(self, name, shape, dt=F32):
                t = at(name, shape, self.at, dt)
                self.at += -(-size(shape) // 32) * 32
                assert self.at <= self.end, (name, self.at, self.end)
                return t

        def sem(name):
            return ctx.enter_context(nc.semaphore(name))

        eye = put("eye_sb", [P, P])
        ones = put("ones_sb", [P, P])
        block64 = put("block_sb", [P, P])
        swap = put("swap_sb", [P, P])
        gains = put("gains_sb", [P, GAINS])
        g_heads = put("g_heads_sb", [P, 3])
        G_Q8, G_SUBI, G_QNS = range(3)
        lams = put("lams_sb", [P, 4, HD])
        lam_sm = put("lam_small", [P, 8])
        eps = put("eps_sb", [P, 1])
        zero = put("zero_sb", [P, 1])
        small = put("small_sb", [P, 64])
        router = put("router_sb", [P, KD, NE])
        ring0 = base[0]
        ring = [put(f"ring{j}", [P, KD, P]) for j in range(6)]
        w_raw = ring[0:2]
        w_hi = [at(f"w_hi{j}", [P, KD, P], ring0 + (2 + j) * 4096, F32R) for j in range(2)]
        w_lo = [at(f"w_lo{j}", [P, KD, P], ring0 + (4 + j) * 4096, F32R) for j in range(2)]
        uT_at = base[0]
        put("normed", [P, KD, TP])
        sq = [put(f"sq{j}", [P, TP]) for j in range(2)]
        acc = put("acc", [P, TP])
        sd = put("sd", [P, TP])
        rs = put("rs", [P, TP])
        xT_at = base[0]
        xT = put("xT", [P, KD, TP])
        scratch = base[0]
        top = nc.sbuf_usable_end
        yT_at = (top - 4 * KD * TP) // 32 * 32

        u_hi = at("u_hi", [P, KD, T1], uT_at, F32R)
        u_lo = at("u_lo", [P, KD, T1], yT_at, F32R)
        o = Overlay(scratch, yT_at)
        x_in = o.put("x_in", [P, NT, D])
        meta_in = o.put("meta_in", [META, D])
        o = Overlay(xT_at, yT_at)
        qT1 = o.put("qT1", [P, T1])
        kT1 = o.put("kT1", [P, T1])
        V1 = o.put("V1", [P, NT, P])
        E1 = [o.put(f"E1_{j}", [P, T1]) for j in range(4)]
        PT1 = [o.put(f"PT1_{j}", [P, 4, P]) for j in range(4)]
        convT = o.put("convT", [P, DCT, T1])
        y_tok = o.put("y_tok", [P, NT, DC])
        u_sb = o.put("u_sb", [P, T1])
        gated = o.put("gated", [P, 2 + T1])
        conv_acc = o.put("conv_acc", [P, T1])
        conv_sq = o.put("conv_sq", [P, T1])
        ss1 = o.put("ss1", [P, 2 * NT])
        bias1 = o.put("bias1", [P, T1])
        vT1 = u_sb
        hid = at("hid", [P, NF, T1], xT_at)
        assert xT_at + 4 * NF * T1 <= yT_at
        hid_hi = [at(f"hid_hi{j}", [P, T1], uT_at + j * 8192, F32R) for j in range(4)]
        hid_lo = [at(f"hid_lo{j}", [P, T1], uT_at + j * 8192 + 4096, F32R) for j in range(4)]
        silu1 = sq
        x2T = at("x2T", [P, KD, TP], yT_at)

        whole = 4 * KD * TP
        u2_hi = at("u2_hi", [P, KD, TP], uT_at, F32R)
        u2_lo = at("u2_lo", [P, KD, TP], uT_at + whole, F32R)
        late_at = uT_at + 2 * whole
        o = Overlay(late_at, top)
        sq2 = [o.put(f"sq2_{j}", [P, TP]) for j in range(2)]
        acc2, sd2, rs_2 = (o.put(n, [P, TP]) for n in ("acc2", "sd2", "rs_2"))
        scratch2 = o.at
        o = Overlay(late_at, scratch2)
        ss2 = o.put("ss2", [P, NT + 1, HEADS])
        junk = o.put("junk", [P, P])
        rs2 = o.put("rs2", [P, NT + 1, HEADS])
        parts_at = o.at
        k_lead = [o.put(f"k_lead{k}", [P, TP], F32R) for k in range(2)]
        k_rest = [o.put(f"k_rest{k}", [P, TP], F32R) for k in range(2)]
        meta_a = o.put("meta_a", [P, NT + 1, 2, META])
        low_a = o.put("low_a", [P, NT + 1, 2])
        tok_at = (top - 4 * (NT + 1) * D) // 32 * 32
        o = Overlay(scratch2, tok_at)
        biasH = o.put("biasH", [P, 2 * T1 - P])
        kmeta = o.put("kmeta", [P, 2 * META])
        qTa = o.put("qTa", [P, TP])
        kTa = o.put("kTa", [P, TP])
        q_parts = [o.put(f"q_parts{k}", [P, TP], F32R) for k in range(2)]
        Va = o.put("Va", [P, NT + 1, P])
        EA = [[o.put(f"EA{j}{m}", [P, T2]) for m in range(2)] for j in range(2)]
        vTa = EA[1][0]
        PTa = [o.put(f"PTa{j}", [P, NT + 1, P]) for j in range(2)]
        o_tok = at("o_tok", [P, NT + 1, D], tok_at)
        o = Overlay(parts_at, tok_at)
        oa_hi = o.put("oa_hi", [P, HEADS, TP], F32R)
        oa_lo = o.put("oa_lo", [P, HEADS, TP], F32R)
        gate_a = [o.put(f"gate_a{j}", [P, TP]) for j in range(2)]
        mergedT = at("mergedT", [P, KD, TP], yT_at)
        o = Overlay(late_at, top)
        obT = o.put("obT", [P, HEADS, TP])
        ob_end = o.at
        raw_b, sq_b, cos_b, sd_b, rs_b = (o.put(n, [P, TP]) for n in ("raw_b", "sq_b", "cos_part", "sd_b", "rs_b"))
        cos = o.put("cos_sb", [P, T2])
        sin = o.put("sin_sb", [P, T2])
        swapped = o.put("swapped", [P, T2])
        kT_at = o.at
        kTb = o.put("kTb", [P, T2])
        Vb = o.put("Vb", [P, NT + 1, HB])
        q_grp = o.put("q_grp", [P, GROUP, T2])
        qs = o.put("qs", [P, T2])
        q_hi = o.put("q_hi", [P, T2], F32R)
        parts_b = o.at
        q_lo = o.put("q_lo", [P, T2], F32R)
        vTb = at("vTb", [P, T2], parts_b)
        k_hi = o.put("k_hi", [P, T2], F32R)
        k_lo = at("k_lo", [P, T2], kT_at, F32R)
        k_meta = o.put("k_meta", [P, META])
        meta_b = o.put("meta_b", [P, NT + 1, META])
        low_b = o.put("low_b", [P, NT + 1])
        PTb1 = o.put("PTb1", [P, NT + 1, P])
        o = Overlay(ob_end, ob_end + 5 * 4 * TP)
        EB = [o.put(f"EB{j}", [P, T2]) for j in range(3)]
        PTb = [o.put("PTb0", [P, NT + 1, P]), PTb1]
        ob_hi = at("ob_hi", [P, HEADS, TP], uT_at, F32R)
        ob_lo = at("ob_lo", [P, HEADS, TP], late_at, F32R)
        gate_b = at("gate_b", [P, KD, TP], ob_end)
        m_hi = at("m_hi", [P, KD, TP], ob_end, F32R)
        m_lo = at("m_lo", [P, KD, TP], yT_at, F32R)
        assert ob_end + whole <= yT_at
        xT2 = at("xT2", [P, KD, TP], uT_at + whole)
        h_row = [at(f"h_row{j}", [P, D], ring0 + j * 4096) for j in range(2)]
        u_row = [at(f"u_row{j}", [P, D], ring0 + 8192 + j * 4096) for j in range(2)]
        o = Overlay(scratch2, top)
        w_gate = o.put("w_gate_sb", [P, EK, KD, P])
        w_up = o.put("w_up_sb", [P, EK, KD, P])
        w_down = o.put("w_down_sb", [P, EK, D])
        xs = [o.put("xs_a", [P, D]), o.put("xs_b", [REST, D])]
        xsT = o.put("xsT", [P, KD, CAP])
        hidT = o.put("hidT", [P, EK, CAP])
        silu_e = [o.put(f"silu_e{j}", [P, CAP]) for j in range(2)]
        yT = o.put("yT", [P, KD, CAP])
        y_row = [o.put("y_row_a", [P, D]), o.put("y_row_b", [REST, D])]
        aff = o.put("aff", [P, NT + 1, LATE + NE])
        affT = o.put("affT", [LATE + NE, T2 // 2])
        logT = o.put("logT", [NE, TP])
        best = o.put("best", [LATE + NE, 8 * ROUNDS])
        where = o.put("where", [LATE + NE, 8 * ROUNDS], U32)
        where_f = o.put("where_f", [LATE + NE, 8 * ROUNDS])
        late_best = o.put("late_best", [NE, CAP])
        late_where = o.put("late_where", [NE, CAP])
        earlier = o.put("earlier", [NE, CAP])
        top_best = o.put("top_best", [NE, CAP])
        top_where = o.put("top_where", [NE, CAP])
        pick = [o.put("pick_a", [P, NE], U32), o.put("pick_b", [REST, NE], U32)]
        pick_g = [o.put("pick_g_a", [P, 1], U32), o.put("pick_g_b", [REST, 1], U32)]
        pick_s = [o.put("pick_s_a", [P, 1], U32), o.put("pick_s_b", [REST, 1], U32)]
        weight = [o.put("weight_a", [P, NE]), o.put("weight_b", [REST, NE])]
        fin = [at(f"fin{j}", [P, D], xT_at + j * 4096) for j in range(NT)]
        g_fin = at("g_fin", [P, D], uT_at)
        fin_sq = at("fin_sq", [P, D], uT_at + 4096)
        fin_s = at("fin_s", [P, 3, NT], uT_at + 8192)

        PS = ctx.enter_context(nc.psum_tensor("PS", [P, 8, BANK], F32))

        def bank(b, n=BANK, start=0, rows=P):
            return PS[0:rows, b, start:start + n]

        def banks(b, n, width):
            return PS[:, b:b + n, 0:width]

        def wide(b, n, rows=P):
            return PS[0:rows, :, :].rearrange("p b n -> p (b n)")[:, b * BANK:b * BANK + n]

        def thirds(t):
            return t.rearrange("p (n w) -> p n w", w=CH)

        x_keep = nc.dram_tensor("x_keep", (P, KD, TP), F32, kind="Internal").ap()
        m_keep = nc.dram_tensor("m_keep", (P, KD, TP), F32, kind="Internal").ap()
        h_rows = nc.dram_tensor("h_rows", (T2, D), F32, kind="Internal").ap()
        u_rows = nc.dram_tensor("u_rows", (T2, D), F32, kind="Internal").ap()

        lasting = """seen eye_ld const_ld gain_ld lam_ld eps_set pad_set gain_set lam_dot lam_exp lam_done dist_ld
            keep_st keep_ld as_init w_ld0 w_ld1 w_rounded w_split w_used""".split()
        first_block = """meta_ld bias_ld x_t x_sq x_act x_dve n_hi n_lo n_lo_odd
            conv_u conv_a conv_k conv_y mix_sq mix_acc cn_sum cn_sd cn_r cn_n cn_hi cn_lo
            a1_sq a1_ss a1_sd a1_r a1_qn a1_vf a1_vt a1_vs a1_s a1_max a1_e a1_t a1_pt_d a1_pt_a a1_o a1_y a1_rd
            a1_ysq a1_ysd a1_yr a1_yn a1_yt a1_hi a1_lo wo_x up_s up_h hid_hi hid_lo dn_z dn_x""".split()
        second_block = """router_ld router_set
            aa_bias aa_v aa_vf aa_qs aa_qh aa_ql aa_kh aa_ks aa_vs aa_s aa_mt aa_ms aa_max aa_e aa_sm aa_c
            aa_t aa_pt aa_o aa_y aa_ssq as_sd as_r as_n as_np as_t as_o as_lo
            rope_ld ob_raw ob_sq ob_ss ob_sd ob_r ob_sw ob_m ob_m2 ob_m3 ob_q ob_v ob_vf ob_vs
            bb_qs bb_kh bb_kl bb_qh bb_ql bb_s bb_mt bb_ms bb_max bb_e bb_rd bb_p bb_t bb_pt bb_o bb_ob
            mg_sa mg_sb mg_ma mg_mb mg_tmp mg_hi mg_lo br_hi br_lo m_st m_ld w2_x
            lg_z lg_c lg_y router_step lg_e lg_t hr_t hr_c tk_step tk_t tk_c
            ex_pick_g ex_pick_s ex_xa ex_xb ex_xt ex_xc ex_g ex_u ex_s ex_h ex_y ex_yt ex_r ex_ra ex_rb
            ex_add_a ex_add_b ex_free gfin_ld fin_q fin_sd fin_r fin_o fin_st""".split()
        S = {n: sem(n) for n in lasting}
        first_sems = {n: nc.alloc_semaphore(name=n) for n in first_block}
        S.update(first_sems)
        xin_lds = [sem(f"xin_ld{j}") for j in range(NT)]
        N = {s: sem(f"norm_{s}") for s in ("sq", "acc", "ss", "sd", "r", "h")}

        bufs = [(None, None, sd, rs, [*sq, acc]), (sq, acc, sd, rs, [*sq, acc]), (sq, acc, sd2, rs_2, [*sq2, acc2]), (sq2, acc2, sd2, rs_2, None)]
        pieces = [1, 1, 2, 2]

        def pieces_upto(k):
            return sum(pieces[:k + 1])

        def tiles_of(k):
            return [(slice(0, NT), P), (slice(NT, NT + 1), TP - T1)][:pieces[k]]

        def square_chunk(act, k, c, slot, x, width):
            act.wait_ge(N["acc"], (k - 1) * (KD + 1) + c + CREDIT)
            seen(act)
            act.activation(bufs[k][0][slot][:, 0:width], x, ACT.Square).then_inc(N["sq"], 1)

        def no_squares(dve, k, width):
            dve.memset(bufs[k][1][:, 0:width], 0.0).then_inc(N["acc"], 1)

        def add_square(dve, k, c, slot, width):
            acc = bufs[k][1][:, 0:width]
            dve.wait_ge(N["sq"], (k - 1) * KD + c + 1)
            dve.wait_ge(N["acc"], (k - 1) * (KD + 1) + c + 1 + CREDIT)
            dve.tensor_tensor(acc, acc, bufs[k][0][slot][:, 0:width], ALU.add).then_inc(N["acc"], 1)

        def head_norm(engine, t):
            m = P if t < NT else META
            o3 = o_tok[0:m, t, :].rearrange("p (h n) -> p h n", n=P)
            return engine.tensor_tensor(o3, o3, ss2[0:m, t, :].unsqueeze(2).broadcast_to([m, HEADS, P]), ALU.mult)

        def token_sums(acc, k, first=0):
            for tiles, m in tiles_of(k):
                for t in range(tiles.start, tiles.stop):
                    last = mm(bank(first, 1, t, m), acc[:, t * P:t * P + m], ones[:, 0:1], start=True, stop=True)
            return last

        def norm_sum(pe, k):
            pe.wait_ge(N["acc"], k * (KD + 1) + CREDIT)
            token_sums(bufs[k][1], k, 6).then_inc(N["ss"], 1)

        def norm_root(act, k):
            act.wait_ge(N["ss"], 2 * k)
            for tiles, m in tiles_of(k):
                act.activation(bufs[k][3][0:m, tiles], bank(6, tiles.stop - tiles.start, tiles.start, m), ACT.Sqrt, scale=1.0 / D, bias=eps[0:m, :]).then_inc(N["sd"], 1)

        def diagonals(dve, diag, recip, whole):
            tiles, m = whole
            n = tiles.stop - tiles.start
            return dve.tensor_tensor(diag[0:m, tiles.start * P:tiles.start * P + n * m].rearrange("p (t n) -> p t n", n=m),
                                     eye[0:m, 0:m].unsqueeze(1).broadcast_to([m, n, m]), recip[0:m, tiles].unsqueeze(2).broadcast_to([m, n, m]), ALU.mult)

        def by_token(k):
            return bufs[k][3][:, 16:32]

        def norm_recip(dve, k):
            dve.wait_ge(N["sd"], pieces_upto(k))
            for tiles, m in tiles_of(k):
                dve.reciprocal(by_token(k)[0:m, tiles], bufs[k][3][0:m, tiles]).then_inc(N["r"], 1)
            dve.wait_ge(N["r"], 2 * pieces_upto(k) - pieces[k])

        def norm_total(dve, k):
            norm_recip(dve, k)
            for whole in tiles_of(k):
                diagonals(dve, bufs[k][2], by_token(k), whole).then_inc(N["r"], 1)
            dve.wait_ge(N["ss"], 2 * k + 1)

        def spread(diag, k, first):
            for b in range(2):
                last = mm(bank(first + b), ones[:, :], diag[:, b * BANK:(b + 1) * BANK], start=True, stop=True)
            if pieces[k] > 1:
                m = TP - T1
                last = mm(bank(first + 2, m), ones[0:m, :], diag[0:m, T1:TP], start=True, stop=True)
            return last

        def norm_spread(pe, k):
            pe.wait_ge(N["r"], 2 * pieces_upto(k))
            spread(bufs[k][2], k, 8 - pieces[k] - 1).then_inc(N["ss"], 1)

        def normed(dve, k, dst, src, c, width):
            return dve.scalar_tensor_tensor(dst, src[:, c, 0:width], gains[:, NORM_GAINS[k] + c:NORM_GAINS[k] + c + 1], wide(8 - pieces[k] - 1, width),
                                            ALU.mult, ALU.mult)

        def lower(engine, k, c, width, hi, lo):
            engine.wait_ge(S["n_hi"], k * KD + c + 1)
            engine.tensor_tensor(lo[:, c, 0:width], bufs[k][4][c % 3][:, 0:width], hi[:, c, 0:width], ALU.subtract).then_inc(S["n_lo_odd" if c % 2 else "n_lo"], 1)

        def wait_lower(engine, k, c):
            engine.wait_ge(S["n_lo_odd" if c % 2 else "n_lo"], k * (KD // 2) + c // 2 + 1)

        def norm_split(dve, k, src, width, hi, lo):
            norm_total(dve, k)
            for c in range(KD + 1):
                if c < KD:
                    if c >= 3:
                        wait_lower(dve, k, c - 3)
                    normed(dve, k, bufs[k][4][c % 3][:, 0:width], src, c, width).then_inc(N["h"], 1)
                if c % 2:
                    lower(dve, k, c - 1, width, hi, lo)

        def norm_split_odd(pool, k, width, hi, lo):
            for c in range(1, KD, 2):
                lower(pool, k, c, width, hi, lo)

        def norm_round(act, k, width, hi):
            for c in range(KD):
                act.wait_ge(N["h"], k * KD + c + 1)
                act.activation(hi[:, c, 0:width], bufs[k][4][c % 3][:, 0:width], ACT.Copy).then_inc(S["n_hi"], 1)

        def seen(engine):
            engine.sem_inc(S["seen"], 1)

        mm = nc.tensor.matmul

        def turn(out, in_, k=P):
            return nc.tensor.transpose(out, in_, eye[0:k, 0:k])

        def project_split(pe, j, n, to, width, hi, lo, ready=None):
            pe.wait_ge(S["w_split"], n + 1)
            for c in range(KD):
                if ready is not None:
                    ready(c)
                for k, (w, src) in enumerate(((w_hi, hi), (w_hi, lo), (w_lo, hi))):
                    for b, to_bank in enumerate(to):
                        last = mm(bank(to_bank, width), w[j][:, c, :], src[:, c, b * width:(b + 1) * width], start=(c == 0 and k == 0),
                                  stop=(c == KD - 1 and k == 2))
            return last.then_inc(S["w_used"], 1)

        def pair(first):
            return (first, first + 1), BANK, u_hi, u_lo

        def triple(first):
            return (first, first + 1, first + 2), CH, u2_hi, u2_lo

        def tile(n):
            return A["stream"][bass.ds(n, 1)].rearrange("a p c n -> p (a c) n")

        def load(sp, n, j):
            sp.dma_start(w_raw[j][:, :, :], tile(n)).then_inc(S[f"w_ld{j}"], 16)

        def split(pool, n, j, loads, used):
            pool.wait_ge(S[f"w_ld{j}"], 16 * loads)
            pool.wait_ge(S["w_used"], tile_done(used))
            seen(pool)
            pool.tensor_copy(w_hi[j][:, :, :], w_raw[j][:, :, :]).then_inc(S["w_rounded"], 1)
            pool.wait_ge(S["w_rounded"], n + 1)
            pool.tensor_tensor(w_lo[j][:, :, :], w_raw[j][:, :, :], w_hi[j][:, :, :], ALU.subtract).then_inc(S["w_split"], 1)

        def chunk(res, d, width):
            return res[:, bass.ds(d, 1), 0:width].rearrange("p a n -> p (a n)")

        def residual(dve, res, d, first, n, w, done):
            x = chunk(res, d, n * w).rearrange("p (n w) -> p n w", w=w)
            dve.tensor_tensor(x, x, banks(first, n, w), ALU.add).then_inc(S[done], 1)

        chunks = [(t, kc) for t in range(NT) for kc in range(t // 4 + 1)]
        turns = [(u, kc) for u in range(2 * NT) for kc in range(u // 8 + 1)]
        NS, NU = len(chunks), len(turns)
        last_chunk = {t: chunks.index((t, t // 4)) for t in range(NT)}
        last_turn = {u: turns.index((u, u // 8)) for u in range(2 * NT)}
        ahead = [[] for _ in turns]
        coming = 2
        for step, (u, kc) in enumerate(turns):
            t, upto = u // 2, (u // 2 + 1, u % 2)
            if u % 2 and t + 2 <= 4:
                upto = (t + 2, 0)
            while kc == 0 and coming < NS and chunks[coming] <= upto:
                ahead[step].append(coming)
                coming += 1
        assert coming == NS

        def gate_tile(d):
            return MG0 + 2 * d - 1

        def branch_tile(d):
            return MG0 + 2 * d + 2

        def tile_done(n):
            return n + 1 + 2 * CREDIT

        with nc.Block() as block:
            @block.sync
            def _(sp):
                for t in range(NT):
                    sp.dma_start(x_in[:, t, :], A["x"][0, t * P:(t + 1) * P, :]).then_inc(xin_lds[t], 16)
                    if t == 0:
                        sp.dma_start(eye[:, :], A["eye"]).then_inc(S["eye_ld"], 16)
                sp.dma_start(meta_in[:, :], A["meta_tokens_2"]).then_inc(S["meta_ld"], 16)

                for j in range(2):
                    load(sp, j, j)
                sp.dma_start(ones[:, :], A["ones"]).then_inc(S["const_ld"], 16)
                sp.dma_start(block64[:, :], A["block"]).then_inc(S["const_ld"], 16)
                sp.dma_start(swap[:, :], A["swap"]).then_inc(S["const_ld"], 16)
                with sp.Fori(1, TILES // 2 + 1) as i:
                    for j in range(2):
                        sp.wait_ge(S["w_split"], 2 * i + j - 1)
                        load(sp, 2 * i + j, j)
                sp.wait_ge(S["w_used"], tile_done(TILES - 1))
                sp.dma_start(biasH[:, :], A["neg_dist"]).then_inc(S["dist_ld"], 16)
                sp.wait_ge(S["dn_x"], KD)
                sp.dma_start(x_keep, x2T[:, :, :]).then_inc(S["keep_st"], 16)

            @block.gpsimd
            def _(pool):
                pool.memset(eps[:, :], EPS).then_inc(S["eps_set"], 1)
                pool.memset(zero[:, :], 0.0).then_inc(S["eps_set"], 1)
                pool.memset(xT[:, :, T2:TP], 0.0).then_inc(S["pad_set"], 1)
                def split_pair(i):
                    for j in range(2):
                        split(pool, 2 * i + j, j, i + 1, 2 * i + j - 2)

                split_pair(0)
                norm_split_odd(pool, 0, T1, u_hi, u_lo)
                with pool.Fori(1, UP0 // 2 + 1) as i:
                    split_pair(i)
                norm_split_odd(pool, 1, T1, u_hi, u_lo)
                with pool.Fori(UP0 // 2 + 1, TILES // 2) as i:
                    split_pair(i)
                split(pool, A0, 0, TILES // 2 + 1, A0 - 2)
                norm_split_odd(pool, 2, TP, u2_hi, u2_lo)

            @block.scalar
            def _(act):
                act.dma_start(gains[:, :], A["vectors"]).then_inc(S["gain_ld"], 16)
                for n, g in enumerate(("lambda_q1_2", "lambda_k1_2", "lambda_q2_2", "lambda_k2_2")):
                    act.dma_start(lams[:, n, :], A[g].broadcast_to([P, HD])).then_inc(S["lam_ld"], 16)
                act.dma_start(bias1[:, :], A["log_count"]).then_inc(S["bias_ld"], 16)

                act.wait_ge(S["eps_set"], 2)
                for t in range(NT):
                    act.wait_ge(xin_lds[t], 16)
                    act.activation(sq[0][:, 0:D], x_in[:, t, :], ACT.Square, accum_out=rs[:, 32 + t:33 + t]).then_inc(S["x_sq"], 1)
                    act.wait_ge(S["x_sq"], t + 1)
                    act.wait_ge(S["x_t"], 2 * t + 2)
                    act.activation(xT[:, 4:8, t * P:(t + 1) * P], bank(2 * (t % 4) + 1).rearrange("p (c n) -> p c n", n=P), ACT.Copy).then_inc(S["x_act"], 1)
                act.activation(rs[:, 0:NT], rs[:, 32:32 + NT], ACT.Sqrt, scale=1.0 / D, bias=eps[:, :]).then_inc(N["sd"], 1)
                act.wait_ge(S["x_t"], 2 * NT + 2)
                act.activation(xT[:, 4:8, T1:T2], bank(1, 4 * META).rearrange("p (c n) -> p c n", n=META), ACT.Copy).then_inc(S["x_act"], 1)
                act.wait_ge(S["x_act"], NT + 1)
                act.wait_ge(S["x_dve"], NT + 1)
                act.wait_ge(S["pad_set"], 1)
                act.dma_start(x_keep, xT[:, :, :]).then_inc(S["keep_st"], 16)
                norm_round(act, 0, T1, u_hi)
                act.wait_ge(S["keep_st"], 16)
                with act.Fori(0, DCT) as p:
                    act.wait_ge(S["w_used"], tile_done(6 * p))
                    act.activation(u_sb[:, :], wide(0, T1), ACT.Copy).then_inc(S["conv_u"], 1)
                    act.wait_ge(S["conv_y"], p + 1)
                    act.wait_ge(S["mix_acc"], p + 1)
                    act.activation(conv_sq[:, :], convT[:, bass.ds(p, 1), :].rearrange("p a n -> p (a n)"), ACT.Square).then_inc(S["mix_sq"], 1)
                    for n in range(2):
                        act.wait_ge(S["w_used"], tile_done(6 * p + 3 + n))
                        act.activation(sq[n][:, 0:T1], wide(2 * n, T1), ACT.Square).then_inc(S["a1_sq"], 1)
                    for n, buf in ((0, sd), (1, acc)):
                        act.wait_ge(S["a1_ss"], 2 * p + n + 1)
                        act.activation(buf[:, 0:T1], wide(4, T1), ACT.Sqrt, scale=1.0 / HD, bias=eps[:, :]).then_inc(S["a1_sd"], 1)
                    act.wait_ge(S["w_used"], tile_done(6 * p + 5))
                    act.wait_ge(S["conv_a"], p + 1)
                    act.activation(vT1[:, :], wide(6, T1), ACT.Copy).then_inc(S["a1_vf"], 1)
                    for n in range(2):
                        act.wait_ge(S["a1_vt"], 2 * p + n + 1)
                        act.activation(V1[:, 4 * n:4 * n + 4, :], bank(6 + n).rearrange("p (t n) -> p t n", n=P), ACT.Copy).then_inc(S["a1_vs"], 1)

                    def exp(u):
                        nk = (u // 2 + 1) * P
                        act.wait_ge(S["a1_max"], 2 * NS * p + 2 * last_chunk[u // 2] + u % 2 + 1)
                        if u >= 4:
                            act.wait_ge(S["a1_rd"], 16 * p + u - 3)
                        act.activation(E1[u % 4][:, 0:nk], E1[u % 4][:, 0:nk], ACT.Exp, scale=-1.0, bias=small[:, u % 4:u % 4 + 1],
                                       accum_out=small[:, 4 + u % 4:5 + u % 4]).then_inc(S["a1_e"], 1)

                    for u in range(4):
                        exp(u)
                    for step, (u, kc) in enumerate(turns):
                        if step % 2:
                            n = min(u // 2 + 1 - 4 * kc, 4)
                            act.wait_ge(S["a1_t"], NU * p + step + 1)
                            if step >= 4:
                                act.wait_ge(S["a1_o"], NU * p + step - 3)
                            act.activation(PT1[step % 4][:, 0:n, :], bank(4 + step % 3, n * P).rearrange("p (j n) -> p j n", n=P), ACT.Copy).then_inc(S["a1_pt_a"], 1)
                        for s in ahead[step]:
                            t = chunks[s][0]
                            if last_chunk[t] == s:
                                exp(2 * t)
                                exp(2 * t + 1)
                act.wait_ge(S["a1_o"], NU * DCT)
                act.dma_start(xT[:, :, :], x_keep).then_inc(S["keep_ld"], 16)
                act.wait_ge(S["cn_sum"], 1)
                act.activation(rs[:, 0:NT], bank(0, NT), ACT.Sqrt, scale=1.0 / DC, bias=eps[:, :]).then_inc(S["cn_sd"], 1)
                act.wait_ge(S["a1_y"], 16 * DCT + CREDIT)
                for t in range(NT):
                    act.activation(sq[0][:, 0:DC], y_tok[:, t, :], ACT.Square, accum_out=ss1[:, t:t + 1]).then_inc(S["a1_ysq"], 1)
                    act.wait_ge(S["a1_ysq"], t + 1)
                act.activation(ss1[:, NT:2 * NT], ss1[:, 0:NT], ACT.Sqrt, scale=1.0 / DC, bias=eps[:, :]).then_inc(S["a1_ysd"], 1)
                act.wait_ge(S["a1_yr"], 1)
                for t in range(NT):
                    act.activation(y_tok[:, t, :], y_tok[:, t, :], ACT.Copy, scale=ss1[:, t:t + 1]).then_inc(S["a1_yn"], 1)
                for i in range(DCT):
                    act.wait_ge(S["cn_n"], i + 1)
                    act.activation(u_hi[:, i, :], convT[:, i, :], ACT.Copy).then_inc(S["cn_hi"], 1)
                for f in range(DCT):
                    act.wait_ge(S["a1_yt"], f + 1)
                    act.activation(u_hi[:, DCT + f, :], wide(2 + 2 * (f % 2), T1), ACT.Copy, scale=gains[:, G_ATTN + f:G_ATTN + f + 1]).then_inc(S["a1_hi"], 1)
                with act.Fori(0, KD // 4) as i:
                    for j in range(4):
                        act.wait_ge(S["wo_x"], 4 * i + j + 1 + 4 * CREDIT)
                        square_chunk(act, 1, 4 * i + j, j % 2, chunk(xT, 4 * i + j, T1), T1)
                act.dma_start(x_keep, xT[:, :, :]).then_inc(S["keep_st"], 16)
                norm_root(act, 1)
                norm_round(act, 1, T1, u_hi)
                with act.Fori(0, NF // 2) as i:
                    for j in range(2):
                        act.wait_ge(S["w_used"], tile_done(UP0 + 4 * i + 2 * j))
                        act.wait_ge(S["up_h"], 2 * i + j - 1 + 2 * CREDIT)
                        act.activation(silu1[j][:, 0:T1], wide(4 * j, T1), ACT.Silu).then_inc(S["up_s"], 1)
                act.wait_ge(S["w_used"], tile_done(DOWN0 - 1))
                act.dma_start(x2T[:, :, :], x_keep).then_inc(S["keep_ld"], 16)
                act.wait_ge(S["up_h"], NF + 2 * CREDIT)

                def round_tile(m, c):
                    act.wait_ge(S["w_used"], tile_done(DOWN0 + m - 2))
                    for k in range(2):
                        act.activation(hid_hi[2 * slot + k][:, :], hid[:, bass.ds(c + k, 1), :].rearrange("p a n -> p (a n)"), ACT.Copy).then_inc(S["hid_hi"], 1)

                with act.Fori(0, NF // 4) as i:
                    for slot in range(2):
                        round_tile(2 * i + slot, 4 * i + 2 * slot)
                slot = 0
                round_tile(NF // 2 - 1, NF - 2)
                slot = 1
                round_tile(NF // 2, 0)

                def square_half(o):
                    for c in range(o * HALF, (o + 1) * HALF):
                        act.wait_ge(S["dn_x"], c + 1)
                        square_chunk(act, 2, c, c % 2, x2T[:, c, :], TP)

                square_half(0)
                with act.Fori(0, NF // 4) as i:
                    for slot in range(2):
                        round_tile(NF // 2 + 1 + 2 * i + slot, 4 * i + 2 * slot + 2)
                square_half(1)
                norm_root(act, 2)
                norm_round(act, 2, TP, u2_hi)
                act.wait_ge(S["lam_dot"], 2)
                act.activation(lam_sm[:, 2:4], lam_sm[:, 0:2], ACT.Exp).then_inc(S["lam_exp"], 1)

            @block.vector
            def _(dve):
                dve.sem_inc(N["acc"], CREDIT)
                dve.sem_inc(S["a1_y"], CREDIT)
                dve.sem_inc(S["wo_x"], 4 * CREDIT)
                dve.sem_inc(S["up_h"], 2 * CREDIT)
                for t in range(NT):
                    dve.wait_ge(S["x_t"], 2 * t + 1)
                    dve.tensor_copy(xT[:, 0:4, t * P:(t + 1) * P], bank(2 * (t % 4)).rearrange("p (c n) -> p c n", n=P)).then_inc(S["x_dve"], 1)
                dve.wait_ge(S["x_t"], 2 * NT + 1)
                dve.tensor_copy(xT[:, 0:4, T1:T2], bank(0, 4 * META).rearrange("p (c n) -> p c n", n=META)).then_inc(S["x_dve"], 1)
                dve.wait_ge(S["gain_ld"], 16)
                for dst, src, k in ((G_Q8, G_Q, HD ** -0.5), (G_SUBI, G_SUB, 1.0 - LAM_INIT), (G_QNS, G_QN, HB ** -0.5)):
                    dve.tensor_scalar(g_heads[:, dst:dst + 1], gains[:, src:src + 1], float(k), None, ALU.mult).then_inc(S["gain_set"], 1)
                dve.wait_ge(S["x_t"], 2 * NT + 2)
                dve.wait_ge(S["eye_ld"], 16)
                dve.wait_ge(S["x_act"], NT + 1)
                norm_split(dve, 0, xT, T1, u_hi, u_lo)
                for c in range(KD - 2, KD):
                    wait_lower(dve, 0, c)
                dve.wait_ge(S["keep_st"], 16)
                dve.memset(conv_acc[:, :], 0.0).then_inc(S["mix_acc"], 1)
                dve.memset(gated[:, 0:2], 0.0).then_inc(S["conv_k"], 1)
                dve.wait_ge(S["bias_ld"], 16)
                dve.wait_ge(S["gain_set"], 3)
                with dve.Fori(0, DCT) as p:
                    k0 = p * 3 + 1
                    dve.wait_ge(S["w_used"], tile_done(6 * p + 2))
                    dve.wait_ge(S["conv_u"], p + 1)
                    dve.wait_ge(S["conv_k"], k0)
                    dve.tensor_tensor(gated[:, 2:2 + T1], wide(4, T1), u_sb[:, :], ALU.mult).then_inc(S["conv_a"], 1)
                    dve.wait_ge(S["conv_a"], p + 1)
                    conv = convT[:, bass.ds(p, 1), :].rearrange("p a n -> p (a n)")
                    for k in range(3):
                        w = gains[:, bass.ds(CONV_W + (2 - k) * DCT + p, 1)]
                        src = gated[:, 2 - k:2 - k + T1]
                        if k == 0:
                            dve.tensor_scalar(conv, src, w, None, ALU.mult).then_inc(S["conv_k"], 1)
                        else:
                            dve.wait_ge(S["conv_k"], k0 + k)
                            dve.scalar_tensor_tensor(conv, src, w, conv, ALU.mult, ALU.add).then_inc(S["conv_k"], 1)
                    dve.wait_ge(S["conv_k"], k0 + 3)
                    dve.tensor_tensor(conv, wide(2, T1), conv, ALU.mult).then_inc(S["conv_y"], 1)
                    dve.wait_ge(S["mix_sq"], p + 1)
                    dve.wait_ge(S["mix_acc"], p + 1)
                    dve.tensor_tensor(conv_acc[:, :], conv_acc[:, :], conv_sq[:, :], ALU.add).then_inc(S["mix_acc"], 1)
                    for n, (dst, root, gain) in enumerate(((qT1, sd, g_heads[:, G_Q8:G_Q8 + 1]), (kT1, acc, gains[:, G_K:G_K + 1]))):
                        if n:
                            dve.wait_ge(S["a1_qn"], 2 * p + 1)
                        dve.wait_ge(S["a1_sd"], 2 * p + n + 1)
                        dve.reciprocal(rs[:, 0:T1], root[:, 0:T1]).then_inc(S["a1_r"], 1)
                        dve.wait_ge(S["a1_r"], 2 * p + n + 1)
                        dve.scalar_tensor_tensor(dst[:, :], wide(2 * n, T1), gain, rs[:, 0:T1], ALU.mult, ALU.mult).then_inc(S["a1_qn"], 1)

                    def scores(s):
                        t, kc = chunks[s]
                        k0, k1 = kc * BANK, min((kc + 1) * BANK, (t + 1) * P)
                        for a in range(2):
                            u = 2 * t + a
                            part, low = small[:, 20 + u % 4:21 + u % 4], small[:, u % 4:u % 4 + 1]
                            if a == 0:
                                dve.wait_ge(S["a1_s"], NS * p + s + 1)
                            if u >= 4 and kc == 0:
                                dve.wait_ge(S["a1_t"], NU * p + last_turn[u - 4] + 1)
                            if kc:
                                dve.wait_ge(S["a1_max"], 2 * NS * p + 2 * (s - 1) + a + 1)
                            seen(dve)
                            dve.tensor_tensor_reduce(E1[u % 4][:, k0:k1], bank(2 * (s % 2) + a, k1 - k0), bias1[:, T1 - (t + 1) * P + k0:T1 - (t + 1) * P + k1],
                                                     -1.0, part if kc else BIG, ALU.add, ALU.min, low if s == last_chunk[t] else part).then_inc(S["a1_max"], 1)

                    def result(u):
                        dve.wait_ge(S["a1_e"], 16 * p + u + 1)
                        dve.reciprocal(small[:, 16 + u % 4:17 + u % 4], small[:, 4 + u % 4:5 + u % 4]).then_inc(S["a1_rd"], 1)
                        dve.wait_ge(S["a1_rd"], 16 * p + u + 1)
                        dve.wait_ge(S["a1_o"], NU * p + last_turn[u] + 1)
                        dve.tensor_scalar(y_tok[:, u // 2, bass.ds(p * P + (u % 2) * HD, HD)], bank(7, HD), small[:, 16 + u % 4:17 + u % 4],
                                          None, ALU.mult).then_inc(S["a1_y"], 1)

                    scores(0)
                    scores(1)
                    for step in range(NU + 3):
                        if step >= 3 and step - 3 in last_turn.values():
                            result(turns[step - 3][0])
                        if step >= NU:
                            continue
                        u, kc = turns[step]
                        for s in ahead[step]:
                            scores(s)
                        if step % 2 == 0:
                            n = min(u // 2 + 1 - 4 * kc, 4)
                            dve.wait_ge(S["a1_t"], NU * p + step + 1)
                            if step >= 4:
                                dve.wait_ge(S["a1_o"], NU * p + step - 3)
                            dve.tensor_copy(PT1[step % 4][:, 0:n, :], bank(4 + step % 3, n * P).rearrange("p (j n) -> p j n", n=P)).then_inc(S["a1_pt_d"], 1)
                no_squares(dve, 1, T1)
                dve.wait_ge(S["cn_sd"], 1)
                dve.reciprocal(rs[:, 16:16 + NT], rs[:, 0:NT]).then_inc(S["cn_r"], 1)
                dve.wait_ge(S["cn_r"], 1)
                diagonals(dve, sd, rs[:, 16:32], (slice(0, NT), P)).then_inc(S["cn_r"], 1)
                dve.wait_ge(S["a1_ysd"], 1)
                dve.reciprocal(ss1[:, 0:NT], ss1[:, NT:2 * NT]).then_inc(S["a1_yr"], 1)
                dve.wait_ge(S["cn_sum"], 2)
                for i in range(DCT + 1):
                    if i < DCT:
                        dve.scalar_tensor_tensor(convT[:, i, :], convT[:, i, :], gains[:, G_CONV + i:G_CONV + i + 1], wide(6, T1), ALU.mult, ALU.mult).then_inc(S["cn_n"], 1)
                    if i:
                        dve.wait_ge(S["cn_hi"], i)
                        dve.tensor_tensor(u_lo[:, i - 1, :], convT[:, i - 1, :], u_hi[:, i - 1, :], ALU.subtract).then_inc(S["cn_lo"], 1)
                for f in range(DCT):
                    dve.wait_ge(S["a1_hi"], f + 1)
                    dve.scalar_tensor_tensor(u_lo[:, DCT + f, :], wide(2 + 2 * (f % 2), T1), gains[:, G_ATTN + f:G_ATTN + f + 1], u_hi[:, DCT + f, :],
                                             ALU.mult, ALU.subtract).then_inc(S["a1_lo"], 1)
                dve.wait_ge(S["keep_ld"], 16)
                with dve.Fori(0, KD // 4) as i:
                    for j in range(4):
                        dve.wait_ge(S["w_used"], tile_done(W_OUT0 + 4 * i + j))
                        residual(dve, xT, 4 * i + j, 2 * j, 2, BANK, "wo_x")
                        add_square(dve, 1, 4 * i + j, j % 2, T1)
                dve.wait_ge(S["wo_x"], KD + 4 * CREDIT)
                norm_split(dve, 1, xT, T1, u_hi, u_lo)
                dve.wait_ge(S["keep_st"], 32)
                for c in range(KD - 2, KD):
                    wait_lower(dve, 1, c)
                with dve.Fori(0, NF // 2) as i:
                    for j in range(2):
                        dve.wait_ge(S["up_s"], 2 * i + j + 1)
                        dve.wait_ge(S["w_used"], tile_done(UP0 + 4 * i + 2 * j + 1))
                        dve.tensor_tensor(hid[:, bass.ds(2 * i + j, 1), :].rearrange("p a n -> p (a n)"), silu1[j][:, 0:T1], wide(4 * j + 2, T1), ALU.mult).then_inc(S["up_h"], 1)

                def rest_tile(m, c):
                    for k in range(2):
                        dve.wait_ge(S["hid_hi"], 2 * m + k + 1)
                        dve.tensor_tensor(hid_lo[2 * slot + k][:, :], hid[:, bass.ds(c + k, 1), :].rearrange("p a n -> p (a n)"), hid_hi[2 * slot + k][:, :],
                                          ALU.subtract).then_inc(S["hid_lo"], 1)

                def add_half(o):
                    dve.wait_ge(S["keep_ld"], 32)
                    for d in range(HALF):
                        if d < HALF - 1:
                            dve.wait_ge(S["dn_z"], (HALF - 1) * o + d + 1)
                        else:
                            dve.wait_ge(S["w_used"], tile_done(DOWN0 + (o + 1) * (NF // 2) - 1))
                        x = x2T[:, o * HALF + d, 0:T1]
                        dve.tensor_tensor(x, x, wide(2 * d, T1), ALU.add).then_inc(S["dn_x"], 1)
                        if d:
                            add_square(dve, 2, o * HALF + d - 1, (d - 1) % 2, TP)
                    add_square(dve, 2, (o + 1) * HALF - 1, (HALF - 1) % 2, TP)

                with dve.Fori(0, NF // 4) as i:
                    for slot in range(2):
                        rest_tile(2 * i + slot, 4 * i + 2 * slot)
                slot = 0
                rest_tile(NF // 2 - 1, NF - 2)
                slot = 1
                rest_tile(NF // 2, 0)
                no_squares(dve, 2, TP)
                add_half(0)
                with dve.Fori(0, NF // 4) as i:
                    for slot in range(2):
                        rest_tile(NF // 2 + 1 + 2 * i + slot, 4 * i + 2 * slot + 2)
                add_half(1)
                dve.wait_ge(S["dn_x"], KD)
                norm_split(dve, 2, x2T, TP, u2_hi, u2_lo)
                dve.wait_ge(S["lam_ld"], 64)
                for c in range(KD - 2, KD):
                    wait_lower(dve, 2, c)
                for n in range(2):
                    dve.tensor_tensor_reduce(junk[:, n * HD:(n + 1) * HD], lams[:, 2 * n, :], lams[:, 2 * n + 1, :], 1.0, 0.0, ALU.mult, ALU.add,
                                             lam_sm[:, n:n + 1]).then_inc(S["lam_dot"], 1)
                dve.wait_ge(S["lam_exp"], 1)
                dve.tensor_scalar(lam_sm[:, 4:5], lam_sm[:, 3:4], lam_sm[:, 2:3], -LAM_INIT, ALU.subtract, ALU.add).then_inc(S["lam_done"], 1)
                dve.wait_ge(S["lam_done"], 1)
                dve.memset(ss2[:, :, :], 1.0).then_inc(S["as_init"], 1)

            @block.tensor
            def _(pe):
                pe.sem_inc(S["w_used"], 2 * CREDIT)
                pe.wait_ge(S["eye_ld"], 16)
                for t in range(NT):
                    pe.wait_ge(xin_lds[t], 16)
                    for half in range(2):
                        if t >= 4:
                            pe.wait_ge(S["x_act" if half else "x_dve"], t - 3)
                        for c in range(4):
                            last = turn(bank(2 * (t % 4) + half, P, c * P), x_in[:, t, (4 * half + c) * P:(4 * half + c + 1) * P])
                        last.then_inc(S["x_t"], 1)
                pe.wait_ge(S["meta_ld"], 16)
                for half in range(2):
                    pe.wait_ge(S["x_act" if half else "x_dve"], 5)
                    for c in range(4):
                        last = turn(bank(half, META, c * META), meta_in[:, (4 * half + c) * P:(4 * half + c + 1) * P], META)
                    last.then_inc(S["x_t"], 1)
                pe.wait_ge(S["const_ld"], 48)
                pe.wait_ge(S["x_dve"], NT + 1)
                norm_spread(pe, 0)
                with pe.Fori(0, DCT) as p:
                    for j in range(3):
                        project_split(pe, j % 2, 6 * p + j, *pair(2 * j), None if j else lambda c: wait_lower(pe, 0, c))
                    pe.wait_ge(S["conv_u"], p + 1)
                    project_split(pe, 1, 6 * p + 3, *pair(0))
                    pe.wait_ge(S["conv_y"], p + 1)
                    project_split(pe, 0, 6 * p + 4, *pair(2))

                    def head_sums(n):
                        pe.wait_ge(S["a1_sq"], 2 * p + n + 1)
                        if n:
                            pe.wait_ge(S["a1_sd"], 2 * p + 1)
                        for b in range(2):
                            last = mm(bank(4 + b), block64[:, :], sq[n][:, b * BANK:(b + 1) * BANK], start=True, stop=True)
                        last.then_inc(S["a1_ss"], 1)

                    head_sums(0)
                    pe.wait_ge(S["a1_y"], 16 * p + CREDIT)
                    project_split(pe, 1, 6 * p + 5, *pair(6), lambda c: head_sums(1) if c == 2 else None)
                    pe.wait_ge(S["a1_vf"], p + 1)
                    for n in range(2):
                        for t in range(4):
                            last = turn(bank(6 + n, P, t * P), vT1[:, (4 * n + t) * P:(4 * n + t + 1) * P])
                        last.then_inc(S["a1_vt"], 1)

                    def scores(s):
                        t, kc = chunks[s]
                        k0, k1 = kc * BANK, min((kc + 1) * BANK, (t + 1) * P)
                        if s == 0:
                            pe.wait_ge(S["a1_qn"], 2 * p + 2)
                        if s >= 2:
                            pe.wait_ge(S["a1_max"], 2 * NS * p + 2 * (s - 2) + 2)
                        for a in range(2):
                            r = slice(a * HD, (a + 1) * HD)
                            last = mm(bank(2 * (s % 2) + a, k1 - k0), qT1[r, t * P:(t + 1) * P], kT1[r, k0:k1], start=True, stop=True)
                        last.then_inc(S["a1_s"], 1)

                    def taken(step):
                        pe.wait_ge(S["a1_pt_a" if step % 2 else "a1_pt_d"], NU // 2 * p + step // 2 + 1)

                    def turn_probs(step):
                        u, kc = turns[step]
                        if kc == 0:
                            pe.wait_ge(S["a1_e"], 16 * p + u + 1)
                        if step >= 3:
                            taken(step - 3)
                        elif step == 2:
                            pe.wait_ge(S["a1_vs"], 2 * p + 1)
                        for j in range(4 * kc, min(4 * kc + 4, u // 2 + 1)):
                            last = turn(bank(4 + step % 3, P, (j % 4) * P), E1[u % 4][:, j * P:(j + 1) * P])
                        last.then_inc(S["a1_t"], 1)

                    def values(step):
                        u, kc = turns[step]
                        t, a = u // 2, u % 2
                        taken(step)
                        if step == 0:
                            pe.wait_ge(S["a1_vs"], 2 * p + 2)
                        elif kc == 0:
                            pe.wait_ge(S["a1_y"], 16 * p + u + CREDIT)
                        for j in range(4 * kc, min(4 * kc + 4, t + 1)):
                            last = mm(bank(7, HD), PT1[step % 4][:, j % 4, :], V1[:, j, a * HD:(a + 1) * HD], start=(j == 0), stop=(j == t))
                        last.then_inc(S["a1_o"], 1)

                    scores(0)
                    scores(1)
                    for step in range(NU):
                        for s in ahead[step]:
                            scores(s)
                        turn_probs(step)
                        if step >= 2:
                            values(step - 2)
                    values(NU - 2)
                    values(NU - 1)
                pe.wait_ge(S["mix_acc"], DCT + 1)
                token_sums(conv_acc, 1).then_inc(S["cn_sum"], 1)
                pe.wait_ge(S["cn_r"], 2)
                spread(sd, 1, 6).then_inc(S["cn_sum"], 1)
                pe.wait_ge(S["a1_yn"], NT)

                def turn_attention(f):
                    for t in range(NT):
                        last = turn(bank(2 + 2 * (f % 2) + t // 4, P, (t % 4) * P), y_tok[:, t, f * P:(f + 1) * P])
                    last.then_inc(S["a1_yt"], 1)

                for f in range(2):
                    turn_attention(f)

                def ready(c):
                    if c < DCT:
                        pe.wait_ge(S["cn_lo"], c + 1)
                    else:
                        pe.wait_ge(S["a1_lo"], c - DCT + 1)
                    if DCT <= c < DCT + 2:
                        turn_attention(c - DCT + 2)

                pe.wait_ge(S["cn_sd"], 1)
                for j in range(4):
                    project_split(pe, j % 2, W_OUT0 + j, *pair(2 * j), None if j else ready)
                with pe.Fori(1, KD // 4) as i:
                    for j in range(4):
                        pe.wait_ge(S["wo_x"], 4 * i + j - 3 + 4 * CREDIT)
                        project_split(pe, j % 2, W_OUT0 + 4 * i + j, *pair(2 * j))
                norm_sum(pe, 1)
                norm_spread(pe, 1)
                with pe.Fori(0, NF // 2) as i:
                    for j in range(2):
                        pe.wait_ge(S["up_h"], 2 * i + j - 1 + 2 * CREDIT)
                        ready = None if j else lambda c: wait_lower(pe, 1, c)
                        project_split(pe, 0, UP0 + 4 * i + 2 * j, *pair(4 * j), ready)
                        project_split(pe, 1, UP0 + 4 * i + 2 * j + 1, *pair(4 * j + 2))

                def down_tile(m, o, first=False, end=False):
                    pe.wait_ge(S["w_split"], DOWN0 + m + 1)
                    order = [(k, d) for d in range(HALF) for k in range(2)] if end else [(k, d) for k in range(2) for d in range(HALF)]
                    for n, (k, d) in enumerate(order):
                        if n == 0 or (not end and d == 0):
                            pe.wait_ge(S["hid_lo"], 2 * m + k + 1 + (1 if end else 0))
                        if first and o and k == 0:
                            pe.wait_ge(S["dn_x"], d + 1)
                        for q, (w, src) in enumerate(((w_hi, hid_hi), (w_hi, hid_lo), (w_lo, hid_hi))):
                            for b in range(2):
                                last = mm(bank(2 * d + b), w[slot][:, k * HALF + d, :], src[2 * slot + k][:, b * BANK:(b + 1) * BANK],
                                          start=(first and k == 0 and q == 0), stop=(end and k == 1 and q == 2))
                        if end and k == 1 and d < HALF - 1:
                            last.then_inc(S["dn_z"], 1)
                    last.then_inc(S["w_used"], 1)

                pe.wait_ge(S["up_h"], NF + 2 * CREDIT)
                for o in range(2):
                    m0 = o * (NF // 2)
                    slot = m0 % 2
                    down_tile(m0, o, first=True)
                    with pe.Fori(0, NF // 4 - 1) as i:
                        for j in range(2):
                            slot = (m0 + 1 + j) % 2
                            down_tile(m0 + 1 + 2 * i + j, o)
                    slot = (m0 + 1) % 2
                    down_tile(m0 + NF // 2 - 2, o)
                    slot = m0 % 2
                    down_tile(m0 + NF // 2 - 1, o, end=True)
                norm_sum(pe, 2)
                norm_spread(pe, 2)
                project_split(pe, 0, A0, *triple(0), lambda c: wait_lower(pe, 2, c))

        nc.clear_and_free_semaphores(list(first_sems.values()))
        nc.all_engine_barrier()
        S.update({n: sem(n) for n in second_block})
        gate_ld = [sem(f"gate_ld{j}") for j in range(EK)]
        up_ld = [sem(f"up_ld{j}") for j in range(EK)]
        down_ld = sem("down_ld")
        row_st = [sem(f"row_st{j}") for j in range(4)]

        with nc.Block() as block:
            @block.sync
            def _(sp):
                sp.dma_start(router[:, :, :], A["w_router_2"]).then_inc(S["router_ld"], 16)
                with sp.Fori(0, HEADS) as h:
                    n = A0 + 3 * h
                    sp.wait_ge(S["w_split"], n + 1)
                    load(sp, n + 2, 0)
                    sp.wait_ge(S["w_split"], n + 3)
                    load(sp, n + 3, 0)
                    load(sp, n + 4, 1)

                def pairs(first, last, also=None):
                    with sp.Fori((first - MG0) // 2, (last - MG0) // 2) as i:
                        for j in range(2):
                            n = MG0 + 2 * i + j
                            sp.wait_ge(S["w_split"], n - 1)
                            load(sp, n, j)
                            if also:
                                also(n - first)

                pairs(MG0 + 2, B0 + 2)
                sp.wait_ge(S["w_used"], tile_done(B0 - 1))
                sp.dma_start(cos[:, :], A["cos"]).then_inc(S["rope_ld"], 16)
                sp.dma_start(sin[:, :], A["sin"]).then_inc(S["rope_ld"], 16)
                pairs(B0 + 2, GB0 + 4)
                sp.wait_ge(S["bb_ob"], HEADS * (NT + 1))
                sp.wait_ge(S["m_st"], 16)

                def merged(c):
                    sp.dma_start(mergedT[:, bass.ds(c, 1), :], m_keep[:, bass.ds(c, 1), :]).then_inc(S["m_ld"], 16)

                pairs(GB0 + 4, BR0 + 2, merged)
                for c in range(KD - 2, KD):
                    merged(c)
                sp.wait_ge(S["w_used"], tile_done(BR0 - 1))

                def residual_chunk(c):
                    sp.dma_start(xT2[:, bass.ds(c, 1), :], x_keep[:, bass.ds(c, 1), :]).then_inc(S["keep_ld"], 16)

                pairs(BR0 + 2, OUT0 + 2, residual_chunk)
                pairs(OUT0 + 2, ALL_TILES)
                sp.wait_ge(S["w_used"], tile_done(ALL_TILES - 1))
                wg, wu, wd = A["w_gate_2"], A["w_up_2"], A["w_down_2"][0]

                def expert_cols(w, e, j):
                    return w[bass.ds(e, 1), j].rearrange("a p c n -> p (a c) n")

                def expert_rows(w, e, j):
                    return w[bass.ds(e, 1), j * P:(j + 1) * P, :].rearrange("a p n -> p (a n)")

                for j in range(EK):
                    sp.dma_start(w_gate[:, j, :, :], expert_cols(wg, 0, j)).then_inc(gate_ld[j], 16)
                    sp.dma_start(w_up[:, j, :, :], expert_cols(wu, 0, j)).then_inc(up_ld[j], 16)
                for j in range(EK):
                    sp.dma_start(w_down[:, j, :], expert_rows(wd, 0, j)).then_inc(down_ld, 16)
                for t in range(NT + 1):
                    rows = P if t < NT else META
                    r0 = META + t * P if t < NT else 0
                    sp.wait_ge(S["hr_c"], 4 * (t + 1))
                    sp.dma_start(h_rows[r0:r0 + rows, :], h_row[t % 2][0:rows, :]).then_inc(row_st[t % 2], 16)
                    sp.dma_start(u_rows[r0:r0 + rows, :], u_row[t % 2][0:rows, :]).then_inc(row_st[2 + t % 2], 16)
                with sp.Fori(1, NE) as e:
                    for j in range(EK):
                        sp.wait_ge(S["ex_g"], e * EK - (EK - 1) + j)
                        sp.dma_start(w_gate[:, j, :, :], expert_cols(wg, e, j)).then_inc(gate_ld[j], 16)
                        sp.wait_ge(S["ex_u"], e * EK - (EK - 1) + j)
                        sp.dma_start(w_up[:, j, :, :], expert_cols(wu, e, j)).then_inc(up_ld[j], 16)
                    sp.wait_ge(S["ex_y"], 3 * e)
                    for j in range(EK):
                        sp.dma_start(w_down[:, j, :], expert_rows(wd, e, j)).then_inc(down_ld, 16)
                sp.wait_ge(S["hr_t"], 2 * (NT + 1))
                sp.dma_start(g_fin[:, :], A["g_final_2"].rearrange("(a n) -> a n", a=1).broadcast_to([P, D])).then_inc(S["gfin_ld"], 16)
                sp.wait_ge(S["ex_add_a"], 16 * NE)
                sp.wait_ge(S["ex_add_b"], 16 * NE)
                for t in range(NT):
                    sp.dma_start(fin[t][:, :], h_rows[META + t * P:META + (t + 1) * P, :]).then_inc(xin_lds[t], 16)
                for t in range(NT):
                    sp.wait_ge(S["fin_o"], t + 1)
                    sp.dma_start(out[0, t * P:(t + 1) * P, :], fin[t][:, :]).then_inc(S["fin_st"], 16)
                sp.wait_ge(S["fin_st"], 16 * NT)

            @block.gpsimd
            def _(pool):
                pool.wait_ge(S["dist_ld"], 16)
                with pool.Fori(0, HEADS) as h:
                    n = A0 + 3 * h
                    split(pool, n + 1, 1, TILES // 2 + h + 1, n - 2)
                    pool.wait_ge(S["aa_max"], h * (2 * NT + 2) + CREDIT)
                    seen(pool)
                    pool.tensor_scalar(biasH[:, :], biasH[:, :], 0.5, None, ALU.mult).then_inc(S["aa_bias"], 1)
                    split(pool, n + 2, 0, TILES // 2 + 2 * h + 2, n)
                    split(pool, n + 3, 0, TILES // 2 + 2 * h + 3, n + 2)

                def pairs(first, last):
                    with pool.Fori((first - MG0) // 2, (last - MG0) // 2) as i:
                        for j in range(2):
                            n = MG0 + 2 * i + j
                            split(pool, n, j, TAKEN[j] + i + 1, n - 2)

                split(pool, MG0 + 1, 1, TAKEN[1] + 1, MG0 - 1)
                pool.wait_ge(S["as_r"], 1)
                for t in range(1, NT, 2):
                    head_norm(pool, t).then_inc(S["as_np"], 1)
                pairs(MG0 + 2, B0)
                for g in range(KV):
                    pairs(B0 + g * ITEMS, B0 + (g + 1) * ITEMS)
                    with pool.Fori(0, GROUP) as j:
                        pool.wait_ge(S["ob_q"], g * (GROUP + 1) + 2 + j)
                        pool.wait_ge(S["bb_s"], (g * GROUP + j) * (NT + 1) + CREDIT)
                        seen(pool)
                        pool.tensor_copy(qs[:, :], q_grp[:, bass.ds(j, 1), :].rearrange("p a n -> p (a n)")).then_inc(S["bb_qs"], 1)
                pairs(GB0, ALL_TILES)
                pool.sem_inc(S["ex_free"], CREDIT)
                pool.wait_ge(S["tk_c"], 4)
                for j in range(4):
                    pool.wait_ge(row_st[j], 16 * ((NT + 2 - j % 2) // 2))

                def gather(e):
                    for r in range(2):
                        pool.tensor_copy(pick_g[r][:, :], pick[r][:, bass.ds(e, 1)]).then_inc(S["ex_pick_g"], 1)
                    pool.wait_ge(S["ex_pick_g"], e * 2 + 2)
                    seen(pool)
                    for r, done in enumerate(("ex_xa", "ex_xb")):
                        pool.indirect_dma_start(xs[r][:, :], None, u_rows, bass.IndirectOffsetOnAxis(ap=pick_g[r][:, :], axis=0)).then_inc(S[done], 16)

                def scatter(e):
                    for r in range(2):
                        pool.tensor_copy(pick_s[r][:, :], pick[r][:, bass.ds(e, 1)]).then_inc(S["ex_pick_s"], 1)
                    pool.wait_ge(S["ex_pick_s"], e * 2 + 2)
                    for r, (rows, done) in enumerate((("ex_ra", "ex_add_a"), ("ex_rb", "ex_add_b"))):
                        pool.wait_ge(S[rows], e * 2 + 2 + CREDIT)
                        seen(pool)
                        pool.indirect_dma_start(h_rows, bass.IndirectOffsetOnAxis(ap=pick_s[r][:, :], axis=0), y_row[r][:, :], None,
                                                compute_op=ALU.add).then_inc(S[done], 16)
                    pool.wait_ge(S["ex_add_a"], e * 16 + 16)
                    pool.wait_ge(S["ex_add_b"], e * 16 + 16)
                    pool.sem_inc(S["ex_free"], 1)

                gather(0)
                with pool.Fori(0, NE - 1) as e:
                    pool.wait_ge(S["ex_xt"], e * 3 + 3)
                    gather(e + 1)
                    scatter(e)
                scatter(NE - 1)

            @block.scalar
            def _(act):
                act.wait_ge(S["as_init"], 1)
                act.wait_ge(S["keep_st"], 48)
                with act.Fori(0, HEADS) as h:
                    n_head = A0 + 3 * h
                    act.wait_ge(S["w_used"], tile_done(n_head))
                    act.activation(thirds(qTa[:, :]), banks(0, 3, CH), ACT.Copy, scale=HD ** -0.5).then_inc(S["aa_qs"], 1)
                    act.wait_ge(S["aa_qs"], h + 1)
                    for k in range(2):
                        half = slice(k * HD, (k + 1) * HD)
                        act.activation(q_parts[k][half, :], qTa[half, :], ACT.Copy).then_inc(S["aa_qh"], 1)
                    act.wait_ge(S["aa_ks"], 7 * h + 1)
                    for k in range(2):
                        for n in (k, 1 - k):
                            act.activation(k_lead[k][n * HD:(n + 1) * HD, :], kTa[k * HD:(k + 1) * HD, :], ACT.Copy).then_inc(S["aa_kh"], 1)
                    act.wait_ge(S["w_used"], tile_done(n_head + 2))
                    act.activation(thirds(vTa[:, 0:2 * CH]), banks(6, 2, CH), ACT.Copy).then_inc(S["aa_vf"], 1)
                    act.activation(vTa[:, 2 * CH:T2], bank(5, T2 - 2 * CH), ACT.Copy).then_inc(S["aa_vf"], 1)
                    for n in range(2):
                        act.wait_ge(S["aa_v"], 3 * h + n + 1)
                        act.activation(Va[:, 4 * n:4 * n + 4, :], bank(5 + n).rearrange("p (t n) -> p t n", n=P), ACT.Copy).then_inc(S["aa_vs"], 1)
                    act.wait_ge(S["aa_v"], 3 * h + 3)
                    act.activation(Va[0:META, NT, :], bank(7, P, 0, META), ACT.Copy).then_inc(S["aa_vs"], 1)

                    def take_pt(t):
                        m = P if t < NT else META
                        act.wait_ge(S["aa_t"], 9 * h + t + 1)
                        if t >= 2:
                            act.wait_ge(S["aa_o"], 9 * h + t - 1)
                        act.activation(PTa[t % 2][:, 0:NT, 0:m], wide(5, NT * P).rearrange("p (j n) -> p j n", n=P)[:, :, 0:m], ACT.Copy).then_inc(S["aa_pt"], 1)
                        act.activation(PTa[t % 2][0:META, NT, 0:m], bank(7, m, 256, META), ACT.Copy).then_inc(S["aa_pt"], 1)

                    def square(t):
                        m = P if t < NT else META
                        act.wait_ge(S["aa_y"], 9 * h + t + 1 + CREDIT)
                        act.activation(junk[0:m, :], o_tok[0:m, t, bass.ds(h * P, P)], ACT.Square,
                                       accum_out=ss2[0:m, t, bass.ds(h, 1)]).then_inc(S["aa_ssq"], 1)
                        act.wait_ge(S["aa_ssq"], 9 * h + t + 1)

                    def exp(t, k):
                        m = P if t < NT else META
                        act.wait_ge(S["aa_max"], 18 * h + 2 * t + k + 1 + CREDIT)
                        e = EA[t % 2][k]
                        act.activation(e[0:m, :], e[0:m, :], ACT.Exp, scale=-1.0, bias=small[0:m, 8 + 2 * (t % 2) + k:9 + 2 * (t % 2) + k],
                                       accum_out=small[0:m, 12 + 2 * (t % 2) + k:13 + 2 * (t % 2) + k]).then_inc(S["aa_e"], 1)

                    def result(t):
                        m = P if t < NT else META
                        act.wait_ge(S["aa_o"], 9 * h + t + 1)
                        seen(act)
                        act.activation(o_tok[0:m, t, bass.ds(h * P, P)], bank(7, P, 0, m), ACT.Copy, scale=small[0:m, 20 + t % 3:21 + t % 3]).then_inc(S["aa_y"], 1)

                    for t in range(NT + 1):
                        exp(t, 0)
                        if t >= 2:
                            result(t - 2)
                        if t >= 1:
                            take_pt(t - 1)
                        exp(t, 1)
                        if t >= 3:
                            square(t - 3)
                    result(NT - 1)
                    take_pt(NT)
                    square(NT - 2)
                    result(NT)
                    for t in range(NT - 1, NT + 1):
                        square(t)
                def sigmoid(d, j, n, first):
                    act.wait_ge(S["w_used"], tile_done(n))
                    act.activation(thirds(gate_a[j][:, :]), banks(first, 3, CH), ACT.Sigmoid).then_inc(S["mg_sa"], 1)

                sigmoid(0, 0, MG0, 0)
                act.wait_ge(S["aa_ssq"], 9 * HEADS)
                act.activation(rs2[:, :, :], ss2[:, :, :], ACT.Sqrt, scale=1.0 / P, bias=eps[:, :]).then_inc(S["as_sd"], 1)
                for t in range(NT + 1):
                    m = P if t < NT else META
                    for half in range(2):
                        act.wait_ge(S["as_t"], 2 * t + half + 1)
                        act.activation(oa_hi[:, 4 * half:4 * half + 4, t * P:t * P + m], bank((6, 0)[t % 2] + half).rearrange("p (c n) -> p c n", n=P)[:, :, 0:m],
                                       ACT.Copy, scale=g_heads[:, G_SUBI:G_SUBI + 1]).then_inc(S["as_o"], 1)
                    if t == 0:
                        sigmoid(1, 1, gate_tile(1), 3)
                with act.Fori(1, KD // 2) as i:
                    for j in range(2):
                        act.wait_ge(S["mg_ma"], 2 * i + j - 1 + CREDIT)
                        sigmoid(2 * i + j, j, gate_tile(2 * i + j), 0)
                act.wait_ge(S["mg_ma"], KD + CREDIT)
                act.dma_start(m_keep, mergedT[:, :, :]).then_inc(S["m_st"], 16)
                for g in range(KV):
                    v0, z0 = 3 * g, g * (GROUP + 1)
                    def raw(n):
                        i = z0 + n
                        gain = g_heads[:, G_QNS:G_QNS + 1] if n else gains[:, G_KN:G_KN + 1]
                        act.wait_ge(S["w_used"], tile_done(B0 + g * ITEMS + n))
                        if i >= 1:
                            act.wait_ge(S["ob_ss"], i)
                            act.wait_ge(S["ob_m"], i)
                            act.wait_ge(S["ob_sw"], i)
                        act.activation(thirds(raw_b[:, :]), banks(3 * (n % 2), 3, CH), ACT.Copy, scale=gain).then_inc(S["ob_raw"], 1)
                        act.activation(thirds(sq_b[:, :]), banks(3 * (n % 2), 3, CH), ACT.Square).then_inc(S["ob_sq"], 1)

                    def root(n):
                        i = z0 + n
                        act.wait_ge(S["ob_ss"], i + 1)
                        if i >= 1:
                            act.wait_ge(S["ob_r"], i)
                        act.activation(sd_b[:, 0:T1], wide(6, T1), ACT.Sqrt, scale=1.0 / HB, bias=eps[:, :]).then_inc(S["ob_sd"], 1)
                        act.wait_ge(S["ob_m2"], 3 * i + 3)
                        act.activation(sd_b[:, T1:T2], bank(3 * (n % 2) + 2, META, 384), ACT.Sqrt, scale=1.0 / HB, bias=eps[:, :]).then_inc(S["ob_sd"], 1)

                    for n in range(GROUP + 1):
                        raw(n)
                        root(n)
                    act.wait_ge(S["ob_q"], z0 + 1)
                    act.activation(k_hi[:, :], kTb[:, :], ACT.Copy).then_inc(S["bb_kh"], 1)
                    act.wait_ge(S["w_used"], tile_done(B0 + g * ITEMS + GROUP + 1))
                    if g == 0:
                        act.wait_ge(S["m_st"], 16)
                    act.activation(thirds(vTb[:, 0:2 * CH]), banks(3, 2, CH), ACT.Copy).then_inc(S["ob_vf"], 1)
                    act.activation(vTb[:, 2 * CH:T2], bank(5, T2 - 2 * CH), ACT.Copy).then_inc(S["ob_vf"], 1)
                    for n in range(2):
                        act.wait_ge(S["ob_v"], v0 + n + 1)
                        act.activation(Vb[:, 4 * n:4 * n + 4, :], bank(6 + n).rearrange("p (t n) -> p t n", n=P), ACT.Copy).then_inc(S["ob_vs"], 1)
                    act.wait_ge(S["ob_v"], v0 + 3)
                    act.activation(Vb[0:META, NT, :], bank(5, P, 0, META), ACT.Copy).then_inc(S["ob_vs"], 1)
                    def head(j):
                        return (g * GROUP + j) * (NT + 1)

                    def queries(j):
                        act.wait_ge(S["ob_q"], z0 + 2 + j)
                        act.wait_ge(S["bb_s"], head(j) + CREDIT)
                        seen(act)
                        act.activation(q_hi[:, :], chunk(q_grp, j, T2), ACT.Copy).then_inc(S["bb_qh"], 1)

                    def take_pt(j, t):
                        m = P if t < NT else META
                        act.wait_ge(S["bb_t"], head(j) + t + 1)
                        if t >= 2:
                            act.wait_ge(S["bb_o"], head(j) + t - 1)
                        act.activation(PTb[t % 2][:, 0:NT, 0:m], wide(5, NT * P).rearrange("p (j n) -> p j n", n=P)[:, :, 0:m], ACT.Copy).then_inc(S["bb_pt"], 1)
                        act.activation(PTb[t % 2][0:META, NT, 0:m], bank(7, m, 256, META), ACT.Copy).then_inc(S["bb_pt"], 1)

                    def attend(j, more):
                        for t in range(NT + 1):
                            m = P if t < NT else META
                            act.wait_ge(S["bb_max"], head(j) + t + 1)
                            act.activation(EB[t % 3][0:m, :], EB[t % 3][0:m, :], ACT.Exp, scale=-1.0, bias=small[0:m, 24 + t % 3:25 + t % 3],
                                           accum_out=small[0:m, 27 + t % 3:28 + t % 3]).then_inc(S["bb_e"], 1)
                            if t >= 1:
                                take_pt(j, t - 1)
                            if t == NT - 1 and more:
                                queries(j + 1)
                        take_pt(j, NT)

                    queries(0)
                    with act.Fori(0, GROUP - 1) as j:
                        attend(j, True)
                    attend(GROUP - 1, False)
                with act.Fori(0, KD // 2) as i:
                    for j in range(2):
                        act.wait_ge(S["w_used"], tile_done(GB0 + 2 * i + j))
                        seen(act)
                        act.activation(gate_b[:, bass.ds(2 * i + j, 1), :].rearrange("p a (n w) -> p (a n) w", w=CH), banks(3 * j, 3, CH), ACT.Sigmoid).then_inc(S["mg_sb"], 1)
                act.wait_ge(S["pad_set"], 4)
                for c in range(HEADS):
                    act.activation(ob_hi[:, c, :], obT[:, c, :], ACT.Copy).then_inc(S["br_hi"], 1)
                with act.Fori(0, KD) as d:
                    act.wait_ge(S["mg_tmp"], d + 1)
                    seen(act)
                    act.activation(m_hi[:, bass.ds(d, 1), :], mergedT[:, bass.ds(d, 1), :], ACT.Copy).then_inc(S["mg_hi"], 1)
                with act.Fori(0, KD // 2) as i:
                    for j in range(2):
                        act.wait_ge(S["w2_x"], 2 * i + j + 1 + 2 * CREDIT)
                        square_chunk(act, 3, 2 * i + j, j, chunk(xT2, 2 * i + j, TP), TP)
                norm_root(act, 3)
                act.wait_ge(S["lg_z"], 1)
                act.activation(thirds(logT[:, :]), banks(0, 3, CH)[0:NE], ACT.Copy).then_inc(S["lg_c"], 1)
                act.wait_ge(S["router_step"], 6)
                act.activation(aff[:, :, 0:NE], aff[:, :, 0:NE], ACT.Exp).then_inc(S["lg_e"], 1)
                act.wait_ge(N["r"], 2 * pieces_upto(3) - pieces[3])
                for t in range(NT + 1):
                    rows = P if t < NT else META
                    if t >= 2:
                        for st in (0, 2):
                            act.wait_ge(row_st[st + t % 2], 16 * (t // 2))
                    for n in range(2):
                        act.wait_ge(S["hr_t"], 2 * t + n + 1)
                        src, cols = bank((2, 6)[t % 2] + n, BANK, 0, rows), slice(n * BANK, (n + 1) * BANK)
                        act.activation(h_row[t % 2][0:rows, cols], src, ACT.Copy).then_inc(S["hr_c"], 1)
                        act.activation(u_row[t % 2][0:rows, cols], src, ACT.Copy, scale=by_token(3)[0:rows, t:t + 1]).then_inc(S["hr_c"], 1)
                act.sem_inc(S["ex_rb"], CREDIT)
                with act.Fori(0, NE) as e:
                    for j in range(EK):
                        act.wait_ge(S["ex_g"], e * EK + j + 1)
                        act.wait_ge(S["ex_h"], e * EK + j - 1 + 2 * CREDIT)
                        act.activation(silu_e[j % 2][:, :], bank(3 + 2 * (j % 2), CAP), ACT.Silu).then_inc(S["ex_s"], 1)
                    act.wait_ge(S["ex_free"], e + CREDIT)
                    for n in range(2):
                        act.wait_ge(S["ex_r"], e * 2 + n + 1)
                        seen(act)
                        act.activation(y_row[1][:, n * BANK:(n + 1) * BANK], bank((7, 0)[n], BANK, 0, REST), ACT.Copy,
                                       scale=weight[1][:, bass.ds(e, 1)]).then_inc(S["ex_rb"], 1)
                for t in range(NT):
                    act.wait_ge(xin_lds[t], 32)
                    act.activation(fin_sq[:, :], fin[t][:, :], ACT.Square, accum_out=fin_s[:, 0, t:t + 1]).then_inc(S["fin_q"], 1)
                    act.wait_ge(S["fin_q"], t + 1)
                    act.activation(fin_s[:, 1, t:t + 1], fin_s[:, 0, t:t + 1], ACT.Sqrt, scale=1.0 / D, bias=eps[:, :]).then_inc(S["fin_sd"], 1)

            @block.vector
            def _(dve):
                for n in ("aa_max", "aa_y", "mg_ma", "ex_ra"):
                    dve.sem_inc(S[n], CREDIT)
                for n in ("ex_h", "w2_x", "mg_sb", "mg_mb"):
                    dve.sem_inc(S[n], 2 * CREDIT)
                ffn_gain = gains[:, NORM_GAINS[3]:NORM_GAINS[3] + KD]
                dve.wait_ge(S["router_ld"], 16)
                dve.tensor_tensor(router[:, :, :], router[:, :, :], ffn_gain.unsqueeze(2).broadcast_to([P, KD, NE]), ALU.mult).then_inc(S["router_set"], 1)
                dve.wait_ge(S["keep_st"], 48)
                dve.memset(kmeta[:, :], 0.0).then_inc(S["as_init"], 1)
                dve.wait_ge(S["as_init"], 2)
                with dve.Fori(0, HEADS) as h:
                    for k in range(2):
                        half, other = slice(k * HD, (k + 1) * HD), slice((1 - k) * HD, (2 - k) * HD)
                        dve.wait_ge(S["aa_qh"], 2 * h + k + 1)
                        dve.tensor_tensor(q_parts[k][other, :], qTa[half, :], q_parts[k][half, :], ALU.subtract).then_inc(S["aa_ql"], 1)
                    dve.wait_ge(S["w_used"], tile_done(A0 + 3 * h + 1))
                    dve.tensor_copy(thirds(kTa[:, :]), banks(3, 3, CH)).then_inc(S["aa_ks"], 1)
                    dve.wait_ge(S["aa_ks"], 7 * h + 1)
                    for k in range(2):
                        half = slice(k * HD, (k + 1) * HD)
                        dve.tensor_copy(kmeta[half, k * META:(k + 1) * META], kTa[half, T1:T2]).then_inc(S["aa_ks"], 1)
                    for k in range(2):
                        for n in range(2):
                            half = slice(k * HD, (k + 1) * HD)
                            if n == 0:
                                dve.wait_ge(S["aa_kh"], 4 * h + 2 * k + 1)
                            dve.tensor_tensor(k_rest[k][n * HD:(n + 1) * HD, :], kTa[half, :], k_lead[k][half, :], ALU.subtract).then_inc(S["aa_ks"], 1)
                    dve.wait_ge(S["aa_bias"], h + 1)

                    dve.wait_ge(S["aa_mt"], h + 1)
                    for m, tiles in ((P, slice(0, NT)), (META, slice(NT, NT + 1))):
                        n = tiles.stop - tiles.start
                        dve.tensor_scalar(meta_a[0:m, tiles, :, :].rearrange("p t k n -> p (t k n)"), bank(4, n * 2 * META, tiles.start * 2 * META, m), -1.0, None,
                                          ALU.mult).then_inc(S["aa_ms"], 1)
                    dve.wait_ge(S["aa_ms"], 4 * h + 2)
                    for m, tiles in ((P, slice(0, NT)), (META, slice(NT, NT + 1))):
                        dve.tensor_reduce(low_a[0:m, tiles, :].rearrange("p t k -> p (t k)"), meta_a[0:m, tiles, :, :].rearrange("p t k n -> p (t k) n"), AX,
                                          ALU.min).then_inc(S["aa_ms"], 1)
                    dve.wait_ge(S["aa_ms"], 4 * h + 4)

                    def scores(t, k):
                        m = P if t < NT else META
                        low = small[0:m, 8 + 2 * (t % 2) + k:9 + 2 * (t % 2) + k]
                        bias = biasH[:, T1 - P - t * P:2 * T1 - P - t * P] if t < NT else zero[0:m, :].broadcast_to([m, T1])
                        if t >= 2 and k == 0:
                            dve.wait_ge(S["aa_t"], 9 * h + t - 1)
                        if t == 1 and k == 0:
                            dve.wait_ge(S["aa_v"], 3 * h + 3)
                        if k == 0:
                            dve.tensor_copy(EA[t % 2][0][0:m, T1:T2], meta_a[0:m, t, 0, :])
                            dve.tensor_copy(EA[t % 2][1][0:m, T1:T2], meta_a[0:m, t, 1, :])
                        dve.wait_ge(S["aa_s"], 18 * h + 2 * t + k + 1)
                        seen(dve)
                        dve.tensor_tensor_reduce(EA[t % 2][k][0:m, 0:T1], wide(2 * k, T1, m), bias, -1.0, low_a[0:m, t, k:k + 1], ALU.add, ALU.min,
                                                 low).then_inc(S["aa_max"], 1)

                    def columns(t):
                        m = P if t < NT else META
                        den = [small[0:m, 12 + 2 * (t % 2) + k:13 + 2 * (t % 2) + k] for k in range(2)]
                        return den, small[0:m, 40 + t % 2:41 + t % 2], small[0:m, 42 + t % 2:43 + t % 2], small[0:m, 20 + t % 3:21 + t % 3]

                    def sums(t):
                        den, r2, c2, r1 = columns(t)
                        if t >= 3:
                            dve.wait_ge(S["aa_y"], 9 * h + t - 2 + CREDIT)
                        dve.wait_ge(S["aa_e"], 18 * h + 2 * t + 2)
                        dve.reciprocal(r2, den[1]).then_inc(S["aa_sm"], 1)
                        dve.reciprocal(r1, den[0]).then_inc(S["aa_sm"], 1)

                    def combine(t):
                        m = P if t < NT else META
                        den, r2, c2, r1 = columns(t)
                        dve.wait_ge(S["aa_sm"], 27 * h + 3 * t + 2)
                        dve.tensor_scalar(c2, den[0], r2, lam_sm[0:m, 4:5], ALU.mult, ALU.mult).then_inc(S["aa_sm"], 1)
                        dve.wait_ge(S["aa_sm"], 27 * h + 3 * t + 3)
                        dve.scalar_tensor_tensor(EA[t % 2][0][0:m, :], EA[t % 2][1][0:m, :], c2, EA[t % 2][0][0:m, :], ALU.mult, ALU.add).then_inc(S["aa_c"], 1)

                    scores(0, 0)
                    scores(0, 1)
                    for t in range(NT + 1):
                        if t < NT:
                            scores(t + 1, 0)
                        sums(t)
                        combine(t)
                        if t < NT:
                            scores(t + 1, 1)
                dve.wait_ge(S["as_sd"], 1)
                dve.reciprocal(ss2[:, :, :], rs2[:, :, :]).then_inc(S["as_r"], 1)
                dve.wait_ge(S["as_r"], 1)
                for t in range(0, NT + 1, 2):
                    head_norm(dve, t).then_inc(S["as_n"], 1)
                for t in range(NT + 1):
                    m = P if t < NT else META
                    for half in range(2):
                        dve.wait_ge(S["as_o"], 2 * t + half + 1)
                        heads = slice(4 * half, 4 * half + 4)
                        dve.scalar_tensor_tensor(oa_lo[:, heads, t * P:t * P + m], bank((6, 0)[t % 2] + half).rearrange("p (c n) -> p c n", n=P)[:, :, 0:m],
                                                 g_heads[:, G_SUBI:G_SUBI + 1], oa_hi[:, heads, t * P:t * P + m], ALU.mult, ALU.subtract).then_inc(S["as_lo"], 1)
                for part in (oa_hi, oa_lo):
                    dve.memset(part[:, :, T2:TP].bitcast(F32), 0.0).then_inc(S["pad_set"], 1)
                def gated(d, j, n):
                    dve.wait_ge(S["mg_sa"], d + 1)
                    dve.wait_ge(S["w_used"], tile_done(n))
                    dve.tensor_tensor(mergedT[:, bass.ds(d, 1), :].rearrange("p a (n w) -> p (a n) w", w=CH), thirds(gate_a[j][:, :]), banks(3, 3, CH), ALU.mult).then_inc(S["mg_ma"], 1)

                with dve.Fori(0, KD // 2 - 1) as i:
                    for j in range(2):
                        gated(2 * i + j, j, branch_tile(2 * i + j))
                gated(KD - 2, 0, branch_tile(KD - 2))
                gated(KD - 1, 1, B0 - 1)
                dve.wait_ge(S["rope_ld"], 32)
                for g in range(KV):
                    z0 = g * (GROUP + 1)
                    for n in range(GROUP + 1):
                        i = z0 + n
                        dst = q_grp[:, n - 1, :] if n else kTb[:, :]
                        dve.wait_ge(S["ob_raw"], i + 1)
                        if i:
                            dve.wait_ge(S["ob_q"], i)
                        if g and n == 0:
                            dve.wait_ge(S["bb_t"], g * GROUP * (NT + 1))
                        dve.tensor_tensor(cos_b[:, 0:T2], raw_b[:, 0:T2], cos[:, :], ALU.mult).then_inc(S["ob_m"], 1)
                        dve.wait_ge(S["ob_sw"], i + 1)
                        for k in range(3):
                            w = min(CH, T2 - k * CH)
                            c = slice(k * CH, k * CH + w)
                            if i and k == 0:
                                dve.wait_ge(S["ob_m3"], i)
                            ins = dve.tensor_tensor(swapped[:, c], bank(3 * (n % 2) + k, w), sin[:, c], ALU.mult)
                            ins.then_inc(S["ob_m2"], 1)
                        dve.wait_ge(S["ob_m2"], 3 * i + 3)
                        dve.wait_ge(S["ob_m"], i + 1)
                        dve.tensor_tensor(swapped[:, :], swapped[:, :], cos_b[:, 0:T2], ALU.add).then_inc(S["ob_m3"], 1)
                        dve.wait_ge(S["ob_sd"], 2 * i + 2)
                        dve.reciprocal(rs_b[:, 0:T2], sd_b[:, 0:T2]).then_inc(S["ob_r"], 1)
                        dve.wait_ge(S["ob_m3"], i + 1)
                        dve.wait_ge(S["ob_r"], i + 1)
                        if i == 1:
                            dve.wait_ge(S["m_st"], 16)
                        dve.tensor_tensor(dst, swapped[:, :], rs_b[:, 0:T2], ALU.mult).then_inc(S["ob_q"], 1)
                    dve.tensor_copy(k_meta[:, :], kTb[:, T1:T2]).then_inc(S["bb_kl"], 1)
                    dve.wait_ge(S["bb_kl"], 2 * g + 1)
                    dve.wait_ge(S["bb_kh"], g + 1)
                    dve.tensor_tensor(k_lo[:, :], kTb[:, :], k_hi[:, :], ALU.subtract).then_inc(S["bb_kl"], 1)

                    def queries(j):
                        dve.wait_ge(S["bb_qh"], g * GROUP + j + 1)
                        dve.tensor_tensor(q_lo[:, :], chunk(q_grp, j, T2), q_hi[:, :], ALU.subtract).then_inc(S["bb_ql"], 1)

                    def head(j):
                        return (g * GROUP + j) * (NT + 1)

                    def meta_scores(j):
                        n_head = g * GROUP + j
                        dve.wait_ge(S["bb_mt"], n_head + 1)
                        for m, tiles in ((P, slice(0, NT)), (META, slice(NT, NT + 1))):
                            n = tiles.stop - tiles.start
                            dve.tensor_scalar(meta_b[0:m, tiles, :].rearrange("p t n -> p (t n)"), bank(4, n * META, tiles.start * META, m), -1.0, None,
                                              ALU.mult).then_inc(S["bb_ms"], 1)
                        dve.wait_ge(S["bb_ms"], 4 * n_head + 2)
                        for m, tiles in ((P, slice(0, NT)), (META, slice(NT, NT + 1))):
                            dve.tensor_reduce(low_b[0:m, tiles], meta_b[0:m, tiles, :], AX, ALU.min).then_inc(S["bb_ms"], 1)
                        dve.wait_ge(S["bb_ms"], 4 * n_head + 4)

                    def scores(j, t):
                        m = P if t < NT else META
                        e = EB[t % 3]
                        if t >= 3:
                            dve.wait_ge(S["bb_t"], head(j) + t - 2)
                        dve.tensor_copy(e[0:m, T1:T2], meta_b[0:m, t, :])
                        dve.wait_ge(S["bb_s"], head(j) + t + 1 + CREDIT)
                        seen(dve)
                        dve.tensor_tensor_reduce(e[0:m, 0:T1], wide(2 * (t % 2), T1, m), zero[0:m, :].broadcast_to([m, T1]), -1.0, low_b[0:m, t:t + 1], ALU.add, ALU.min,
                                                 small[0:m, 24 + t % 3:25 + t % 3]).then_inc(S["bb_max"], 1)

                    def divide(j, t):
                        m = P if t < NT else META
                        r = small[0:m, 30 + t % 3:31 + t % 3]
                        dve.wait_ge(S["bb_e"], head(j) + t + 1)
                        dve.reciprocal(r, small[0:m, 27 + t % 3:28 + t % 3]).then_inc(S["bb_rd"], 1)
                        dve.wait_ge(S["bb_rd"], head(j) + t + 1)
                        dve.tensor_scalar(EB[t % 3][0:m, :], EB[t % 3][0:m, :], r, None, ALU.mult).then_inc(S["bb_p"], 1)

                    def result(j, t):
                        m = P if t < NT else META
                        dve.wait_ge(S["bb_o"], head(j) + t + 1)
                        dve.tensor_copy(obT[:, bass.ds(g * GROUP + j, 1), t * P:t * P + m].rearrange("p a n -> p (a n)"), bank(7, m)).then_inc(S["bb_ob"], 1)

                    def attend(j, more):
                        for t in range(NT + 1):
                            if 1 <= t < NT:
                                scores(j, t + 1)
                            elif t == NT and more:
                                meta_scores(j + 1)
                            divide(j, t)
                            if t >= 1:
                                result(j, t - 1)
                            if t == NT - 1 and more:
                                queries(j + 1)
                        if more:
                            for t in range(2):
                                dve.wait_ge(S["bb_t"], head(j) + NT - 1 + t)
                                scores(j + 1, t)
                        result(j, NT)

                    dve.wait_ge(S["ob_v"], 3 * g + 3)
                    queries(0)
                    meta_scores(0)
                    scores(0, 0)
                    scores(0, 1)
                    with dve.Fori(0, GROUP - 1) as j:
                        attend(j, True)
                    attend(GROUP - 1, False)
                dve.memset(obT[:, :, T2:TP], 0.0).then_inc(S["pad_set"], 1)
                for c in range(HEADS):
                    dve.wait_ge(S["br_hi"], c + 1)
                    dve.tensor_tensor(ob_lo[:, c, :], obT[:, c, :], ob_hi[:, c, :], ALU.subtract).then_inc(S["br_lo"], 1)
                with dve.Fori(0, KD // 2) as i:
                    for j in range(2):
                        d = 2 * i + j
                        gate, m = (t[:, bass.ds(d, 1), :].rearrange("p a (n w) -> p (a n) w", w=CH) for t in (gate_b, mergedT))
                        dve.wait_ge(S["w_used"], tile_done(BR0 + d))
                        dve.tensor_tensor(gate, gate, banks(3 * j, 3, CH), ALU.mult).then_inc(S["mg_mb"], 1)
                        dve.wait_ge(S["m_ld"], 16 * d + 16)
                        dve.wait_ge(S["mg_mb"], d + 1 + 2 * CREDIT)
                        dve.tensor_tensor(m, m, gate, ALU.add).then_inc(S["mg_tmp"], 1)
                        dve.wait_ge(S["mg_hi"], d + 1)
                        dve.tensor_tensor(m_lo[:, bass.ds(d, 1), :], mergedT[:, bass.ds(d, 1), :], m_hi[:, bass.ds(d, 1), :], ALU.subtract).then_inc(S["mg_lo"], 1)
                dve.wait_ge(S["keep_ld"], 32 + 16 * KD)
                no_squares(dve, 3, TP)
                with dve.Fori(0, KD // 2) as i:
                    for j in range(2):
                        dve.wait_ge(S["w_used"], tile_done(OUT0 + 2 * i + j))
                        residual(dve, xT2, 2 * i + j, 3 * j, 3, CH, "w2_x")
                        add_square(dve, 3, 2 * i + j, j, TP)
                dve.wait_ge(S["w2_x"], KD + 2 * CREDIT)
                norm_recip(dve, 3)
                dve.memset(aff[:, :, :], 0.0).then_inc(S["router_step"], 1)
                dve.memset(affT[:, :], 0.0).then_inc(S["router_step"], 1)
                dve.wait_ge(S["router_step"], 2)
                dve.wait_ge(S["lg_y"], 1)
                once = aff[:, :, 0:NE]
                dve.tensor_tensor(aff[:, 0:NT, 0:NE], bank(4, NT * NE).rearrange("p (t n) -> p t n", n=NE),
                                  by_token(3)[:, 0:NT].unsqueeze(2).broadcast_to([P, NT, NE]), ALU.mult).then_inc(S["router_step"], 1)
                dve.tensor_scalar(aff[0:META, NT, 0:NE], bank(4, NE, NT * NE, META), by_token(3)[0:META, NT:NT + 1], None, ALU.mult).then_inc(S["router_step"], 1)
                dve.wait_ge(S["router_step"], 4)
                row_max, row_sum = small[:, 32:32 + NT + 1], small[:, 48:48 + NT + 1]
                dve.tensor_reduce(row_max, once, AX, ALU.max).then_inc(S["router_step"], 1)
                dve.wait_ge(S["router_step"], 5)
                dve.tensor_tensor(once, once, row_max.unsqueeze(2).broadcast_to([P, NT + 1, NE]), ALU.subtract).then_inc(S["router_step"], 1)
                dve.wait_ge(S["lg_e"], 1)
                dve.tensor_reduce(row_sum, once, AX, ALU.add).then_inc(S["router_step"], 1)
                dve.wait_ge(S["router_step"], 7)
                dve.reciprocal(row_max, row_sum).then_inc(S["router_step"], 1)
                dve.wait_ge(S["router_step"], 8)
                dve.tensor_tensor(once, once, row_max.unsqueeze(2).broadcast_to([P, NT + 1, NE]), ALU.mult).then_inc(S["router_step"], 1)
                dve.wait_ge(S["router_step"], 9)
                dve.tensor_copy(aff[:, :, LATE:LATE + NE], once).then_inc(S["router_step"], 1)
                half = T2 // 2
                n = half - META
                late = slice(LATE, LATE + NE)
                dve.wait_ge(S["lg_t"], 1)
                dve.tensor_copy(affT[0:NE, META:half], bank(0, n, 0, NE)).then_inc(S["router_step"], 1)
                dve.tensor_copy(affT[late, 0:BANK - n], PS[late, 0, n:BANK]).then_inc(S["router_step"], 1)
                dve.wait_ge(S["lg_t"], 2)
                dve.tensor_copy(affT[late, BANK - n:half], PS[late, 1, 0:BANK]).then_inc(S["router_step"], 1)
                dve.wait_ge(S["lg_t"], 3)
                dve.tensor_copy(affT[0:NE, 0:META], bank(4, META, 0, NE)).then_inc(S["router_step"], 1)
                dve.wait_ge(S["router_step"], 14)
                for r in range(ROUNDS):
                    e8 = slice(8 * r, 8 * r + 8)
                    dve.max(best[:, e8], affT[:, :]).then_inc(S["tk_step"], 1)
                    dve.wait_ge(S["tk_step"], 3 * r + 1)
                    dve.max_index(where[:, e8], best[:, e8], affT[:, :]).then_inc(S["tk_step"], 1)
                    if r < ROUNDS - 1:
                        dve.wait_ge(S["tk_step"], 3 * r + 2)
                        dve.match_replace(affT[:, :], best[:, e8], affT[:, :], -1.0).then_inc(S["tk_step"], 1)
                        dve.wait_ge(S["tk_step"], 3 * r + 3)
                done = 3 * ROUNDS - 1
                dve.wait_ge(S["tk_step"], done)
                dve.tensor_copy(where_f[:, :], where[:, :]).then_inc(S["tk_step"], 1)
                dve.tensor_copy(late_best[:, :], best[late, CAP - 1::-1]).then_inc(S["tk_step"], 1)
                dve.wait_ge(S["tk_step"], done + 2)
                dve.tensor_scalar(late_where[:, :], where_f[late, CAP - 1::-1], float(half), None, ALU.add).then_inc(S["tk_step"], 1)
                dve.tensor_tensor(earlier[:, :], best[0:NE, 0:CAP], late_best[:, :], ALU.is_ge).then_inc(S["tk_step"], 1)
                dve.tensor_tensor(top_best[:, :], best[0:NE, 0:CAP], late_best[:, :], ALU.max).then_inc(S["tk_step"], 1)
                dve.wait_ge(S["tk_step"], done + 3)
                dve.tensor_tensor(top_where[:, :], where_f[0:NE, 0:CAP], late_where[:, :], ALU.subtract).then_inc(S["tk_step"], 1)
                dve.wait_ge(S["tk_step"], done + 6)
                dve.tensor_tensor(top_where[:, :], top_where[:, :], earlier[:, :], ALU.mult).then_inc(S["tk_step"], 1)
                dve.wait_ge(S["tk_step"], done + 7)
                dve.tensor_tensor(top_where[:, :], top_where[:, :], late_where[:, :], ALU.add).then_inc(S["tk_step"], 1)
                dve.wait_ge(S["tk_t"], 1)
                for r, rows in enumerate((P, REST)):
                    dve.tensor_copy(pick[r][:, :], bank(0, NE, 2 * r * NE, rows)).then_inc(S["tk_c"], 1)
                    dve.tensor_copy(weight[r][:, :], bank(0, NE, (2 * r + 1) * NE, rows)).then_inc(S["tk_c"], 1)
                dve.wait_ge(S["tk_c"], 4)
                def take_tokens(e):
                    for n, (c, k) in enumerate(((0, 3), (3, 3), (6, 2))):
                        dve.wait_ge(S["ex_xt"], e * 3 + n + 1)
                        dve.tensor_tensor(xsT[:, c:c + k, :], bank(2 + n, k * CAP).rearrange("p (c n) -> p c n", n=CAP),
                                          ffn_gain[:, c:c + k].unsqueeze(2).broadcast_to([P, k, CAP]), ALU.mult).then_inc(S["ex_xc"], 1)

                def expert(e, more):
                    for j in range(EK):
                        dve.wait_ge(S["ex_s"], e * EK + j + 1)
                        dve.wait_ge(S["ex_u"], e * EK + j + 1)
                        dve.tensor_tensor(hidT[:, j, :], silu_e[j % 2][:, :], bank(4 + 2 * (j % 2), CAP), ALU.mult).then_inc(S["ex_h"], 1)
                    for n, (b, c, k) in enumerate(((7, 0, 3), (0, 3, 3), (1, 6, 2))):
                        dve.wait_ge(S["ex_y"], e * 3 + n + 1)
                        dve.tensor_copy(yT[:, c:c + k, :], bank(b, k * CAP).rearrange("p (c n) -> p c n", n=CAP)).then_inc(S["ex_yt"], 1)
                    if more:
                        take_tokens(e + 1)
                    dve.wait_ge(S["ex_free"], e + CREDIT)
                    for n in range(2):
                        dve.wait_ge(S["ex_r"], e * 2 + n + 1)
                        dve.tensor_scalar(y_row[0][:, n * BANK:(n + 1) * BANK], bank(5 + n), weight[0][:, bass.ds(e, 1)], None, ALU.mult).then_inc(S["ex_ra"], 1)

                take_tokens(0)
                with dve.Fori(0, NE - 1) as e:
                    expert(e, True)
                expert(NE - 1, False)
                dve.wait_ge(S["gfin_ld"], 16)
                for t in range(NT):
                    dve.wait_ge(S["fin_sd"], t + 1)
                    dve.reciprocal(fin_s[:, 2, t:t + 1], fin_s[:, 1, t:t + 1]).then_inc(S["fin_r"], 1)
                    dve.wait_ge(S["fin_r"], t + 1)
                    dve.scalar_tensor_tensor(fin[t][:, :], fin[t][:, :], fin_s[:, 2, t:t + 1], g_fin[:, :], ALU.mult, ALU.mult).then_inc(S["fin_o"], 1)

            @block.tensor
            def _(pe):
                pe.sem_inc(S["bb_s"], CREDIT)
                with pe.Fori(0, HEADS) as h:
                    n_head = A0 + 3 * h
                    project_split(pe, 1, n_head + 1, *triple(3))
                    def scores(t, k):
                        m = P if t < NT else META
                        if t == 0 and k == 0:
                            pe.wait_ge(S["aa_ks"], 7 * h + 7)
                            pe.wait_ge(S["aa_ql"], 2 * h + 2)
                            pe.wait_ge(S["aa_kh"], 4 * h + 4)
                            pe.wait_ge(S["aa_qs"], h + 1)
                        if t:
                            pe.wait_ge(S["aa_max"], 18 * h + 2 * t + k - 1 + CREDIT)
                        if m < P:
                            seen(pe)
                        for keys, part in ((0, k_lead), (1, k_rest)):
                            for b in range(2):
                                last = mm(bank(2 * k + b, BANK, 0, m), q_parts[k][:, t * P:t * P + m], part[k][:, b * BANK:(b + 1) * BANK],
                                          start=(keys == 0), stop=(keys == 1))
                        last.then_inc(S["aa_s"], 1)

                    def ready(c):
                        if c == KD - 2:
                            pe.wait_ge(S["aa_ks"], 7 * h + 3)
                            for t in range(NT + 1):
                                m = P if t < NT else META
                                if m < P:
                                    seen(pe)
                                last = mm(bank(4, 2 * META, t * 2 * META, m), qTa[:, t * P:t * P + m], kmeta[:, :], start=True, stop=True)
                            last.then_inc(S["aa_mt"], 1)
                            scores(0, 0)
                            scores(0, 1)

                    pe.wait_ge(S["aa_y"], 9 * h + CREDIT)
                    pe.wait_ge(S["aa_ks"], 7 * h + 1)
                    project_split(pe, 0, n_head + 2, (6, 7, 5), CH, u2_hi, u2_lo, ready)

                    def turn_probs(t):
                        m = P if t < NT else META
                        e = EA[t % 2][0]
                        if t == 0:
                            pe.wait_ge(S["aa_vs"], 3 * h + 3)
                        pe.wait_ge(S["aa_c"], 9 * h + t + 1)
                        if m < P:
                            seen(pe)
                        for j in range(NT):
                            turn(bank(5 + j // 4, m, (j % 4) * P), e[0:m, j * P:(j + 1) * P], m)
                        if t >= 1:
                            pe.wait_ge(S["aa_y"], 9 * h + t + CREDIT)
                            if m < P:
                                seen(pe)
                        turn(bank(7, m, 256, META), e[0:m, T1:T2], m).then_inc(S["aa_t"], 1)

                    def values(t):
                        m = P if t < NT else META
                        pe.wait_ge(S["aa_pt"], 18 * h + 2 * t + 2)
                        for j in range(NT):
                            mm(bank(7, P, 0, m), PTa[t % 2][:, j, 0:m], Va[:, j, :], start=(j == 0), stop=False)
                        mm(bank(7, P, 0, m), PTa[t % 2][0:META, NT, 0:m], Va[0:META, NT, :], start=False, stop=True).then_inc(S["aa_o"], 1)

                    pe.wait_ge(S["aa_vf"], 2 * h + 2)
                    for t in range(NT + 1):
                        m = P if t < NT else META
                        last = turn(bank(5 + t // 4, P, (t % 4) * P, m), vTa[:, t * P:t * P + m])
                        if t in (3, 7, 8):
                            last.then_inc(S["aa_v"], 1)
                    scores(1, 0)
                    for t in range(NT + 1):
                        if t < NT:
                            scores(t + 1, 1)
                        if t >= 1:
                            values(t - 1)
                        if t + 2 <= NT:
                            scores(t + 2, 0)
                        if t < NT:
                            turn_probs(t)
                    pe.wait_ge(S["aa_max"], 18 * h + 18 + CREDIT)
                    project_split(pe, 0, n_head + 3, *triple(0), lambda c: turn_probs(NT) if c == KD - 2 else None)
                    values(NT)
                project_split(pe, 1, gate_tile(1), *triple(3))
                for t in range(NT + 1):
                    m = P if t < NT else META
                    pe.wait_ge(S["as_np" if t % 2 else "as_n"], t // 2 + 1)
                    for half in range(2):
                        if t >= 2:
                            pe.wait_ge(S["as_lo"], 2 * (t - 2) + half + 1)
                        elif t:
                            pe.wait_ge(S["mg_sa"], 1)
                        else:
                            pe.wait_ge(S["aa_y"], 9 * HEADS + CREDIT)
                        for c in range(4):
                            last = turn(bank((6, 0)[t % 2] + half, m, c * P), o_tok[0:m, t, (4 * half + c) * P:(4 * half + c + 1) * P], m)
                        last.then_inc(S["as_t"], 1)
                pe.wait_ge(S["as_lo"], 2 * (NT + 1))
                pe.wait_ge(S["pad_set"], 3)

                def branch_a(d, j, n):
                    pe.wait_ge(S["mg_ma"], d + CREDIT)
                    project_split(pe, j, n, (3, 4, 5), CH, oa_hi, oa_lo)

                pe.wait_ge(S["mg_sa"], 2)
                with pe.Fori(0, KD - 2) as d:
                    branch_a(d, 0, branch_tile(d))
                    pe.wait_ge(S["mg_sa"], d + 2)
                    project_split(pe, 1, gate_tile(d + 2), *triple(0))
                branch_a(KD - 2, 0, branch_tile(KD - 2))
                branch_a(KD - 1, 1, B0 - 1)
                pe.wait_ge(S["mg_sa"], KD)
                for g in range(KV):
                    z0 = g * (GROUP + 1)
                    def normed(n):
                        i = z0 + n
                        first = 3 * (n % 2)
                        pe.wait_ge(S["ob_sq"], i + 1)
                        pe.wait_ge(S["ob_raw"], i + 1)
                        mm(bank(first + 2, META, 384), ones[:, :], sq_b[:, T1:T2], start=True, stop=True)
                        for b in range(3):
                            last = mm(bank(first + b, CH), swap[:, :], raw_b[:, b * CH:(b + 1) * CH], start=True, stop=True)
                        last.then_inc(S["ob_sw"], 1)
                        if n:
                            pe.wait_ge(S["ob_sd"], 2 * i)
                        for b in range(2):
                            last = mm(bank(6 + b), ones[:, :], sq_b[:, b * BANK:(b + 1) * BANK], start=True, stop=True)
                        last.then_inc(S["ob_ss"], 1)

                    if g:
                        pe.wait_ge(S["bb_ob"], g * GROUP * (NT + 1))
                    for n in range(GROUP + 1):
                        i = z0 + n
                        if i == 1:
                            pe.wait_ge(S["mg_ma"], KD + CREDIT)
                        if n >= 2:
                            pe.wait_ge(S["ob_m2"], 3 * (i - 1))
                            pe.wait_ge(S["ob_sd"], 2 * (i - 1))
                        project_split(pe, n % 2, B0 + g * ITEMS + n, *triple(3 * (n % 2)))
                        if n:
                            normed(n - 1)
                    normed(GROUP)
                    pe.wait_ge(S["ob_m2"], 3 * (z0 + GROUP))
                    pe.wait_ge(S["ob_sd"], 2 * (z0 + GROUP))
                    project_split(pe, 1, B0 + g * ITEMS + GROUP + 1, *triple(3))
                    pe.wait_ge(S["ob_vf"], 2 * g + 2)
                    pe.wait_ge(S["ob_sd"], 2 * (z0 + GROUP + 1))
                    for t in range(NT + 1):
                        m = P if t < NT else META
                        last = turn(bank(6 + t // 4 if t < NT else 5, P, (t % 4) * P, m), vTb[:, t * P:t * P + m])
                        if t in (3, 7, 8):
                            last.then_inc(S["ob_v"], 1)

                    def head(j):
                        return (g * GROUP + j) * (NT + 1)

                    def meta_scores(j):
                        pe.wait_ge(S["bb_qs"], g * GROUP + j + 1)
                        for t in range(NT + 1):
                            m = P if t < NT else META
                            if m < P:
                                seen(pe)
                            last = mm(bank(4, META, t * META, m), qs[:, t * P:t * P + m], k_meta[:, :], start=True, stop=True)
                        last.then_inc(S["bb_mt"], 1)

                    def scores(j, t):
                        m = P if t < NT else META
                        if t >= 2:
                            pe.wait_ge(S["bb_max"], head(j) + t - 1)
                        if t == 0:
                            pe.wait_ge(S["bb_ql"], g * GROUP + j + 1)
                        if m < P:
                            seen(pe)
                        for k, (q, keys) in enumerate(((q_hi, k_hi), (q_hi, k_lo), (q_lo, k_hi))):
                            for b in range(2):
                                last = mm(bank(2 * (t % 2) + b, BANK, 0, m), q[:, t * P:t * P + m], keys[:, b * BANK:(b + 1) * BANK], start=(k == 0), stop=(k == 2))
                        last.then_inc(S["bb_s"], 1)

                    def turn_probs(j, t):
                        m = P if t < NT else META
                        e = EB[t % 3]
                        pe.wait_ge(S["bb_p"], head(j) + t + 1)
                        if m < P:
                            seen(pe)
                        for i in range(NT):
                            turn(bank(5 + i // 4, m, (i % 4) * P), e[0:m, i * P:(i + 1) * P], m)
                        if t >= 1:
                            pe.wait_ge(S["bb_ob"], head(j) + t)
                            if m < P:
                                seen(pe)
                        turn(bank(7, m, 256, META), e[0:m, T1:T2], m).then_inc(S["bb_t"], 1)

                    def values(j, t):
                        m = P if t < NT else META
                        pe.wait_ge(S["bb_pt"], 2 * head(j) + 2 * t + 2)
                        for i in range(NT):
                            mm(bank(7, m), Vb[:, i, :], PTb[t % 2][:, i, 0:m], start=(i == 0), stop=False)
                        mm(bank(7, m), Vb[0:META, NT, :], PTb[t % 2][0:META, NT, 0:m], start=False, stop=True).then_inc(S["bb_o"], 1)

                    def attend(j, more):
                        for t in range(NT + 1):
                            if t + 2 <= NT:
                                scores(j, t + 2)
                            if t >= 1:
                                values(j, t - 1)
                            if t == NT and more:
                                meta_scores(j + 1)
                                pe.wait_ge(S["bb_max"], head(j) + NT + 1)
                                scores(j + 1, 0)
                            turn_probs(j, t)
                        if more:
                            scores(j + 1, 1)
                        values(j, NT)

                    pe.wait_ge(S["ob_vs"], 3 * g + 3)
                    pe.wait_ge(S["bb_kl"], 2 * g + 2)
                    meta_scores(0)
                    scores(0, 0)
                    scores(0, 1)
                    with pe.Fori(0, GROUP - 1) as j:
                        attend(j, True)
                    attend(GROUP - 1, False)
                pe.wait_ge(S["bb_ob"], HEADS * (NT + 1))
                with pe.Fori(0, KD // 2) as i:
                    for j in range(2):
                        pe.wait_ge(S["mg_sb"], 2 * i + j - 1 + 2 * CREDIT)
                        project_split(pe, j, GB0 + 2 * i + j, *triple(3 * j))
                pe.wait_ge(S["mg_sb"], KD + 2 * CREDIT)
                with pe.Fori(0, KD // 2) as i:
                    for j in range(2):
                        pe.wait_ge(S["mg_mb"], 2 * i + j - 1 + 2 * CREDIT)
                        project_split(pe, j, BR0 + 2 * i + j, (3 * j, 3 * j + 1, 3 * j + 2), CH, ob_hi, ob_lo,
                                      None if j else lambda c: pe.wait_ge(S["br_lo"], c + 1))
                pe.wait_ge(S["mg_mb"], KD - 1 + 2 * CREDIT)
                with pe.Fori(0, KD // 2) as i:
                    for j in range(2):
                        pe.wait_ge(S["w2_x"], 2 * i + j - 1 + 2 * CREDIT)
                        project_split(pe, j, OUT0 + 2 * i + j, (3 * j, 3 * j + 1, 3 * j + 2), CH, m_hi, m_lo,
                                      None if j else lambda c: pe.wait_ge(S["mg_lo"], c + 1))
                pe.wait_ge(S["router_set"], 1)
                pe.wait_ge(S["w2_x"], KD - 1 + 2 * CREDIT)
                for c in range(KD):
                    if c == KD - 1:
                        norm_sum(pe, 3)
                    for b in range(3):
                        last = mm(bank(b, CH, 0, NE), router[:, c, :], xT2[:, c, b * CH:(b + 1) * CH], start=(c == 0), stop=(c == KD - 1))
                last.then_inc(S["lg_z"], 1)
                pe.wait_ge(S["lg_c"], 1)
                for t in range(NT + 1):
                    m = P if t < NT else META
                    last = turn(bank(4, NE, t * NE, m), logT[:, t * P:t * P + m], NE)
                last.then_inc(S["lg_y"], 1)

                def rows(t):
                    m = P if t < NT else META
                    for n in range(2):
                        if t >= 2:
                            pe.wait_ge(S["hr_c"], 4 * (t - 2) + 2 * n + 2)
                        for c in range(4):
                            last = turn(bank((2, 6)[t % 2] + n, P, c * P, m), xT2[:, 4 * n + c, t * P:t * P + m])
                        last.then_inc(S["hr_t"], 1)

                for t in range(2):
                    rows(t)
                pe.wait_ge(S["router_step"], 10)
                for t in range(NT + 1):
                    m = P if t < NT else META
                    last = turn(bank(t // 4 if t < NT else 4, m, (t % 4) * P, LATE + NE), aff[0:m, t, :], m)
                    if t in (3, 7, 8):
                        last.then_inc(S["lg_t"], 1)
                for t in range(2, NT + 1):
                    rows(t)
                pe.wait_ge(S["tk_step"], 3 * ROUNDS + 7)
                for r, (c, n) in enumerate(((0, P), (P, REST))):
                    for k, src in enumerate((top_where, top_best)):
                        last = turn(bank(0, NE, (2 * r + k) * NE, n), src[:, c:c + n], NE)
                last.then_inc(S["tk_t"], 1)
                pe.wait_ge(S["tk_c"], 4)
                pe.wait_ge(S["hr_c"], 4 * (NT + 1))
                def turn_tokens(e):
                    pe.wait_ge(S["ex_xa"], 16 * e + 16)
                    pe.wait_ge(S["ex_xb"], 16 * e + 16)
                    for c in range(KD):
                        turn(bank(2 + c // 3, P, (c % 3) * CAP), xs[0][:, c * P:(c + 1) * P])
                        last = turn(bank(2 + c // 3, REST, (c % 3) * CAP + P), xs[1][:, c * P:(c + 1) * P], REST)
                        if c in (2, 5, 7):
                            last.then_inc(S["ex_xt"], 1)

                def expert(e, more):
                    pe.wait_ge(S["ex_xc"], e * 3 + 3)
                    for j in range(EK):
                        if j == 1:
                            pe.wait_ge(S["ex_ra"], e * 2 + CREDIT)
                        if j >= 2:
                            pe.wait_ge(S["ex_h"], e * EK + j - 1 + 2 * CREDIT)
                        for w, b, ld, done in ((w_gate, 3, gate_ld, "ex_g"), (w_up, 4, up_ld, "ex_u")):
                            pe.wait_ge(ld[j], 16 * e + 16)
                            for c in range(KD):
                                last = mm(bank(b + 2 * (j % 2), CAP), w[:, j, c, :], xsT[:, c, :], start=(c == 0), stop=(c == KD - 1))
                            last.then_inc(S[done], 1)
                    pe.wait_ge(S["ex_h"], e * EK + EK + 2 * CREDIT)
                    pe.wait_ge(S["ex_rb"], e * 2 + CREDIT)
                    pe.wait_ge(down_ld, EK * 16 * e + EK * 16)
                    for c in range(KD):
                        b = (7, 0, 1)[c // 3]
                        for j in range(EK):
                            last = mm(bank(b, CAP, (c % 3) * CAP), w_down[:, j, c * P:(c + 1) * P], hidT[:, j, :], start=(j == 0), stop=(j == EK - 1))
                        if c in (2, 5, 7):
                            last.then_inc(S["ex_y"], 1)
                    if more:
                        turn_tokens(e + 1)
                    for n in range(2):
                        pe.wait_ge(S["ex_yt"], e * 3 + 2 + n)
                        for c in range(4):
                            turn(bank(5 + n, P, c * P), yT[:, 4 * n + c, 0:P])
                            last = turn(bank((7, 0)[n], P, c * P, REST), yT[:, 4 * n + c, P:CAP])
                        last.then_inc(S["ex_r"], 1)

                turn_tokens(0)
                with pe.Fori(0, NE - 1) as e:
                    expert(e, True)
                expert(NE - 1, False)



def layout(inputs):
    a = {n: np.asarray(v) for n, v in inputs.items()}

    def by_column_tile(w):
        lead, k, n = w.shape[:-2], w.shape[-2], w.shape[-1]
        w = w.reshape(*lead, k // P, P, n // P, P)
        r = len(lead)
        return w.transpose(*range(r), r + 2, r + 1, r, r + 3)

    def by_feature(g):
        return g.reshape(-1, P).T

    vectors = [by_feature(a[n][0]) for n in ("g_mix", "g_ffn", "g_mix_2", "g_ffn_2")]
    vectors += [by_feature(a["conv_w"][0, k]) for k in range(3)]
    vectors += [by_feature(a["g_conv_out"][0]), by_feature(a["g_attn_out"][0])]
    vectors += [np.tile(a[n][0], 2)[:, None] for n in ("g_q", "g_k")]
    vectors += [a[n][0][:, None] for n in ("g_subln_2", "g_qnorm_2", "g_knorm_2")]
    out = {"vectors": np.concatenate(vectors, 1)}
    w_in, w_out, w_gate, w_up = (by_column_tile(a[n][0]) for n in ("w_in", "w_out", "w_gate", "w_up"))
    tiles = [w_in[k * DCT + i] for i in range(DCT) for k in range(6)]
    tiles += list(w_out)
    tiles += [w[i] for i in range(NF) for w in (w_gate, w_up)]
    down = a["w_down"][0].reshape(NF // 2, 2, P, 2, HALF, P).transpose(3, 0, 2, 1, 4, 5).reshape(NF, P, KD, P)
    w_in2, w_a, w_b, w_out2 = (by_column_tile(a[n][0]) for n in ("w_in_2", "w_branch_a_2", "w_branch_b_2", "w_out_2"))
    late = [w_in2[c + h] for h in range(HEADS) for c in (QA, KA, VA)]
    late += [w_in2[GA]] + [t for d in range(KD - 1) for t in (w_in2[GA + d + 1], w_a[d])] + [w_a[KD - 1]]
    late += [w_in2[c] for g in range(KV) for c in (KB + g, *range(QB + g * GROUP, QB + (g + 1) * GROUP), VB + g)]
    late += [*w_in2[GB:GB + KD], *w_b, *w_out2]
    out["stream"] = np.concatenate([np.stack(tiles), down, np.stack(late)])
    for n in ("w_gate_2", "w_up_2"):
        out[n] = by_column_tile(a[n][0])
    for n in ("x", "meta_tokens_2", "lambda_q1_2", "lambda_k1_2", "lambda_q2_2", "lambda_k2_2", "w_down_2", "g_final_2"):
        out[n] = a[n]
    out["w_router_2"] = a["w_router_2"][0].reshape(KD, P, NE).transpose(1, 0, 2)
    return {n: np.ascontiguousarray(v) for n, v in (out | host_constants()).items()}


def kernel(**inputs):
    import concourse.bacc as bacc
    from concourse.bass_utils import run_bass_kernel_spmd as run

    nc = bacc.Bacc("TRN2", target_bir_lowering=False, num_devices=1)
    arrays, aps = {}, {}
    for name, a in layout(inputs).items():
        arrays[f"in_{name}"] = a
        aps[name] = nc.dram_tensor(f"in_{name}", a.shape, mybir.dt.from_np(a.dtype), kind="ExternalInput").ap()
    out = nc.dram_tensor("out", (1, T1, D), F32, kind="ExternalOutput").ap()
    build(nc, aps, out)
    r = run(nc, [arrays], core_ids=[0])
    return r.results[0]["out"]
```
